# Optimizing a Trainium2 kernel written in Bass

```python
import math
import jax, jax.numpy as jnp
from jax import lax
import numpy as np

D_MODEL = 1024
BATCH = 1
SEQ = 512
DEPTH = 2

CTX_LEN = 256
GRID_W = 64
N_MIXERS = 4
GROUP_W = D_MODEL // N_MIXERS
D_MIX = GROUP_W * N_MIXERS
HEAD_DIM = 64
HG_DK = 64
HG_DV = 64
HG_HEADS = GROUP_W // HG_DV
HG_CHUNK = 64
GA_HEADS = GROUP_W // HEAD_DIM
GA_KV = GA_HEADS // 2
DF_V = 64
DF_QK = DF_V // 2
DF_HEADS = GROUP_W // DF_V
WN_HEADS = GROUP_W // HEAD_DIM
WN_KV = WN_HEADS // 2
WINDOW = 128
Q_BLOCK = 128
ROPE_THETA = 10000.0
LN_EPS = 1e-5
RMS_EPS = 1e-6

IN_WIDTHS = (
    HG_HEADS * HG_DK, HG_HEADS * HG_DV, HG_HEADS * HG_DK, HG_HEADS * HG_DK,
    GA_HEADS * HEAD_DIM, GA_KV * HEAD_DIM, GA_KV * HEAD_DIM,
    DF_HEADS * 2 * DF_QK, DF_HEADS * 2 * DF_QK, DF_HEADS * DF_V,
    WN_HEADS * HEAD_DIM, WN_KV * HEAD_DIM, WN_KV * HEAD_DIM,
    D_MIX,
)
IN_WIDTH = sum(IN_WIDTHS)
SPLIT_AT = tuple(int(v) for v in np.cumsum(IN_WIDTHS)[:-1])


def rms_norm(x, g):
    xf = x.astype(jnp.float32)
    y = xf * lax.rsqrt(jnp.mean(xf * xf, axis=-1, keepdims=True) + RMS_EPS)
    return (y * g).astype(x.dtype)

def layer_norm(x, g, b):
    xf = x.astype(jnp.float32)
    mu = jnp.mean(xf, axis=-1, keepdims=True)
    var = jnp.mean(jnp.square(xf - mu), axis=-1, keepdims=True)
    return ((xf - mu) * lax.rsqrt(var + LN_EPS) * g + b).astype(x.dtype)

def split_heads(t, n_heads):
    return t.reshape(t.shape[:-1] + (n_heads, t.shape[-1] // n_heads))

def merge_heads(t):
    return t.reshape(t.shape[:2] + (-1,))

def axial_rope(n_tok, dim):
    rows = n_tok // GRID_W
    row = jnp.repeat(jnp.arange(rows, dtype=jnp.float32), GRID_W)
    col = jnp.broadcast_to(jnp.arange(GRID_W, dtype=jnp.float32), (rows, GRID_W)).reshape(-1)
    d_axis = dim // 2
    inv = ROPE_THETA ** (-jnp.arange(0, d_axis, 2, dtype=jnp.float32) / d_axis)
    ang_r = row[:, None] * inv
    ang_c = col[:, None] * inv
    ang = jnp.concatenate([ang_r, ang_r, ang_c, ang_c], axis=-1)
    return jnp.cos(ang), jnp.sin(ang)

def apply_rope(x, rope):
    cos, sin = rope
    a1, a2, b1, b2 = jnp.split(x, 4, axis=-1)
    rot = jnp.concatenate([-a2, a1, -b2, b1], axis=-1)
    return (x * cos[:, None, :] + rot * sin[:, None, :]).astype(x.dtype)

def sweep_query_blocks(fn, q):
    b, s = q.shape[0], q.shape[1]
    nb = s // Q_BLOCK
    qb = jnp.moveaxis(q.reshape((b, nb, Q_BLOCK) + q.shape[2:]), 1, 0)
    out = lax.map(fn, qb)
    return jnp.moveaxis(out, 0, 1).reshape((b, s) + out.shape[3:])

def hgrn_forget(z, lb):
    f = lb + (1.0 - lb) * jax.nn.sigmoid(z.astype(jnp.float32))
    return (1.0 - f).astype(z.dtype), jnp.log(f)

def gla_chunk_scan(q, k, v, logf, s0):
    b, t, h, _ = q.shape
    dv = v.shape[-1]
    nc = t // HG_CHUNK

    def to_chunks(a):
        return jnp.moveaxis(a.reshape(b, nc, HG_CHUNK, h, a.shape[-1]), 1, 0)

    incl = jnp.tril(jnp.ones((HG_CHUNK, HG_CHUNK), dtype=bool))

    def step(s, xs):
        qc, kc, vc, fc = xs
        qf, kf, vf = qc.astype(jnp.float32), kc.astype(jnp.float32), vc.astype(jnp.float32)
        bcum = jnp.cumsum(fc, axis=1)
        o_inter = jnp.einsum('bthk,bhkv->bthv', qf * jnp.exp(bcum), s)
        diff = bcum[:, :, None] - bcum[:, None, :]
        decay = jnp.exp(jnp.where(incl[None, :, :, None, None], diff, -jnp.inf))
        att = jnp.einsum('bthk,bshk,btshk->bhts', qf, kf, decay)
        o_intra = jnp.einsum('bhts,bshv->bthv', att, vf)
        blast = bcum[:, -1]
        s_new = jnp.exp(blast)[..., None] * s + jnp.einsum(
            'bshk,bshv->bhkv', kf * jnp.exp(blast[:, None] - bcum), vf)
        return s_new, (o_inter + o_intra).astype(v.dtype)

    s_fin, o = lax.scan(step, s0, (to_chunks(q), to_chunks(k), to_chunks(v), to_chunks(logf)))
    return jnp.moveaxis(o, 0, 1).reshape(b, t, h, dv), s_fin

def gla_final_state(k, v, logf):
    after = lax.cumsum(logf, axis=1, reverse=True) - logf
    return jnp.einsum('bshk,bshv->bhkv', k.astype(jnp.float32) * jnp.exp(after), v.astype(jnp.float32))

def hgrn2_mixer(q, i, f_fwd, f_bwd, qc, ic, fc_fwd, fc_bwd, lb, norm_g, ctx_out):
    hs = lambda t: split_heads(t, HG_HEADS)
    flip = lambda t: jnp.flip(t, axis=1)
    q, qc = jax.nn.silu(hs(q)), jax.nn.silu(hs(qc))
    i, ic = hs(i), hs(ic)
    lb_f = lb[0].reshape(HG_HEADS, HG_DK)
    lb_b = lb[1].reshape(HG_HEADS, HG_DK)
    k_f, lf_f = hgrn_forget(hs(f_fwd), lb_f)
    k_b, lf_b = hgrn_forget(hs(f_bwd), lb_b)
    kc_f, lfc_f = hgrn_forget(hs(fc_fwd), lb_f)
    kc_b, lfc_b = hgrn_forget(hs(fc_bwd), lb_b)
    b = qc.shape[0]
    if ctx_out:
        zeros = jnp.zeros((b, HG_HEADS, HG_DK, HG_DV), jnp.float32)
        oc_f, s_cf = gla_chunk_scan(qc, kc_f, ic, lfc_f, zeros)
        oc_b, s_cb = gla_chunk_scan(flip(qc), flip(kc_b), flip(ic), flip(lfc_b), zeros)
        yc = merge_heads(rms_norm(oc_f + flip(oc_b), norm_g))
    else:
        s_cf = gla_final_state(kc_f, ic, lfc_f)
        s_cb = gla_final_state(flip(kc_b), flip(ic), flip(lfc_b))
        yc = None
    o_f, _ = gla_chunk_scan(q, k_f, i, lf_f, s_cf)
    o_b, _ = gla_chunk_scan(flip(q), flip(k_b), flip(i), flip(lf_b), s_cb)
    y = merge_heads(rms_norm(o_f + flip(o_b), norm_g))
    return y, yc

def global_gqa(q, k, v, sink=None):
    b, s, h, d = q.shape
    kv = k.shape[2]
    g = h // kv
    scale = d ** -0.5
    qg = q.reshape(b, s, kv, g, d)

    def block(qb):
        logits = jnp.einsum('bqkgd,btkd->bkgqt', qb, k).astype(jnp.float32) * scale
        if sink is None:
            p = jax.nn.softmax(logits, axis=-1)
        else:
            col = jnp.broadcast_to(sink.astype(jnp.float32).reshape(kv, g)[None, :, :, None, None],
                                   logits.shape[:-1] + (1,))
            p = jax.nn.softmax(jnp.concatenate([logits, col], axis=-1), axis=-1)[..., :-1]
        return jnp.einsum('bkgqt,btkd->bqkgd', p.astype(v.dtype), v)

    return sweep_query_blocks(block, qg).reshape(b, s, h, d)

def diff_attention(q, k, v, lam, lam_init, subln_g):
    scale = q.shape[-1] ** -0.5

    def block(qb):
        logits = jnp.einsum('bqhmd,bthmd->bhmqt', qb, k).astype(jnp.float32) * scale
        p = jax.nn.softmax(logits, axis=-1)
        w = p[:, :, 0] - lam * p[:, :, 1]
        return jnp.einsum('bhqt,bthd->bqhd', w.astype(v.dtype), v)

    o = sweep_query_blocks(block, q)
    return rms_norm(o, subln_g) * (1.0 - lam_init)

def window_gqa_latent(q, k, v, k_ctx, v_ctx, sink):
    b, s, h, d = q.shape
    kv = k.shape[2]
    g = h // kv
    nb = s // Q_BLOCK
    scale = d ** -0.5

    def banded(t):
        tp = jnp.pad(t, ((0, 0), (Q_BLOCK, Q_BLOCK), (0, 0), (0, 0)))
        tb = tp.reshape(b, nb + 2, Q_BLOCK, kv, d)
        return jnp.concatenate([tb[:, :-2], tb[:, 1:-1], tb[:, 2:]], axis=2)

    kb, vb = banded(k), banded(v)
    qb = q.reshape(b, nb, Q_BLOCK, kv, g, d)
    blk = jnp.arange(nb)[:, None, None]
    qpos = blk * Q_BLOCK + jnp.arange(Q_BLOCK)[None, :, None]
    kpos = (blk - 1) * Q_BLOCK + jnp.arange(3 * Q_BLOCK)[None, None, :]
    allowed = (jnp.abs(kpos - qpos) <= WINDOW) & (kpos >= 0) & (kpos < s)
    lw = jnp.einsum('bnqkgd,bnskd->bnkgqs', qb, kb).astype(jnp.float32) * scale
    lw = jnp.where(allowed[None, :, None, None], lw, -jnp.inf)
    lc = jnp.einsum('bnqkgd,bskd->bnkgqs', qb, k_ctx).astype(jnp.float32) * scale
    ls = jnp.broadcast_to(sink.astype(jnp.float32).reshape(kv, g)[None, None, :, :, None, None],
                          lw.shape[:-1] + (1,))
    p = jax.nn.softmax(jnp.concatenate([lw, lc, ls], axis=-1), axis=-1).astype(v.dtype)
    n_w = 3 * Q_BLOCK
    n_c = k_ctx.shape[1]
    o = (jnp.einsum('bnkgqs,bnskd->bnqkgd', p[..., :n_w], vb)
         + jnp.einsum('bnkgqs,bskd->bnqkgd', p[..., n_w:n_w + n_c], v_ctx))
    return o.reshape(b, s, h, d)

def mixer_layer(x, cx, c, c_ctx, w_in, w_out, w_ada, b_ada, ln_g, ln_b, lb, hg_norm_g,
                ga_qn, ga_kn, df_lam, df_subln_g, wn_sink, rope64, rope32, layer_idx, ctx_out):
    alpha = (2.0 * DEPTH) ** 0.25
    shift, scale, gate = jnp.split(jax.nn.silu(c) @ w_ada + b_ada, 3, axis=-1)
    shift_c, scale_c, gate_c = jnp.split(jax.nn.silu(c_ctx) @ w_ada + b_ada, 3, axis=-1)
    h = x * (1.0 + scale[:, None]) + shift[:, None]
    hc = cx * (1.0 + scale_c) + shift_c
    (a_q, a_i, a_ff, a_fb, b_q, b_k, b_v, c_q, c_k, c_v, d_q, d_k, d_v, g_lat) = jnp.split(h @ w_in, SPLIT_AT, axis=-1)
    (a_qc, a_ic, a_ffc, a_fbc, b_qc, b_kc, b_vc, c_qc, c_kc, c_vc, d_qc, d_kc, d_vc, g_ctx) = jnp.split(hc @ w_in, SPLIT_AT, axis=-1)

    y_a, yc_a = hgrn2_mixer(a_q, a_i, a_ff, a_fb, a_qc, a_ic, a_ffc, a_fbc, lb, hg_norm_g, ctx_out)

    qB = apply_rope(rms_norm(split_heads(b_q, GA_HEADS), ga_qn), rope64)
    kB = apply_rope(rms_norm(split_heads(b_k, GA_KV), ga_kn), rope64)
    vB = split_heads(b_v, GA_KV)
    kBc = rms_norm(split_heads(b_kc, GA_KV), ga_kn)
    vBc = split_heads(b_vc, GA_KV)
    y_b = merge_heads(global_gqa(qB, jnp.concatenate([kB, kBc], 1), jnp.concatenate([vB, vBc], 1)))

    bsz, n = x.shape[0], x.shape[1]
    n_ctx = cx.shape[1]
    def diff_qk(t, length, rotate):
        t = t.reshape(bsz, length, DF_HEADS * 2, DF_QK)
        if rotate:
            t = apply_rope(t, rope32)
        return t.reshape(bsz, length, DF_HEADS, 2, DF_QK)
    lam_init = 0.8 - 0.6 * math.exp(-0.3 * layer_idx)
    lamf = df_lam.astype(jnp.float32)
    lam = jnp.exp(jnp.sum(lamf[0] * lamf[1])) - jnp.exp(jnp.sum(lamf[2] * lamf[3])) + lam_init
    qC, kC, vC = diff_qk(c_q, n, True), diff_qk(c_k, n, True), split_heads(c_v, DF_HEADS)
    kCc, vCc = diff_qk(c_kc, n_ctx, False), split_heads(c_vc, DF_HEADS)
    y_c = merge_heads(diff_attention(qC, jnp.concatenate([kC, kCc], 1), jnp.concatenate([vC, vCc], 1),
                                     lam, lam_init, df_subln_g))

    qD = apply_rope(split_heads(d_q, WN_HEADS), rope64)
    kD = apply_rope(split_heads(d_k, WN_KV), rope64)
    vD = split_heads(d_v, WN_KV)
    kDc, vDc = split_heads(d_kc, WN_KV), split_heads(d_vc, WN_KV)
    y_d = merge_heads(window_gqa_latent(qD, kD, vD, kDc, vDc, wn_sink))

    y = jnp.concatenate([y_a, y_b, y_c, y_d], axis=-1) * jax.nn.silu(g_lat)
    x_new = layer_norm(alpha * x + gate[:, None] * (y @ w_out), ln_g, ln_b)
    if not ctx_out:
        return x_new, None

    yc_b = merge_heads(global_gqa(rms_norm(split_heads(b_qc, GA_HEADS), ga_qn), kBc, vBc))
    yc_c = merge_heads(diff_attention(diff_qk(c_qc, n_ctx, False), kCc, vCc, lam, lam_init, df_subln_g))
    yc_d = merge_heads(global_gqa(split_heads(d_qc, WN_HEADS), kDc, vDc, wn_sink))
    yc = jnp.concatenate([yc_a, yc_b, yc_c, yc_d], axis=-1) * jax.nn.silu(g_ctx)
    cx_new = layer_norm(alpha * cx + gate_c * (yc @ w_out), ln_g, ln_b)
    return x_new, cx_new

def first_inputs(seed: int = 0) -> dict:
    key = jax.random.key(seed)
    ks = jax.random.split(key, 17)
    f32 = jnp.float32
    nrm = lambda k, shape, s: jax.random.normal(k, shape, f32) * s
    beta = (8.0 * DEPTH) ** -0.25
    return {
        "x": nrm(ks[0], (BATCH, SEQ, D_MODEL), 1.0),
        "c": nrm(ks[1], (BATCH, D_MODEL), 1.0),
        "ctx": nrm(ks[2], (BATCH, CTX_LEN, D_MODEL), 1.0),
        "c_ctx": nrm(ks[3], (D_MODEL,), 1.0),
        "w_in": nrm(ks[4], (DEPTH, D_MODEL, IN_WIDTH), D_MODEL ** -0.5),
        "w_out": nrm(ks[5], (DEPTH, D_MIX, D_MODEL), (D_MIX ** -0.5) * beta),
        "w_ada": nrm(ks[6], (DEPTH, D_MODEL, 3 * D_MODEL), 0.5 * D_MODEL ** -0.5),
        "b_ada": nrm(ks[7], (DEPTH, 3 * D_MODEL), 0.02),
        "ln_g": 1.0 + nrm(ks[8], (DEPTH, D_MODEL), 0.02),
        "ln_b": nrm(ks[9], (DEPTH, D_MODEL), 0.02),
        "hg_lb_logits": nrm(ks[10], (DEPTH, 2, HG_HEADS * HG_DK), 0.1),
        "hg_norm_g": 1.0 + nrm(ks[11], (DEPTH, HG_DV), 0.02),
        "ga_q_norm_g": 1.0 + nrm(ks[12], (DEPTH, HEAD_DIM), 0.02),
        "ga_k_norm_g": 1.0 + nrm(ks[13], (DEPTH, HEAD_DIM), 0.02),
        "df_lambda": nrm(ks[14], (DEPTH, 4, DF_QK), 0.1),
        "df_subln_g": 1.0 + nrm(ks[15], (DEPTH, DF_V), 0.02),
        "wn_sink": nrm(ks[16], (DEPTH, WN_HEADS), 0.5),
    }

def first_block(x, c, ctx, c_ctx, w_in, w_out, w_ada, b_ada, ln_g, ln_b, hg_lb_logits, hg_norm_g,
              ga_q_norm_g, ga_k_norm_g, df_lambda, df_subln_g, wn_sink):
    n = x.shape[1]
    rope64 = axial_rope(n, HEAD_DIM)
    rope32 = axial_rope(n, DF_QK)
    lb_sm = jax.nn.softmax(hg_lb_logits.astype(jnp.float32), axis=0)
    lower_bounds = jnp.cumsum(lb_sm, axis=0) - lb_sm[0]
    cx = ctx
    for l in range(DEPTH):
        x, cx = mixer_layer(x, cx, c, c_ctx, w_in[l], w_out[l], w_ada[l], b_ada[l], ln_g[l], ln_b[l],
                            lower_bounds[l], hg_norm_g[l], ga_q_norm_g[l], ga_k_norm_g[l], df_lambda[l],
                            df_subln_g[l], wn_sink[l], rope64, rope32, l, l < DEPTH - 1)
    return x


DEPTH_2 = 1

MIX_W = D_MODEL // N_MIXERS
N_Q_HEADS = MIX_W // HEAD_DIM
N_KV_HEADS = 2
Q_PER_KV = N_Q_HEADS // N_KV_HEADS
KV_W = N_KV_HEADS * HEAD_DIM
GMLP_GROUPS = 4
GMLP_CHUNK = 128
CMP_LEN = 32
CMP_STRIDE = 16
CMP_HIDDEN = 128
SEL_BLOCK = 64
SEL_TOPK = 8
N_LOCAL_BLOCKS = 2
WINDOW_2 = 512
CONF_KERNEL = 31
SCONV_KERNEL = 3
D_FF = 4 * D_MODEL
NSA_GATE_W = N_Q_HEADS * 3
IN_WIDTHS_2 = (MIX_W, MIX_W, MIX_W, KV_W, KV_W, KV_W, KV_W, KV_W, KV_W, NSA_GATE_W, MIX_W, MIX_W, MIX_W, MIX_W, MIX_W)
IN_COLS = sum(IN_WIDTHS_2)
NEG_INF = -1e30


def _rms(x, g, eps=1e-6):
    xf = x.astype(jnp.float32)
    y = xf * lax.rsqrt(jnp.mean(xf * xf, axis=-1, keepdims=True) + eps)
    return (y * g.astype(jnp.float32)).astype(x.dtype)

def _layernorm(x, g, b, eps=1e-5):
    xf = x.astype(jnp.float32)
    mu = jnp.mean(xf, axis=-1, keepdims=True)
    var = jnp.mean(jnp.square(xf - mu), axis=-1, keepdims=True)
    return ((xf - mu) * lax.rsqrt(var + eps) * g.astype(jnp.float32) + b.astype(jnp.float32)).astype(x.dtype)

def _causal_depthwise_conv(x, w):
    k = w.shape[0]
    return lax.conv_general_dilated(x, w[:, None, :].astype(x.dtype), window_strides=(1,),
                                    padding=[(k - 1, 0)], dimension_numbers=('NWC', 'WIO', 'NWC'),
                                    feature_group_count=x.shape[-1])

def _gmlp_spatial_gate(u, v, ln_g, ln_b, ws, bs):
    B, S, _ = v.shape
    nc = S // GMLP_CHUNK
    v = _layernorm(v, ln_g, ln_b).reshape(B, nc, GMLP_CHUNK, GMLP_GROUPS, MIX_W // GMLP_GROUPS)
    mask = np.tril(np.ones((GMLP_CHUNK, GMLP_CHUNK), dtype=bool))
    wsm = jnp.where(mask, ws, 0).astype(v.dtype)
    mixed = jnp.einsum('gts,bnsgc->bntgc', wsm, v) + bs.T[None, None, :, :, None].astype(v.dtype)
    return u * mixed.reshape(B, S, MIX_W)

def _overlap_matrix(n_cmp, n_sel):
    cs = np.arange(n_cmp) * CMP_STRIDE
    ce = cs + CMP_LEN
    ss = np.arange(n_sel) * SEL_BLOCK
    se = ss + SEL_BLOCK
    return ((cs[:, None] < se[None, :]) & (ce[:, None] > ss[None, :])).astype(np.float32)

def _nsa(q, kc, vc, ks, vs, kw, vw, gate_logits, q_g, k_g, cmp_pe, cmp_w1, cmp_w2):
    B, S, _ = q.shape
    T = Q_BLOCK
    nqb = S // T
    pos = jnp.arange(S)
    scale = HEAD_DIM ** -0.5
    heads = lambda t: t.reshape(B, S, N_KV_HEADS, HEAD_DIM)
    q = _rms(q.reshape(B, S, N_KV_HEADS, Q_PER_KV, HEAD_DIM), q_g)

    n_cmp = (S - CMP_LEN) // CMP_STRIDE + 1
    cmp_idx = np.arange(n_cmp)[:, None] * CMP_STRIDE + np.arange(CMP_LEN)[None, :]

    def compress(t, pe, w1, w2):
        blk = jnp.take(heads(t), cmp_idx, axis=1) + pe[None, None, :, None, :]
        blk = jnp.swapaxes(blk, 2, 3).reshape(B, n_cmp, N_KV_HEADS, CMP_LEN * HEAD_DIM)
        hid = jax.nn.gelu(jnp.einsum('bnhf,fe->bnhe', blk, w1))
        return jnp.einsum('bnhe,ed->bnhd', hid, w2)

    k_cmp = _rms(compress(kc, cmp_pe[0], cmp_w1[0], cmp_w2[0]), k_g[0])
    v_cmp = compress(vc, cmp_pe[1], cmp_w1[1], cmp_w2[1])
    cmp_valid = cmp_idx[:, -1][None, :] <= np.arange(S)[:, None]
    s = jnp.einsum('bshgd,bnhd->bhgsn', q, k_cmp).astype(jnp.float32) * scale
    p_cmp = jnp.where(cmp_valid, jax.nn.softmax(jnp.where(cmp_valid, s, NEG_INF), axis=-1), 0.0)
    o_cmp = jnp.einsum('bhgsn,bnhd->bshgd', p_cmp.astype(v_cmp.dtype), v_cmp)

    n_sel = S // SEL_BLOCK
    k_top = min(SEL_TOPK, n_sel)
    p_slc = jnp.einsum('bhgsn,nj->bhsj', p_cmp, jnp.asarray(_overlap_matrix(n_cmp, n_sel)))
    blk = np.arange(n_sel)[None, :]
    cur = (np.arange(S) // SEL_BLOCK)[:, None]
    forced = (blk == 0) | ((cur - blk >= 0) & (cur - blk < N_LOCAL_BLOCKS))
    causal = blk <= cur
    score = jnp.where(forced, jnp.inf, jnp.where(causal, p_slc, -jnp.inf))
    sel_idx = lax.top_k(score, k_top)[1]

    ks_h = jnp.swapaxes(_rms(heads(ks), k_g[1]), 1, 2)
    vs_h = jnp.swapaxes(heads(vs), 1, 2)
    gather = jax.vmap(jax.vmap(lambda a, i: a[i]))
    tok_off = jnp.arange(SEL_BLOCK)

    def sel_block(args):
        qb, ib, pb = args
        tok = (ib[..., None] * SEL_BLOCK + tok_off).reshape(B, N_KV_HEADS, T, k_top * SEL_BLOCK)
        flat = tok.reshape(B, N_KV_HEADS, -1)
        kg = gather(ks_h, flat).reshape(B, N_KV_HEADS, T, k_top * SEL_BLOCK, HEAD_DIM)
        vg = gather(vs_h, flat).reshape(B, N_KV_HEADS, T, k_top * SEL_BLOCK, HEAD_DIM)
        sb = jnp.einsum('bthgd,bhtkd->bhgtk', qb, kg).astype(jnp.float32) * scale
        m = (tok <= pb[:, None])[:, :, None]
        pr = jax.nn.softmax(jnp.where(m, sb, NEG_INF), axis=-1).astype(vg.dtype)
        return jnp.einsum('bhgtk,bhtkd->bthgd', pr, vg)

    q_blocks = jnp.moveaxis(q.reshape(B, nqb, T, N_KV_HEADS, Q_PER_KV, HEAD_DIM), 1, 0)
    i_blocks = jnp.moveaxis(sel_idx.reshape(B, N_KV_HEADS, nqb, T, k_top), 2, 0)
    p_blocks = pos.reshape(nqb, T)
    o_sel = jnp.moveaxis(lax.map(sel_block, (q_blocks, i_blocks, p_blocks)), 0, 1)
    o_sel = o_sel.reshape(B, S, N_KV_HEADS, Q_PER_KV, HEAD_DIM)

    kw_h = _rms(heads(kw), k_g[2])
    vw_h = heads(vw)
    win_idx = np.arange(nqb)[:, None] * T + np.arange(WINDOW_2 + T)[None, :]
    kpos = (win_idx - WINDOW_2)[:, None, :]
    qpos = np.arange(S).reshape(nqb, T)[:, :, None]
    wmask = (kpos <= qpos) & (kpos > qpos - WINDOW_2) & (kpos >= 0)
    pad = ((0, 0), (WINDOW_2, 0), (0, 0), (0, 0))
    kb = jnp.take(jnp.pad(kw_h, pad), win_idx, axis=1)
    vb = jnp.take(jnp.pad(vw_h, pad), win_idx, axis=1)
    qb = q.reshape(B, nqb, T, N_KV_HEADS, Q_PER_KV, HEAD_DIM)
    sw = jnp.einsum('bnthgd,bnmhd->bnhgtm', qb, kb).astype(jnp.float32) * scale
    pw = jax.nn.softmax(jnp.where(wmask[:, None, None], sw, NEG_INF), axis=-1).astype(vb.dtype)
    o_win = jnp.einsum('bnhgtm,bnmhd->bnthgd', pw, vb).reshape(B, S, N_KV_HEADS, Q_PER_KV, HEAD_DIM)

    g = jax.nn.sigmoid(gate_logits.reshape(B, S, N_KV_HEADS, Q_PER_KV, 3))
    o = g[..., 0:1] * o_cmp + g[..., 1:2] * o_sel + g[..., 2:3] * o_win
    return o.reshape(B, S, MIX_W)

def second_inputs(seed: int = 0) -> dict:
    key = jax.random.key(seed)
    ks = jax.random.split(key, 26)
    L = DEPTH_2
    nrm = lambda k, shape, sc: jax.random.normal(k, shape, jnp.float32) * sc
    res_sc = (2.0 * DEPTH_2) ** -0.5
    return {
        "x": nrm(ks[0], (BATCH, SEQ, D_MODEL), 1.0),
        "norm1_g": 1.0 + nrm(ks[1], (L, D_MODEL), 0.02),
        "w_in": nrm(ks[2], (L, D_MODEL, IN_COLS), D_MODEL ** -0.5),
        "gmlp_ln_g": 1.0 + nrm(ks[3], (L, MIX_W), 0.02),
        "gmlp_ln_b": nrm(ks[4], (L, MIX_W), 0.02),
        "gmlp_ws": nrm(ks[5], (L, GMLP_GROUPS, GMLP_CHUNK, GMLP_CHUNK), GMLP_CHUNK ** -0.5),
        "gmlp_bs": 1.0 + nrm(ks[6], (L, GMLP_GROUPS, GMLP_CHUNK), 0.02),
        "nsa_q_norm_g": 1.0 + nrm(ks[7], (L, HEAD_DIM), 0.02),
        "nsa_k_norm_g": 1.0 + nrm(ks[8], (L, 3, HEAD_DIM), 0.02),
        "nsa_cmp_pe": nrm(ks[9], (L, 2, CMP_LEN, HEAD_DIM), 0.02),
        "nsa_cmp_w1": nrm(ks[10], (L, 2, CMP_LEN * HEAD_DIM, CMP_HIDDEN), (CMP_LEN * HEAD_DIM) ** -0.5),
        "nsa_cmp_w2": nrm(ks[11], (L, 2, CMP_HIDDEN, HEAD_DIM), CMP_HIDDEN ** -0.5),
        "conf_conv_w": nrm(ks[12], (L, CONF_KERNEL, MIX_W), CONF_KERNEL ** -0.5),
        "conf_conv_b": nrm(ks[13], (L, MIX_W), 0.02),
        "conf_ln_g": 1.0 + nrm(ks[14], (L, MIX_W), 0.02),
        "conf_ln_b": nrm(ks[15], (L, MIX_W), 0.02),
        "sconv_w": nrm(ks[16], (L, SCONV_KERNEL, MIX_W), SCONV_KERNEL ** -0.5),
        "w_branch": nrm(ks[17], (L, N_MIXERS, MIX_W, D_MODEL), MIX_W ** -0.5),
        "w_gate": nrm(ks[18], (L, D_MODEL, N_MIXERS * D_MODEL), D_MODEL ** -0.5),
        "b_gate": nrm(ks[19], (L, N_MIXERS * D_MODEL), 0.02),
        "w_out": nrm(ks[20], (L, D_MODEL, D_MODEL), D_MODEL ** -0.5 * res_sc),
        "norm2_g": 1.0 + nrm(ks[21], (L, D_MODEL), 0.02),
        "w_mlp1": nrm(ks[22], (L, D_MODEL, D_FF), D_MODEL ** -0.5),
        "w_mlp2": nrm(ks[23], (L, D_FF, D_MODEL), D_FF ** -0.5 * res_sc),
    }

def second_block(x, norm1_g, w_in, gmlp_ln_g, gmlp_ln_b, gmlp_ws, gmlp_bs, nsa_q_norm_g, nsa_k_norm_g,
              nsa_cmp_pe, nsa_cmp_w1, nsa_cmp_w2, conf_conv_w, conf_conv_b, conf_ln_g, conf_ln_b,
              sconv_w, w_branch, w_gate, b_gate, w_out, norm2_g, w_mlp1, w_mlp2):
    B, S, D = x.shape
    split_points = np.cumsum(IN_WIDTHS_2)[:-1].tolist()
    for l in range(DEPTH_2):
        xn = _rms(x, norm1_g[l])
        (gu, gv, q, kc, vc, ks_, vs_, kw, vw, ng, ca, cb, sB, sC, sh) = jnp.split(
            jnp.einsum('bsd,de->bse', xn, w_in[l]), split_points, axis=-1)
        y_a = _gmlp_spatial_gate(jax.nn.gelu(gu), jax.nn.gelu(gv), gmlp_ln_g[l], gmlp_ln_b[l], gmlp_ws[l], gmlp_bs[l])
        y_b = _nsa(q, kc, vc, ks_, vs_, kw, vw, ng, nsa_q_norm_g[l], nsa_k_norm_g[l],
                   nsa_cmp_pe[l], nsa_cmp_w1[l], nsa_cmp_w2[l])
        z = ca * jax.nn.sigmoid(cb)
        z = _causal_depthwise_conv(z, conf_conv_w[l]) + conf_conv_b[l]
        y_c = jax.nn.silu(_layernorm(z, conf_ln_g[l], conf_ln_b[l]))
        y_d = sB * _causal_depthwise_conv(sC * sh, sconv_w[l])
        ys = jnp.stack([y_a, y_b, y_c, y_d], axis=2)
        proj = jnp.einsum('bsnc,ncd->bsnd', ys, w_branch[l])
        gates = jax.nn.sigmoid(jnp.einsum('bsd,de->bse', xn, w_gate[l]) + b_gate[l]).reshape(B, S, N_MIXERS, D)
        mixed = jnp.sum(gates * proj, axis=2)
        x = x + jnp.einsum('bsd,de->bse', mixed, w_out[l])
        hn = _rms(x, norm2_g[l])
        hid = jnp.square(jax.nn.relu(jnp.einsum('bsd,df->bsf', hn, w_mlp1[l])))
        x = x + jnp.einsum('bsf,fd->bsd', hid, w_mlp2[l])
    return x


_first_inputs = second_inputs


def second_inputs(seed=0):
    import zlib

    import numpy as np

    out = dict(_first_inputs(seed))
    spreads = {}
    factors = {'norm1_g': 3.39,
     'gmlp_ln_g': 200.0,
     'gmlp_ln_b': 200.0,
     'gmlp_bs': 172.139,
     'nsa_q_norm_g': 200.0,
     'nsa_k_norm_g': 200.0,
     'nsa_cmp_pe': 200.0,
     'conf_conv_b': 39.482,
     'conf_ln_g': 200.0,
     'conf_ln_b': 200.0,
     'b_gate': 8.0,
     'norm2_g': 16.994,
     'nsa_cmp_w1': 5.939,
     'nsa_cmp_w2': 5.422}
    for name, (base, spread) in spreads.items():
        noise = np.random.default_rng([zlib.crc32(name.encode()), seed]).standard_normal(out[name].shape)
        drawn = base * np.exp(spread * noise) if base else spread * noise
        out[name] = __import__('jax').numpy.asarray(drawn.astype(out[name].dtype))
    for name, factor in factors.items():
        out[name] = (out[name] * factor).astype(out[name].dtype)
    return out


_narrow_inputs = second_inputs


def second_inputs(seed=0):

    out = dict(_narrow_inputs(seed))
    wider = {'gmlp_ln_g': 5.26,
     'gmlp_ln_b': 5.43,
     'gmlp_bs': 3.84,
     'nsa_q_norm_g': 4.58,
     'nsa_k_norm_g': 4.35,
     'conf_ln_g': 11.66,
     'conf_ln_b': 11.64,
     'norm2_g': 3.73}
    for name, times in wider.items():
        mean = out[name].mean()
        out[name] = (mean + times * (out[name] - mean)).astype(out[name].dtype)
    return out


def setup_inputs(seed=0):
    out = dict(first_inputs(seed))
    for name, value in second_inputs(seed + 1).items():
        if name != "x":
            out[name + "_2"] = value
    return out


def reference(
    x, c, ctx, c_ctx, w_in, w_out, w_ada, b_ada, ln_g, ln_b, hg_lb_logits, hg_norm_g,
    ga_q_norm_g, ga_k_norm_g, df_lambda, df_subln_g, wn_sink, norm1_g_2, w_in_2, gmlp_ln_g_2,
    gmlp_ln_b_2, gmlp_ws_2, gmlp_bs_2, nsa_q_norm_g_2, nsa_k_norm_g_2, nsa_cmp_pe_2,
    nsa_cmp_w1_2, nsa_cmp_w2_2, conf_conv_w_2, conf_conv_b_2, conf_ln_g_2, conf_ln_b_2,
    sconv_w_2, w_branch_2, w_gate_2, b_gate_2, w_out_2, norm2_g_2, w_mlp1_2, w_mlp2_2,
):
    x = first_block(
        x, c, ctx, c_ctx, w_in, w_out, w_ada, b_ada, ln_g, ln_b, hg_lb_logits, hg_norm_g,
        ga_q_norm_g, ga_k_norm_g, df_lambda, df_subln_g, wn_sink,
    )
    return second_block(
        x, norm1_g_2, w_in_2, gmlp_ln_g_2, gmlp_ln_b_2, gmlp_ws_2, gmlp_bs_2, nsa_q_norm_g_2,
        nsa_k_norm_g_2, nsa_cmp_pe_2, nsa_cmp_w1_2, nsa_cmp_w2_2, conf_conv_w_2, conf_conv_b_2,
        conf_ln_g_2, conf_ln_b_2, sconv_w_2, w_branch_2, w_gate_2, b_gate_2, w_out_2, norm2_g_2,
        w_mlp1_2, w_mlp2_2,
    )


_drawn_inputs = setup_inputs


def setup_inputs(seed=0):
    import zlib

    import numpy as np

    out = dict(_drawn_inputs(seed))
    spreads = {}
    factors = {'ctx': 2.81,
     'b_ada': 4.551,
     'hg_lb_logits': 8.0,
     'hg_norm_g': 23.847,
     'ga_q_norm_g': 27.336,
     'ga_k_norm_g': 26.377,
     'df_lambda': 5.825,
     'df_subln_g': 35.593,
     'wn_sink': 64.0}
    for name, (base, spread) in spreads.items():
        noise = np.random.default_rng([zlib.crc32(name.encode()), seed]).standard_normal(out[name].shape)
        drawn = base * np.exp(spread * noise) if base else spread * noise
        out[name] = __import__('jax').numpy.asarray(drawn.astype(out[name].dtype))
    for name, factor in factors.items():
        out[name] = (out[name] * factor).astype(out[name].dtype)
    return out
```

```python
import math
from contextlib import ExitStack

import numpy as np

import concourse.bass as bass
from concourse import mybir
from concourse.alu_op_type import AluOpType as ALU

F32 = mybir.dt.float32
U8 = mybir.dt.uint8
ACT = mybir.ActivationFunctionType
AX = mybir.AxisListType.X

P = 128
D = 1024
KT = D // P
SEQ, CTX = 512, 256
TOK = SEQ + CTX
LT, CT = SEQ // P, CTX // P
TT = LT + CT
DEPTH = 2
GRID_W = 64
HD = 64
DQ = 32
NH, NKV = 4, 2
IN_W = 3840
C_AQ, C_AI, C_FF, C_FB, C_B, C_C, C_CV, C_D, C_G = 0, 256, 512, 768, 1024, 1536, 2048, 2304, 2816
IN_W2 = 2828
N_CMP, CMP_LEN, CMP_STRIDE, CMP_HID = 31, 32, 16, 128
CONV_K, SCONV_K = 31, 3
D_FF = 4096
FT = D_FF // P
RMS_EPS, LN_EPS = 1e-6, 1e-5
ALPHA = (2.0 * DEPTH) ** 0.25
SLOT = 1024
N_SLOTS = 6
ARENA = 50632
LOG_FLOOR = 1e-19


class Engine:

    def __init__(self, eng, sem):
        self.eng, self.sem, self.count, self.seen = eng, sem, 0, {}

    def after(self, *tokens):
        for t in tokens:
            if t is None:
                continue
            if isinstance(t, list):
                self.after(*t)
                continue
            sem, value = t
            if self.seen.get(id(sem), 0) < value:
                self.seen[id(sem)] = value
                self.eng.wait_ge(sem, value)

    def did(self, instruction):
        self.count += 1
        instruction.then_inc(self.sem, 1)
        return (self.sem, self.count)

    def now(self):
        return (self.sem, self.count) if self.count else None


class Transfers:

    def __init__(self, sem):
        self.sem, self.count = sem, 0

    def did(self, dma):
        self.count += 16
        dma.then_inc(self.sem, 16)
        return (self.sem, self.count)


class Bank:

    def __init__(self, ap):
        self.ap, self.read_by = ap, []


class WeightRing:

    def __init__(self, sync, slots, sems, plan):
        self.sync, self.slots = sync, slots
        self.loads = [Transfers(s) for s in sems]
        self.plan, self.issued, self.taken = plan, 0, 0
        self.arrived = {}
        for _ in range(min(len(slots), len(plan))):
            self.issue(None)

    def view(self, n):
        shape = self.plan[n][1]
        ap = self.slots[n % len(self.slots)][:, 0:shape[0] * shape[1]]
        return ap.rearrange("p (k n) -> p k n", k=shape[0])

    def issue(self, released_by):
        n = self.issued
        if n >= len(self.plan):
            return
        self.issued += 1
        self.sync.after(released_by)
        self.arrived[n] = self.loads[n % len(self.slots)].did(
            self.sync.eng.dma_start(self.view(n), self.plan[n][0]))

    def take(self, tag):
        n = self.taken
        self.taken += 1
        assert self.plan[n][2] == tag, (self.plan[n][2], tag)
        return self.view(n), self.arrived[n]

    def release(self, last_read):
        self.issue(last_read)


def interleave(*streams):
    live = list(streams)
    while live:
        for s in list(live):
            try:
                next(s)
            except StopIteration:
                live.remove(s)


def rows_plan(w, c0, n, tag):
    v = w.rearrange("(k p) n -> p k n", p=P)
    return [(v[:, 2 * i:2 * i + 2, c0:c0 + n], (2, n), tag) for i in range(v.shape[1] // 2)]


def cols_plan(w, c0, tag, n=P):
    v = w.rearrange("(k p) n -> p k n", p=P)
    return [(v[:, :, c0:c0 + n], (KT, n), tag)]


def weight_plan(a):
    plan = []
    for l in range(DEPTH):
        w = a["w_in"][l]
        for n in range(6):
            plan += rows_plan(a["w_ada"][l], 512 * n, 512, "ada")
        for t in range(2):
            for c in (C_AQ, C_FF, C_FB):
                plan += cols_plan(w, c + P * t, "hg")
            if t == 0:
                plan += rows_plan(w, C_AI, 256, "ai")
                plan += rows_plan(w, C_B, 512, "b")
                plan += rows_plan(w, C_C, 512, "c")
            else:
                plan += rows_plan(w, C_CV, 256, "cv")
                plan += rows_plan(w, C_D, 512, "d")
                plan += rows_plan(w, C_G, 512, "g") + rows_plan(w, C_G + 512, 512, "g")
        for n in range(2):
            plan += rows_plan(a["w_out"][l], 512 * n, 512, "out")
    w = a["w_in_2"][0]
    plan += rows_plan(w, 0, 512, "gmlp") + rows_plan(w, 512, 256, "q") + rows_plan(w, 1024, 512, "kv")
    plan += rows_plan(w, 1536, P, "ng")
    for c in FM2:
        plan += cols_plan(w, c, "fm")
    for d in range(KT):
        for n in range(4):
            plan += cols_plan(a["w_gate_2"][0], n * D + d * P, "gate")
        plan += cols_plan(a["w_branch_2"][0].rearrange("n c d -> (n c) d"), d * P, "branch")
    for n in range(2):
        plan += rows_plan(a["w_out_2"][0], 512 * n, 512, "out2")
    for f in range(FT):
        plan += cols_plan(a["w_mlp1_2"][0], f * P, "mlp1")
    for n in range(2):
        plan += rows_plan(a["w_mlp2_2"][0], 512 * n, 512, "mlp2")
    return plan


FM2 = (768, 896, 1548, 1676, 1804, 1932, 2060, 2188, 2316, 2444, 2572, 2700)


def build(nc, a, out):
    ctx = ExitStack()
    with ctx:
        def sem(name):
            return ctx.enter_context(nc.semaphore(name))

        T = Engine(nc.tensor, sem("pe_steps"))
        S = Engine(nc.scalar, sem("act_steps"))
        V = Engine(nc.vector, sem("dve_steps"))
        G = Engine(nc.gpsimd, sem("pool_steps"))
        Y = Engine(nc.sync, sem("sp_steps"))
        pe, act, dve, pool = nc.tensor, nc.scalar, nc.vector, nc.gpsimd

        base = ctx.enter_context(nc.sbuf_tensor("arena", [P, ARENA], F32))

        class Region:

            def __init__(self, start, size):
                self.start, self.size, self.at = start, size, 0

            def reset(self):
                self.at = 0

            def cut(self, *dims):
                n = int(np.prod(dims))
                assert self.at + n <= self.size, (self.at, n, self.size)
                ap = base[:, self.start + self.at:self.start + self.at + n]
                self.at += n
                if len(dims) == 2:
                    return ap.rearrange("p (a b) -> p a b", a=dims[0])
                if len(dims) == 3:
                    return ap.rearrange("p (a b c) -> p a b c", a=dims[0], b=dims[1])
                if len(dims) == 4:
                    return ap.rearrange("p (a b c d) -> p a b c d", a=dims[0], b=dims[1], c=dims[2])
                return ap

        at = 0
        regions = []
        for size in (6144, 17152, 4608, 6144, 7680, N_SLOTS * SLOT, 2760):
            regions.append(Region(at, size))
            at += size
        assert at == ARENA, at
        R_HT, R_WORK, R_V, R_G, R_QK, R_RING, R_TMP = regions

        def tile(name, shape, dt=F32):
            return ctx.enter_context(nc.sbuf_tensor(name, [P] + shape, dt))

        ident = tile("ident", [P])
        level_mask = tile("level_mask", [7, P], U8)
        cos64, sin64 = tile("cos64", [LT, HD]), tile("sin64", [LT, HD])
        cos32, sin32 = tile("cos32", [LT, DQ]), tile("sin32", [LT, DQ])
        low_mask, up_mask = tile("low_mask", [P]), tile("up_mask", [P])
        cols_a = tile("cols_a", [72])
        small = tile("small", [64])
        stats = tile("stats", [320])
        ada_t = tile("ada_t", [24, 2])
        csil = tile("csil", [KT, 2])
        lb = tile("lb", [2, 2, 2])
        lb1m = tile("lb1m", [2, 2, 2])

        psum = ctx.enter_context(nc.psum_tensor("psum", [P, 8, 512], F32))
        psum_flat = psum[:].rearrange("p b n -> p (b n)")
        banks = [Bank(psum[:, b, :]) for b in range(8)]

        slots = [R_RING.cut(SLOT) for _ in range(N_SLOTS)]
        ring = WeightRing(Y, slots, [sem(f"weights_{i}") for i in range(N_SLOTS)], weight_plan(a))

        constants = Transfers(sem("constants"))
        parameters = Transfers(sem("parameters"))
        x_loads = [Transfers(sem(f"x_load_{i}")) for i in range(2)]
        x_stores = Transfers(sem("x_stores"))
        out_stores = Transfers(sem("out_stores"))

        def load(dst, src, group, by=G):
            return group.did(by.eng.dma_start(dst, src))

        stage = R_TMP.cut(P)
        levels_wide = base[:, R_QK.start:R_QK.start + 7 * P].rearrange("p (l n) -> p l n", l=7)
        for dst, src in ((ident[:], a["c_ident"]), (levels_wide, a["c_levels"]),
                         (cos64[:], a["c_cos64"]), (sin64[:], a["c_sin64"]),
                         (cos32[:], a["c_cos32"]), (sin32[:], a["c_sin32"]),
                         (low_mask[:], a["c_low"]), (up_mask[:], a["c_up"])):
            load(dst, src, constants)
        load(stage[0:8, :], a["c"].rearrange("b (k p) -> (b k) p", p=P), constants)
        load(stage[8:16, :], a["c_ctx"].rearrange("(k p) -> k p", p=P), constants)
        load(stage[16:24, :], a["hg_lb_logits"].rearrange("l d (t p) -> (l d t) p", p=P), constants)
        ready = load(stage[24:72, :], a["b_ada"].rearrange("l (j p) -> (l j) p", p=P), constants)

        def bc(ap, axis, shape):
            return ap.unsqueeze(axis).to_broadcast(shape)

        def everyone():
            return [e.now() for e in (T, S, V, G)]

        def fence():
            all_now = everyone()
            for e in (T, S, V, G):
                e.after(*all_now)

        def rstd(v, scale, eps, r, tmp, token):
            V.after(token)
            t = V.did(dve.tensor_scalar(v, v, scale, eps, ALU.mult, ALU.add))
            S.after(t)
            t = S.did(act.activation(tmp, v, ACT.Ln))
            S.after(t)
            t = S.did(act.activation(r, tmp, ACT.Exp, scale=-0.5))
            V.after(t)
            t = V.did(dve.tensor_tensor(tmp, r, r, ALU.mult))
            V.after(t)
            t = V.did(dve.tensor_tensor(tmp, tmp, v, ALU.mult))
            V.after(t)
            t = V.did(dve.tensor_scalar(tmp, tmp, -0.5, 1.5, ALU.mult, ALU.add))
            V.after(t)
            return V.did(dve.tensor_tensor(r, r, tmp, ALU.mult))

        V.after(ready)
        V.did(dve.tensor_copy(level_mask[:], levels_wide))

        T.after(ready)
        t = T.did(pe.transpose(banks[0].ap[:, 0:72], stage[0:72, :], ident[0:72, 0:72]))
        S.after(t)
        t = S.did(act.activation(cols_a[:], banks[0].ap[:, 0:72], ACT.Copy))
        banks[0].read_by = [t]
        S.after(t)
        csil_ready = S.did(act.activation(csil[:], cols_a[:, 0:16].rearrange("p (v k) -> p k v", v=2), ACT.Silu))
        lg = cols_a[:, 16:24].rearrange("p (l n) -> p l n", l=2)
        sm = small[:, 0:16].rearrange("p (l n) -> p l n", l=4)
        V.after(t)
        t = V.did(dve.tensor_tensor(sm[:, 0, :], lg[:, 0, :], lg[:, 1, :], ALU.max))
        V.after(t)
        V.did(dve.tensor_tensor(sm[:, 1, :], lg[:, 0, :], sm[:, 0, :], ALU.subtract))
        t = V.did(dve.tensor_tensor(sm[:, 2, :], lg[:, 1, :], sm[:, 0, :], ALU.subtract))
        S.after(t)
        t = S.did(act.activation(sm[:, 1:3, :], sm[:, 1:3, :], ACT.Exp))
        V.after(t)
        t = V.did(dve.tensor_tensor(sm[:, 3, :], sm[:, 1, :], sm[:, 2, :], ALU.add))
        V.after(t)
        t = V.did(dve.reciprocal(sm[:, 3, :], sm[:, 3, :]))
        V.after(t)
        V.did(dve.memset(lb[:, 0], 0.0))
        t = V.did(dve.tensor_tensor(lb[:, 1].rearrange("p d t -> p (d t)"), sm[:, 2, :], sm[:, 3, :], ALU.mult))
        V.after(t)
        lb_ready = V.did(dve.tensor_scalar(lb1m[:], lb[:], -1.0, 1.0, ALU.mult, ALU.add))

        def product_rows(tag, tiles, lhs, lhs_ready, n, use, evacuate, cols=lambda m: None, kt=KT):
            got = [ring.take(tag) for _ in range(kt // 2)]
            for j, m in enumerate(tiles):
                b = banks[use[j % len(use)]]
                c0, c1 = cols(m) or (0, n)
                T.after(lhs_ready, b.read_by)
                for k in range(kt):
                    view, arrived = got[k // 2]
                    T.after(arrived)
                    mm = pe.matmul(b.ap[:, c0:c1], lhs(k, m), view[:, k % 2, c0:c1], start=k == 0, stop=k == kt - 1)
                    if j == len(tiles) - 1 and k % 2 == 1 and k < kt - 1:
                        ring.release(T.did(mm))
                done = T.did(mm)
                if j == len(tiles) - 1:
                    ring.release(done)
                b.read_by = evacuate(m, b.ap, done)
                yield

        def product_cols(tag, rhs, rhs_ready, spans, use, evacuate):
            view, arrived = ring.take(tag)
            T.after(rhs_ready, arrived)
            for j, (t0, t1) in enumerate(spans):
                b = banks[use[j % len(use)]]
                T.after(b.read_by)
                for k in range(KT):
                    mm = pe.matmul(b.ap[:, 0:t1 - t0], view[:, k, :], rhs(k, t0, t1), start=k == 0, stop=k == KT - 1)
                done = T.did(mm)
                if j == len(spans) - 1:
                    ring.release(done)
                b.read_by = evacuate(t0, t1, b.ap[:, 0:t1 - t0], done)

        def transposed(src, n_blocks, bank, token, width=P):
            T.after(token, bank.read_by)
            for i in range(n_blocks):
                mm = pe.transpose(bank.ap[0:width, i * P:(i + 1) * P], src[:, i * width:(i + 1) * width], ident[:])
            return T.did(mm)

        def attend(items, prob, prob_t, free):
            pairs = [(banks[2], banks[3]), (banks[4], banks[5])]
            state = {}
            n_pair = [0]

            def score(i):
                it = items[i]
                st = state[i] = {"sum": [], "p": []}
                for q, segments in it["maps"]:
                    n = n_pair[0]
                    n_pair[0] += 1
                    pr = pairs[n % 2]
                    s_ap = psum_flat[:, 1024 * (1 + n % 2):1024 * (2 + n % 2)]
                    T.after(it["q_ready"](), pr[0].read_by, pr[1].read_by, it["k_ready"])
                    for rhs, c0 in segments:
                        w = rhs.shape[-1]
                        mm = pe.matmul(s_ap[:, c0:c0 + w], q, rhs, start=True, stop=True)
                    t = T.did(mm)
                    V.after(t)
                    for c0, mask in it.get("masks", ()):
                        w = mask.shape[-1]
                        V.after(V.did(dve.tensor_tensor(s_ap[:, c0:c0 + w], s_ap[:, c0:c0 + w], mask, ALU.add)))
                    col = stats[:, 8 * (i % 40):8 * (i % 40) + 8]
                    j = len(st["sum"])
                    lo, hi = it["range"]
                    t = V.did(dve.reduce_max(col[:, j:j + 1], s_ap[:, lo:hi], AX, negate=True))
                    V.after(t)
                    if it.get("sink"):
                        neg_sink, sink = it["sink"]
                        t = V.did(dve.tensor_scalar(col[:, j:j + 1], col[:, j:j + 1], it["scale"], neg_sink, ALU.mult, ALU.min))
                    elif it["scale"] != 1.0:
                        t = V.did(dve.tensor_scalar(col[:, j:j + 1], col[:, j:j + 1], it["scale"], None, ALU.mult))
                    p = prob[n % len(prob)]
                    S.after(t, free["p"][n % len(prob)])
                    t = S.did(act.activation(p[:, lo:hi], s_ap[:, lo:hi], ACT.Exp, bias=col[:, j:j + 1],
                                             scale=it["scale"], accum_out=col[:, 2 + j:3 + j]))
                    pr[0].read_by = pr[1].read_by = [t]
                    if it.get("sink"):
                        t = S.did(act.activation(col[:, 6:7], sink, ACT.Exp, bias=col[:, 0:1]))
                        V.after(t)
                        t = V.did(dve.tensor_tensor(col[:, 2:3], col[:, 2:3], col[:, 6:7], ALU.add))
                    st["sum"].append(col[:, 2 + j:3 + j])
                    st["p"].append((p, n % len(prob), t))
                V.after(t)
                t = V.did(dve.reciprocal(it["rec"], st["sum"][0]))
                p = st["p"][0][0]
                if "neg_lam" in it:
                    lo, hi = it["range"]
                    V.did(dve.reciprocal(col[:, 4:5], st["sum"][1]))
                    t = V.now()
                    V.after(t)
                    t = V.did(dve.scalar_tensor_tensor(col[:, 5:6], st["sum"][0], it["neg_lam"], col[:, 4:5], ALU.mult, ALU.mult))
                    V.after(t)
                    p2 = st["p"][1][0]
                    t = V.did(dve.scalar_tensor_tensor(p[:, lo:hi], p2[:, lo:hi], col[:, 5:6], p[:, lo:hi], ALU.mult, ALU.add))
                    free["p"][st["p"][1][1]] = [t]
                if it.get("valid") is not None:
                    lo, hi = it["range"]
                    t = V.did(dve.tensor_tensor(p[:, lo:hi], p[:, lo:hi], it["valid"], ALU.mult))
                st["ready"] = t

            def turn(i):
                it, st = items[i], state[i]
                p, n_p, _ = st["p"][0]
                n = i % 2
                st["pt"] = []
                blocks = it["blocks"]
                for half in range(0, len(blocks), 3):
                    bank = banks[6 + (half // 3)]
                    part = blocks[half:half + 3]
                    T.after(st["ready"], [x[2] for x in st["p"]], bank.read_by)
                    for j, (c0, w, _) in enumerate(part):
                        mm = pe.transpose(bank.ap[0:w, j * P:(j + 1) * P], p[:, c0:c0 + w], ident[:])
                    t = T.did(mm)
                    w = part[0][1]
                    e = (S, V)[(half // 3 + i) % 2]
                    e.after(t, free["pt"][n] if half == 0 else free["pt_second"][n])
                    dst = prob_t[n][0:w, half * P:(half + len(part)) * P]
                    src = bank.ap[0:w, 0:len(part) * P]
                    if e is S:
                        t = S.did(act.activation(dst, src, ACT.Copy))
                    else:
                        t = V.did(dve.tensor_copy(dst, src))
                    bank.read_by = [t]
                    st["pt"].append(t)
                free["p"][n_p] = [T.now()]

            def value(i):
                it, st = items[i], state[i]
                n = i % 2
                T.after(st["pt"], it["v_ready"])
                if it["first"]:
                    T.after(it["bank"].read_by)
                blocks = it["blocks"]
                for j, (_, w, v) in enumerate(blocks):
                    mm = pe.matmul(it["bank"].ap[:, it["col"]:it["col"] + P], prob_t[n][0:w, j * P:(j + 1) * P], v,
                                   start=j == 0, stop=j == len(blocks) - 1)
                t = T.did(mm)
                free["pt"][n] = free["pt_second"][n] = [t]
                if it.get("finish"):
                    it["bank"].read_by = it["finish"](t)
                del state[i]

            for i in range(len(items) + 2):
                if i < len(items):
                    if items[i].get("prepare"):
                        items[i]["prepare"]()
                    score(i)
                if 0 <= i - 1 < len(items):
                    turn(i - 1)
                if i >= 2:
                    value(i - 2)
                yield

        h_t = R_HT.cut(KT, TOK)
        gated = R_G.cut(TT, D)
        q_b, q_c, q_d = R_QK.cut(TT, 256), R_QK.cut(TT, 256), R_QK.cut(TT, 256)
        k_b, k_c, k_d = R_QK.cut(1, TOK), R_QK.cut(2, TOK), R_QK.cut(1, TOK)
        v_a, v_b, v_c, v_d = R_V.cut(TT, 256), R_V.cut(TT, P), R_V.cut(TT, 256), R_V.cut(TT, P)
        R_TMP.reset()
        raw = [R_TMP.cut(512), R_TMP.cut(512)]
        t_cos, t_sin = R_TMP.cut(512), R_TMP.cut(512)
        k_rows = R_TMP.cut(256)
        gain_b = R_TMP.cut(384)
        t_small = R_TMP.cut(3, 24)
        raw_free = [[], []]
        k_rows_free = []
        free_cell = {"n": 0, "k_rows": [], "sin": [], "cos": []}

        x_scratch = a["x_scratch"].rearrange("(m p) d -> m p d", p=P)
        x_in = a["x"][0].rearrange("(m p) d -> m p d", p=P)
        ctx_in = a["ctx"][0].rearrange("(m p) d -> m p d", p=P)

        def ada(l):
            t_add = None
            for n in range(6):
                got = [ring.take("ada") for _ in range(KT // 2)]
                b = banks[n % 2]
                T.after(csil_ready, b.read_by)
                for k in range(KT):
                    T.after(got[k // 2][1])
                    mm = pe.matmul(b.ap[0:2, :], csil[:, k, :], got[k // 2][0][:, k % 2, :], start=k == 0, stop=k == KT - 1)
                    if k % 2:
                        t = T.did(mm)
                        ring.release(t)
                row = raw[n % 2]
                S.after(t, raw_free[n % 2])
                t = S.did(act.activation(row[0:2, :], b.ap[0:2, :], ACT.Copy))
                b.read_by = [t]
                b2 = banks[2 + n % 2]
                T.after(t, b2.read_by)
                for j in range(4):
                    mm = pe.transpose(b2.ap[:, 2 * j:2 * j + 2], row[0:2, j * P:(j + 1) * P], ident[0:2, 0:2])
                t = T.did(mm)
                raw_free[n % 2] = [t]
                V.after(t)
                bias = cols_a[:, 24 + 24 * l + 4 * n:24 + 24 * l + 4 * n + 4]
                t_add = V.did(dve.tensor_tensor(ada_t[:, 4 * n:4 * n + 4, :], b2.ap[:, 0:8].rearrange("p (j v) -> p j v", v=2),
                                                bc(bias, 2, [P, 4, 2]), ALU.add))
                b2.read_by = [t_add]
            V.after(t_add)
            return V.did(dve.tensor_scalar(ada_t[:, 8:16, :], ada_t[:, 8:16, :], 1.0, None, ALU.add))

        def modulate(x_tile, x_ready, ada_ready):
            last = []
            for m in range(TT):
                src, free = x_tile(m)
                v = 0 if m < LT else 1
                for half in range(2):
                    b = banks[4 + (2 * m + half) % 4]
                    t = transposed(src[:, half * 512:half * 512 + 512], 4, b, x_ready(m))
                    e = (S, V)[half]
                    e.after(t, ada_ready)
                    for j in range(4):
                        k = 4 * half + j
                        dst, ps = h_t[:, k, m * P:(m + 1) * P], b.ap[:, j * P:(j + 1) * P]
                        if e is S:
                            t = S.did(act.activation(dst, ps, ACT.Identity, bias=ada_t[:, k, v:v + 1], scale=ada_t[:, 8 + k, v:v + 1]))
                        else:
                            t = V.did(dve.tensor_scalar(dst, ps, ada_t[:, 8 + k, v:v + 1], ada_t[:, k, v:v + 1], ALU.mult, ALU.add))
                    b.read_by = [t]
                    last.append(t)
                free(T.now())
            return last

        def heads_rows(m, ps, ready, n_q, n_k, d, gain, q_dst, k_dst, v_dst):
            i = free_cell["n"] % 2
            free_cell["n"] += 1
            r = raw[i]
            nq, nk = n_q * d, n_k * d
            n = nq + nk
            c0 = 0 if q_dst is not None else nq
            S.after(ready, raw_free[i])
            t = S.did(act.activation(r[:, c0:n], ps[:, c0:n], ACT.Copy))
            if v_dst is not None:
                t = S.did(act.activation(v_dst, ps[:, n:512], ACT.Copy))
            read = [t]
            if gain is not None:
                h0 = c0 // d
                nh = n_q + n_k
                sq = t_sin
                V.after(t, free_cell["sin"])
                t = V.did(dve.tensor_tensor(sq[:, c0:n], r[:, c0:n], r[:, c0:n], ALU.mult))
                V.after(t)
                ss = t_small[:, 0, h0:nh]
                t = V.did(dve.reduce_sum(ss, sq[:, c0:n].rearrange("p (h d) -> p h d", d=d), AX))
                t = rstd(ss, 1.0 / d, RMS_EPS, t_small[:, 1, h0:nh], t_small[:, 2, h0:nh], t)
                V.after(t)
                rr = r[:, c0:n].rearrange("p (h d) -> p h d", d=d)
                t = V.did(dve.tensor_tensor(rr, rr, bc(t_small[:, 1, h0:nh], 2, [P, nh - h0, d]), ALU.mult))
                V.after(t, gain_ready[0])
                t = V.did(dve.tensor_tensor(r[:, c0:n], r[:, c0:n], gain_b[:, c0:n], ALU.mult))
            if m < LT:
                cos, sin = (cos64, sin64) if d == HD else (cos32, sin32)
                nh = n // d
                V.after(t, free_cell["sin"])
                V.did(dve.tensor_tensor(t_cos[:, 0:n].rearrange("p (h d) -> p h d", d=d),
                                        r[:, 0:n].rearrange("p (h d) -> p h d", d=d),
                                        bc(cos[:, m, :], 1, [P, nh, d]), ALU.mult))
                x4 = d // 4
                split = lambda ap: ap.rearrange("p (h e s x) -> p h e s x", e=2, s=2, x=x4)
                tab = sin[:, m, :].rearrange("p (e s x) -> p e s x", e=2, s=2)
                for s in range(2):
                    t = V.did(dve.tensor_tensor(split(t_sin[:, 0:n])[:, :, :, s, :], split(r[:, 0:n])[:, :, :, 1 - s, :],
                                                bc(tab[:, :, s, :], 1, [P, nh, 2, x4]), ALU.mult))
                raw_free[i] = [t]
                V.after(t)
                V.did(dve.tensor_tensor(q_dst, t_cos[:, 0:nq], t_sin[:, 0:nq], ALU.add))
                V.after(free_cell["k_rows"])
                t = V.did(dve.tensor_tensor(k_rows[:, 0:nk], t_cos[:, nq:n], t_sin[:, nq:n], ALU.add))
                k_src = k_rows[:, 0:nk]
            else:
                if q_dst is not None:
                    G.after(t)
                    raw_free[i] = [G.did(pool.tensor_copy(q_dst, r[:, 0:nq]))]
                else:
                    raw_free[i] = []
                k_src = r[:, nq:n]
            b = banks[2 + free_cell["n"] % 2]
            t = transposed(k_src, nk // P, b, t)
            if m < LT:
                free_cell["k_rows"] = [t]
            else:
                raw_free[i].append(t)
            S.after(t)
            t = S.did(act.activation(k_dst[:, :, m * P:(m + 1) * P],
                                     b.ap[:, 0:nk].rearrange("p (b n) -> p b n", n=P), ACT.Copy))
            b.read_by = [t]
            return read

        gain_ready = [None]

        def split_halves(ap, h):
            return ap.rearrange("p (n s h) -> p n s h", s=2, h=h)

        def hgrn_inputs(l, t, ctx_out, work):
            rhs = lambda k, t0, t1: h_t[:, k, t0:t1]
            f, r, e, att, att_c, q, k_f, k_b, o = work
            done = []

            def evac_q(t0, t1, ps, ready):
                S.after(ready)
                x = S.did(act.activation(q[:, t0:t1], ps, ACT.Silu))
                done.append(x)
                return [x]

            product_cols("hg", rhs, h_ready[0], [(0, SEQ)] + ([(SEQ, TOK)] if ctx_out else []), (0, 1), evac_q)
            for d, k in ((0, k_f), (1, k_b)):
                def evac_f(t0, t1, ps, ready):
                    S.after(ready)
                    x = S.did(act.activation(f[:, d, t0:t1], ps, ACT.Sigmoid))
                    V.after(x, lb_ready)
                    y = V.did(dve.tensor_scalar(f[:, d, t0:t1], f[:, d, t0:t1], lb1m[:, l, d, t:t + 1], lb[:, l, d, t:t + 1], ALU.mult, ALU.add))
                    V.after(y)
                    V.did(dve.tensor_scalar(k[:, t0:t1], f[:, d, t0:t1], -1.0, 1.0, ALU.mult, ALU.add))
                    y = V.did(dve.tensor_scalar(f[:, d, t0:t1], f[:, d, t0:t1], LOG_FLOOR, None, ALU.max))
                    S.after(y)
                    done.append(S.did(act.activation(f[:, d, t0:t1], f[:, d, t0:t1], ACT.Ln)))
                    return [x]

                product_cols("hg", rhs, h_ready[0], [(0, SEQ), (SEQ, TOK)], (0, 1), evac_f)
            return done

        def hgrn(l, t, ctx_out, work, inputs_ready):
            f, r, e, att, att_c, q, k_f, k_b, o = work
            nq = TOK if ctx_out else SEQ
            att_flat = [att[:, hh].rearrange("p i t -> p (i t)") for hh in range(2)]
            e_free = [[], []]
            G.after(inputs_ready)
            V.after(inputs_ready)
            T.after(inputs_ready)
            t_r = G.did(pool.memset(r[:], 0.0))
            t_k = V.did(dve.tensor_tensor(e[1][:, 1, 0:nq], k_f[:, 0:nq], k_b[:, 0:nq], ALU.add))

            def next_bank():
                bank_turn[0] += 1
                return banks[2 + bank_turn[0] % 6]

            def products(keys, queries, ready):
                T.after(ready)
                got = []
                for g in range(4 if ctx_out else 2):
                    b = next_bank()
                    T.after(b.read_by)
                    hh = g % 2
                    for j in range(LT if g < 2 else CT):
                        c = j if g < 2 else LT + j
                        rows = slice(64 * hh, 64 * hh + 64)
                        mm = pe.matmul(b.ap[:, j * P:(j + 1) * P], keys[rows, c * P:(c + 1) * P],
                                       queries[rows, c * P:(c + 1) * P], start=True, stop=True)
                    got.append((b, T.did(mm)))
                return got

            def places(g):
                if g < 2:
                    x = SEQ + P
                    return [(att_flat[g][:, 0:LT * x].rearrange("p (j x) -> p j x", x=x)[:, :, 0:P], slice(0, 512))]
                return [(att_c[:, g - 2, c, c * P:(c + 1) * P].unsqueeze(1), slice(c * P, (c + 1) * P)) for c in range(CT)]

            got = products(e[1][:, 1], q, t_k)
            base = []
            for g, (b, ready) in enumerate(got):
                S.after(ready)
                for dst, src in places(g):
                    x = S.did(act.activation(dst, b.ap[:, src].rearrange("p (j n) -> p j n", n=P), ACT.Copy))
                b.read_by = [x]
                base.append(x)
            e_free[1] = [T.now()]
            t_upd = t_r
            yield
            for level in range(9):
                h = 1 << level
                n = TOK if level < 8 else SEQ
                E = e[level % 2]
                sf = split_halves(f[:, 0, 0:n], h)
                sb = split_halves(f[:, 1, 0:n], h)
                rf, rb = split_halves(r[:, 0, 0:n], h), split_halves(r[:, 1, 0:n], h)
                eq, ek = split_halves(E[:, 0, 0:n], h), split_halves(E[:, 1, 0:n], h)
                S.after(t_upd, e_free[level % 2])
                S.did(act.activation(eq[:, :, 0], sb[:, :, 0], ACT.Exp))
                S.did(act.activation(eq[:, :, 1], sf[:, :, 1], ACT.Exp))
                S.did(act.activation(ek[:, :, 0], rf[:, :, 0], ACT.Exp))
                t_e = S.did(act.activation(ek[:, :, 1], rb[:, :, 1], ACT.Exp))
                V.after(t_e)
                V.did(dve.tensor_tensor(E[:, 0, 0:min(n, nq)], E[:, 0, 0:min(n, nq)], q[:, 0:min(n, nq)], ALU.mult))
                V.did(dve.tensor_tensor(ek[:, :, 0], ek[:, :, 0], split_halves(k_f[:, 0:n], h)[:, :, 0], ALU.mult))
                t_m = V.did(dve.tensor_tensor(ek[:, :, 1], ek[:, :, 1], split_halves(k_b[:, 0:n], h)[:, :, 1], ALU.mult))
                w = n // (2 * h)
                V.did(dve.tensor_tensor(rf[:, :, 0], rf[:, :, 0], sf[:, :, 1, h - 1:h].to_broadcast([P, w, h]), ALU.add))
                V.did(dve.tensor_tensor(rb[:, :, 1], rb[:, :, 1], sb[:, :, 0, 0:1].to_broadcast([P, w, h]), ALU.add))
                V.after(V.now())
                V.did(dve.tensor_tensor(sf[:, :, 1], sf[:, :, 1], sf[:, :, 0, h - 1:h].to_broadcast([P, w, h]), ALU.add))
                t_upd = V.did(dve.tensor_tensor(sb[:, :, 0], sb[:, :, 0], sb[:, :, 1, 0:1].to_broadcast([P, w, h]), ALU.add))
                V.after(t_upd)
                if h < P:
                    got = products(E[:, 1], E[:, 0], t_m)
                    for g, (b, ready) in enumerate(got):
                        V.after(ready, base)
                        for dst, src in places(g):
                            nb = (src.stop - src.start) // P
                            x = V.did(dve.copy_predicated(dst, bc(level_mask[:, level, :], 1, [P, nb, P]),
                                                          b.ap[:, src].rearrange("p (j n) -> p j n", n=P)))
                        b.read_by = [x]
                elif h == P:
                    T.after(t_m)
                    for g in range(4 if ctx_out else 2):
                        b = next_bank()
                        T.after(b.read_by)
                        blocks = [(g % 2, s, q_) for s, q_ in (((0, 1), (2, 3), (1, 0), (3, 2)) if g < 2 else ((4, 5), (5, 4)))]
                        for j, (hh, s, q_) in enumerate(blocks):
                            rows = slice(64 * hh, 64 * hh + 64)
                            mm = pe.matmul(b.ap[:, j * P:(j + 1) * P], E[rows, 1, s * P:(s + 1) * P],
                                           E[rows, 0, q_ * P:(q_ + 1) * P], start=True, stop=True)
                        ready = T.did(mm)
                        S.after(ready)
                        if g < 2:
                            x = 2 * SEQ + 2 * P
                            for i, at0 in enumerate((P, SEQ)):
                                dst = att_flat[g][:, at0:at0 + 2 * x].rearrange("p (j x) -> p j x", x=x)[:, :, 0:P]
                                y = S.did(act.activation(dst, b.ap[:, i * 256:i * 256 + 256].rearrange("p (j n) -> p j n", n=P), ACT.Copy))
                        else:
                            for j, (hh, s, q_) in enumerate(blocks):
                                y = S.did(act.activation(att_c[:, hh, s - LT, (q_ - LT) * P:(q_ - LT + 1) * P],
                                                         b.ap[:, j * P:(j + 1) * P], ACT.Copy))
                        b.read_by = [y]
                else:
                    T.after(t_m)
                    for hh in range(2):
                        rows = slice(64 * hh, 64 * hh + 64)
                        for s0 in (0, 2):
                            q0 = SEQ // 2 - s0 * P
                            b = banks[2 + (2 * hh + s0 // 2)]
                            T.after(b.read_by)
                            for j in range(2):
                                mm = pe.matmul(b.ap[:, j * 256:(j + 1) * 256], E[rows, 1, (s0 + j) * P:(s0 + j + 1) * P],
                                               E[rows, 0, q0:q0 + 256], start=True, stop=True)
                            ready = T.did(mm)
                            S.after(ready)
                            b.read_by = [S.did(act.activation(att[:, hh, s0:s0 + 2, q0:q0 + 256],
                                                              b.ap[:, 0:512].rearrange("p (j n) -> p j n", n=256), ACT.Copy))]
                e_free[level % 2] = [T.now()]
                yield
            S.after(t_upd, e_free[0], e_free[1])
            for d in range(2):
                S.did(act.activation(e[d][:, 0, 0:SEQ], f[:, d, 0:SEQ], ACT.Exp))
                t_e = S.did(act.activation(e[d][:, 1, SEQ:TOK], r[:, d, SEQ:TOK], ACT.Exp))
            V.after(t_e)
            for d, k in ((0, k_f), (1, k_b)):
                V.did(dve.tensor_tensor(e[d][:, 0, 0:SEQ], e[d][:, 0, 0:SEQ], q[:, 0:SEQ], ALU.mult))
                t_m = V.did(dve.tensor_tensor(e[d][:, 1, SEQ:TOK], e[d][:, 1, SEQ:TOK], k[:, SEQ:TOK], ALU.mult))
            T.after(t_m)
            for hh in range(2):
                rows = slice(64 * hh, 64 * hh + 64)
                for c in range(CT):
                    b = banks[2 + (2 * hh + c)]
                    T.after(b.read_by)
                    for d in range(2):
                        mm = pe.matmul(b.ap[:, 0:SEQ], e[d][rows, 1, SEQ + c * P:SEQ + (c + 1) * P], e[d][rows, 0, 0:SEQ],
                                       start=d == 0, stop=d == 1)
                    x = T.did(mm)
                    S.after(x)
                    b.read_by = [S.did(act.activation(att[:, hh, LT + c, :], b.ap[:, 0:SEQ], ACT.Copy))]
            yield
            att_done = [S.now(), V.now()]
            for j in range(TT if ctx_out else LT):
                b = banks[2 + j % 6]
                T.after(b.read_by, att_done, v_a_ready[0])
                for hh in range(2):
                    if j < LT:
                        terms = [(att[:, hh, i, j * P:(j + 1) * P], i) for i in range(TT)]
                    else:
                        terms = [(att_c[:, hh, c, (j - LT) * P:(j - LT + 1) * P], LT + c) for c in range(CT)]
                    for i, (w_ap, s) in enumerate(terms):
                        mm = pe.matmul(b.ap[:, hh * P:(hh + 1) * P], w_ap, v_a[:, s, t * P:(t + 1) * P],
                                       start=i == 0, stop=i == len(terms) - 1)
                x = T.did(mm)
                S.after(x)
                y = S.did(act.activation(o[:, j, t * P:(t + 1) * P].rearrange("p (h d) -> p h d", d=HD),
                                         b.ap[:, 0:384].rearrange("p (h x) -> p h x", x=192)[:, :, 0:HD], ACT.Copy))
                b.read_by = [y]
            yield

        bank_turn = [0]
        v_a_ready = [None]
        h_ready = [None]

        def head_norm_gate(o, m0, m1, gain, gain_ready_t, scale, c0, ready, sq, st):
            n = (m1 - m0) * NH
            oo = o[:, m0:m1, :]
            V.after(ready)
            t = V.did(dve.tensor_tensor(sq, oo, oo, ALU.mult))
            V.after(t)
            t = V.did(dve.reduce_sum(st[:, 0, 0:n], sq.rearrange("p m (h d) -> p (m h) d", d=HD), AX))
            t = rstd(st[:, 0, 0:n], 1.0 / HD, RMS_EPS, st[:, 1, 0:n], st[:, 2, 0:n], t)
            V.after(t, gain_ready_t)
            o4 = oo.rearrange("p m (h d) -> p (m h) d", d=HD)
            t = V.did(dve.tensor_tensor(o4, o4, bc(st[:, 1, 0:n], 2, [P, n, HD]), ALU.mult))
            V.after(t)
            if scale != 1.0:
                t = V.did(dve.tensor_scalar(oo, oo, scale, None, ALU.mult))
                V.after(t)
            t = V.did(dve.tensor_tensor(o4, o4, bc(gain, 1, [P, n, HD]), ALU.mult))
            V.after(t)
            g = gated[:, m0:m1, c0:c0 + 256]
            return V.did(dve.tensor_tensor(g, g, oo, ALU.mult))

        def hgrn_buffers():
            R_WORK.reset()
            f, r = R_WORK.cut(2, TOK), R_WORK.cut(2, TOK)
            e = [R_WORK.cut(2, TOK), R_WORK.cut(2, TOK)]
            att, att_c = R_WORK.cut(2, TT, SEQ), R_WORK.cut(2, CT, CTX)
            q, k_f, k_b, o = R_WORK.cut(TOK), R_WORK.cut(TOK), R_WORK.cut(TOK), R_WORK.cut(TT, 256)
            return f, r, e, att, att_c, q, k_f, k_b, o

        gain_hg, gain_df = tile("gain_hg", [HD]), tile("gain_df", [HD])
        sinks, neg_sinks = tile("sinks", [NH]), tile("neg_sinks", [NH])
        lam_rows, lam = tile("lam_rows", [4, DQ]), tile("lam", [8])

        def spread(ap, n):
            return ap.unsqueeze(0).to_broadcast([P, n])

        def layer(l, x_tile, x_ready):
            ctx_out = l < DEPTH - 1
            last_q = TT if ctx_out else LT
            lam_init = 0.8 - 0.6 * math.exp(-0.3 * l)
            G.after(*everyone())
            for h in range(NH + NKV):
                load(gain_b[:, h * HD:(h + 1) * HD], spread(a["ga_q_norm_g" if h < NH else "ga_k_norm_g"][l], HD), parameters)
            load(gain_hg[:], spread(a["hg_norm_g"][l], HD), parameters)
            load(gain_df[:], spread(a["df_subln_g"][l], HD), parameters)
            load(sinks[:], spread(a["wn_sink"][l], NH), parameters)
            params = load(lam_rows[:].rearrange("p a b -> p (a b)"), spread(a["df_lambda"][l].rearrange("a b -> (a b)"), 4 * DQ), parameters)
            gain_ready[0] = params
            V.after(params)
            V.did(dve.tensor_scalar(neg_sinks[:], sinks[:], -1.0, None, ALU.mult))
            t = V.did(dve.tensor_tensor(lam_rows[:, 0::2, :], lam_rows[:, 0::2, :], lam_rows[:, 1::2, :], ALU.mult))
            V.after(t)
            t = V.did(dve.reduce_sum(lam[:, 0:2], lam_rows[:, 0::2, :], AX))
            S.after(t)
            t = S.did(act.activation(lam[:, 2:4], lam[:, 0:2], ACT.Exp))
            V.after(t)
            t = V.did(dve.tensor_tensor(lam[:, 4:5], lam[:, 3:4], lam[:, 2:3], ALU.subtract))
            V.after(t)
            t_lam = V.did(dve.tensor_scalar(lam[:, 5:6], lam[:, 4:5], -lam_init, None, ALU.add))

            ada_ready = ada(l)
            h_ready[0] = modulate(x_tile, x_ready, ada_ready)
            fence()
            for e in (T, S, V, G):
                e.after(x_stores_done[0])
            lhs = lambda k, m: h_t[:, k, m * P:(m + 1) * P]
            every = list(range(TT))
            work = hgrn_buffers()
            done_v = {}

            def copy_to(dst, key):
                def evacuate(m, ps, ready):
                    S.after(ready)
                    t = S.did(act.activation(dst(m), ps[:, 0:dst(m).shape[-1]], ACT.Copy))
                    done_v[key] = t
                    return [t]
                return evacuate

            def proj_first():
                yield from product_rows("ai", every, lhs, h_ready[0], 256, (0, 1), copy_to(lambda m: v_a[:, m, :], "a"))
                v_a_ready[0] = done_v["a"]
                skip = lambda lo: (lambda m: (lo, 512) if m >= last_q else None)
                yield from product_rows("b", every, lhs, h_ready[0], 512, (0, 1), lambda m, ps, t: heads_rows(
                    m, ps, t, NH, NKV, HD, gain_b, q_b[:, m, :] if m < last_q else None, k_b, v_b[:, m, :]), cols=skip(256))
                yield from product_rows("c", every, lhs, h_ready[0], 512, (0, 1), lambda m, ps, t: heads_rows(
                    m, ps, t, 8, 8, DQ, None, q_c[:, m, :] if m < last_q else None, k_c, None), cols=skip(256))

            def silu_gate(c0):
                def evacuate(m, ps, ready):
                    S.after(ready)
                    return [S.did(act.activation(gated[:, m, c0:c0 + 512], ps, ACT.Silu))]
                return evacuate

            def proj_second():
                skip = lambda lo: (lambda m: (lo, 512) if m >= last_q else None)
                yield from product_rows("cv", every, lhs, h_ready[0], 256, (0, 1), copy_to(lambda m: v_c[:, m, :], "c"))
                yield from product_rows("d", every, lhs, h_ready[0], 512, (0, 1), lambda m, ps, t: heads_rows(
                    m, ps, t, NH, NKV, HD, None, q_d[:, m, :] if m < last_q else None, k_d, v_d[:, m, :]), cols=skip(256))
                for c0 in (0, 512):
                    yield from product_rows("g", every[0:last_q], lhs, h_ready[0], 512, (0, 1), silu_gate(c0))

            for t, stream in ((0, proj_first), (1, proj_second)):
                inputs = hgrn_inputs(l, t, ctx_out, work)
                if t == 0:
                    st = stream()
                    for _ in range(TT):
                        next(st)
                else:
                    st = stream()
                interleave(hgrn(l, t, ctx_out, work, inputs), st)
                fence()

            sq = R_WORK_view(0, last_q, 256)
            st4 = stats[:, 0:72].rearrange("p (a b) -> p a b", a=3)
            head_norm_gate(work[8], 0, last_q, gain_hg[:], params, 1.0, 0, S.now(), sq, st4)
            fence()

            R_WORK.reset()
            prob = [R_WORK.cut(TOK) for _ in range(4)]
            prob_t = [R_WORK.cut(TOK) for _ in range(2)]
            q_pad = {"b": [[R_WORK.cut(P) for _ in range(4)] for _ in range(2)],
                     "c": [[R_WORK.cut(P) for _ in range(8)] for _ in range(2)]}
            o_c, o_sq = R_WORK.cut(2, 256), R_WORK.cut(2, 256)
            pad_at = R_WORK.start + 6 * TOK
            t_pad = G.did(pool.memset(base[:, pad_at:pad_at + 24 * P], 0.0))
            free = {"p": [[], [], [], []], "pt": [[], []], "pt_second": [[], []]}
            fence()

            def padded_queries(src, sets, n_maps, rows_to, scale):
                n = [0]
                ready = {}
                free_q = [[], []]

                def prepare(m):
                    i = n[0] % 2
                    n[0] += 1
                    b = banks[6 + i]
                    t = transposed(src[:, m, :], 2, b, None)
                    toks = []
                    for g in range(n_maps):
                        e = (S, V)[g % 2]
                        e.after(t, free_q[i], t_pad)
                        r0, r1, w = rows_to(g)
                        blk = g * 2 // n_maps
                        dst, ps = sets[i][g][r1:r1 + w, :], b.ap[r0:r0 + w, blk * P:(blk + 1) * P]
                        if e is S:
                            toks.append(S.did(act.activation(dst, ps, ACT.Copy, scale=scale)))
                        else:
                            toks.append(V.did(dve.tensor_scalar(dst, ps, scale, None, ALU.mult)))
                    b.read_by = toks[-2:]
                    ready["t"] = toks[-2:]
                    return sets[i], i
                return prepare, ready, free_q

            def items_of(kind):
                items = []
                if kind == "c":
                    prepare, ready, free_q = padded_queries(q_c, q_pad["c"], 8, lambda g: (32 * (g % 4), 32 * (g % 4), 32), 1.0)
                else:
                    prepare, ready, free_q = padded_queries(q_b if kind == "b" else q_d, q_pad["b"], 4,
                                                            lambda h: (64 * (h % 2), 64 * (h // 2), 64), HD ** -0.5)
                for m in range(last_q):
                    shared = {"m": m}
                    if m >= LT:
                        lo_tile = hi_tile = LT
                    elif kind == "d":
                        lo_tile, hi_tile = max(m - 1, 0), min(m + 2, LT)
                    else:
                        lo_tile, hi_tile = 0, LT
                    w = (hi_tile - lo_tile) * P
                    lo = SEQ - w
                    tiles = list(range(lo_tile, hi_tile)) + [LT, LT + 1]

                    def make(h, m=m, lo=lo, lo_tile=lo_tile, hi_tile=hi_tile, tiles=tiles, shared=shared, w=w):
                        def segments(kt):
                            s = [(kt[:, lo_tile * P:hi_tile * P], lo)] if w else []
                            return s + [(kt[:, SEQ:TOK], SEQ)]

                        def prepare_m():
                            shared["sets"], shared["i"] = prepare(m)

                        it = {"prepare": prepare_m if h == 0 else None, "q_ready": lambda: ready["t"], "k_ready": None,
                              "range": (lo, TOK), "v_ready": None, "first": h == 0, "bank": banks[m % 2], "col": h * P}
                        if kind == "c":
                            it["maps"] = Lazy(lambda: [(shared["sets"][2 * h + j], segments(k_c[:, (2 * h + j) // 4, :])) for j in range(2)])
                            it["scale"], it["neg_lam"] = DQ ** -0.5, lam[:, 5:6]
                            v = lambda s: v_c[:, s, (h // 2) * P:(h // 2 + 1) * P]
                        else:
                            kt, vv = (k_b, v_b) if kind == "b" else (k_d, v_d)
                            it["maps"] = Lazy(lambda: [(shared["sets"][h], segments(kt[:, 0, :]))])
                            it["scale"] = 1.0
                            v = lambda s: vv[:, s, :]
                        if kind == "d":
                            it["sink"] = (neg_sinks[:, h:h + 1], sinks[:, h:h + 1])
                            if m < LT:
                                it["masks"] = ([(lo, up_mask[:])] if m > 0 else []) + ([(SEQ - P, low_mask[:])] if m < LT - 1 else [])
                        it["blocks"] = [(lo + j * P, P, v(s)) for j, s in enumerate(tiles)]
                        it["rec"] = rec_all[:, kinds.index(kind), m, h:h + 1]
                        if h == NH - 1:
                            it["finish"] = lambda t: finish(kind, m, t, shared, free_q)
                        return it
                    items += [make(h) for h in range(NH)]
                return items

            def finish(kind, m, t, shared, free_q):
                free_q[shared["i"]] = [t]
                b = banks[m % 2]
                rec = rec_all[:, kinds.index(kind), m, :]
                V.after(t, V.now())
                if kind == "c":
                    i = m % 2
                    for h in range(NH):
                        x = V.did(dve.tensor_scalar(o_c[:, i, h * HD:(h + 1) * HD], b.ap[:, h * P + (h % 2) * HD:h * P + (h % 2) * HD + HD],
                                                    rec[:, h:h + 1], None, ALU.mult))
                    st4 = stats_c[:, i]
                    head_norm_gate_c(o_c[:, i:i + 1, :], m, gain_df[:], 1.0 - lam_init, x, o_sq[:, i:i + 1, :], st4)
                    return [x]
                c0 = 256 if kind == "b" else 768
                for h in range(NH):
                    g = gated[:, m, c0 + h * HD:c0 + (h + 1) * HD]
                    x = V.did(dve.scalar_tensor_tensor(g, b.ap[:, h * P + (h // 2) * HD:h * P + (h // 2) * HD + HD], rec[:, h:h + 1], g, ALU.mult, ALU.mult))
                return [x]

            def head_norm_gate_c(o, m, gain, scale, ready, sq, st):
                V.after(ready)
                t = V.did(dve.tensor_tensor(sq, o, o, ALU.mult))
                V.after(t)
                t = V.did(dve.reduce_sum(st[:, 0, :], sq.rearrange("p m (h d) -> p (m h) d", d=HD), AX))
                t = rstd(st[:, 0, :], 1.0 / HD, RMS_EPS, st[:, 1, :], st[:, 2, :], t)
                V.after(t, params)
                o4 = o.rearrange("p m (h d) -> p (m h) d", d=HD)
                t = V.did(dve.tensor_tensor(o4, o4, bc(st[:, 1, :], 2, [P, NH, HD]), ALU.mult))
                V.after(t)
                t = V.did(dve.scalar_tensor_tensor(o4, o4, scale, bc(gain, 1, [P, NH, HD]), ALU.mult, ALU.mult))
                V.after(t)
                g = gated[:, m:m + 1, 512:768]
                return V.did(dve.tensor_tensor(g, g, o, ALU.mult))

            kinds = ["b", "c", "d"]
            V.after(t_lam)
            for kind in kinds:
                for _ in attend(items_of(kind), prob if kind == "c" else prob[0:2], prob_t, free):
                    pass
                fence()

            y_done = []
            for m in range(last_q):
                for half in range(2):
                    b = banks[(2 * m + half) % 8]
                    t = transposed(gated[:, m, half * 512:half * 512 + 512], 4, b, None)
                    e = (S, V)[half]
                    e.after(t)
                    dst = h_t[:, 4 * half:4 * half + 4, m * P:(m + 1) * P]
                    src = b.ap.rearrange("p (j n) -> p j n", n=P)
                    t = S.did(act.activation(dst, src, ACT.Copy)) if e is S else V.did(dve.tensor_copy(dst, src))
                    b.read_by = [t]
                    y_done.append(t)

            R_WORK.reset()
            z, xs = R_WORK.cut(TT, D), R_WORK.cut(TT, D)
            G.after(x_stores_done[0])
            if l == 0:
                load(xs[:, 0:LT, :], a["x"][0].rearrange("(m p) d -> p m d", p=P), parameters)
                load(xs[:, LT:TT, :], a["ctx"][0].rearrange("(m p) d -> p m d", p=P), parameters)
            else:
                load(xs[:, 0:LT, :], a["x_scratch"][0:SEQ].rearrange("(m p) d -> p m d", p=P), parameters)
            ln_g, ln_b, gate_bc, diag = cut_at(R_QK, 0, D), cut_at(R_QK, D, D), cut_at(R_QK, 2 * D, 2 * D).rearrange("p (v d) -> p v d", v=2), cut_at(R_QK, 4 * D, 8 * P).rearrange("p (i n) -> p i n", i=8)
            load(ln_g, spread(a["ln_g"][l], D), parameters)
            tail_ready = load(ln_b, spread(a["ln_b"][l], D), parameters)
            ones = cut_at(R_QK, 5 * D, P)
            t_one = G.did(pool.memset(ones, 1.0))
            free_d = [None] * 2
            for v in range(2 if ctx_out else 1):
                for half in range(2):
                    i = half
                    V.after(free_d[i])
                    for j in range(4):
                        t = V.did(dve.tensor_scalar(diag[:, 4 * i + j, :], ident[:], ada_t[:, 16 + 4 * half + j, v:v + 1], None, ALU.mult))
                    b = banks[half]
                    T.after(t, t_one, b.read_by)
                    t = T.did(pe.matmul(b.ap, ones, diag[:, 4 * i:4 * i + 4, :].rearrange("p i n -> p (i n)"), start=True, stop=True))
                    free_d[i] = t
                    S.after(t)
                    t_gate = S.did(act.activation(gate_bc[:, v, half * 512:half * 512 + 512], b.ap, ACT.Copy))
                    b.read_by = [t_gate]

            bn = stats[:, 0:72].rearrange("p (m a b) -> p m a b", m=6, a=2)
            mv = stats[:, 72:84].rearrange("p (m b) -> p m b", m=6)
            var, rs, tmp6 = stats[:, 84:90], stats[:, 90:96], stats[:, 96:102]
            for n in range(2):
                c0 = 512 * n

                def evacuate(m, ps, ready):
                    zz = z[:, m, c0:c0 + 512]
                    V.after(ready, t_gate, tail_ready)
                    t = V.did(dve.tensor_tensor(zz, ps, gate_bc[:, 0 if m < LT else 1, c0:c0 + 512], ALU.mult))
                    V.after(t)
                    t2 = V.did(dve.scalar_tensor_tensor(zz, xs[:, m, c0:c0 + 512], ALPHA, zz, ALU.mult, ALU.add))
                    V.after(t2)
                    V.did(dve.bn_stats(bn[:, m, n, :], zz))
                    return [t]

                for _ in product_rows("out", list(range(last_q)), lhs, y_done, 512, (2, 3, 4, 5), evacuate):
                    pass
            V.after(V.now())
            for m in range(last_q):
                V.did(dve.bn_aggr(mv[:, m, :], bn[:, m, :, :].rearrange("p a b -> p (a b)")))
            V.after(V.now())
            t = V.did(dve.tensor_copy(var[:, 0:last_q], mv[:, 0:last_q, 1]))
            t = rstd(var[:, 0:last_q], 1.0, LN_EPS, rs[:, 0:last_q], tmp6[:, 0:last_q], t)
            z_ready = []
            for m in range(last_q):
                V.after(t)
                t2 = V.did(dve.tensor_scalar(z[:, m, :], z[:, m, :], mv[:, m, 0:1], rs[:, m:m + 1], ALU.subtract, ALU.mult))
                V.after(t2)
                t2 = V.did(dve.tensor_tensor(z[:, m, :], z[:, m, :], ln_g, ALU.mult))
                G.after(t2)
                t3 = G.did(pool.tensor_tensor(z[:, m, :], z[:, m, :], ln_b, ALU.add))
                z_ready.append(t3)
                if ctx_out and m < LT:
                    G.after(t3)
                    x_stores_done[0] = x_stores.did(pool.dma_start(x_scratch[m], z[:, m, :]))
            return z, z_ready

        def cut_at(region, at_, n):
            assert at_ + n <= region.size
            return base[:, region.start + at_:region.start + at_ + n]

        def R_WORK_view(at_, m, n):
            return cut_at(R_WORK, at_, m * n).rearrange("p (m n) -> p m n", m=m)

        class Lazy:

            def __init__(self, make):
                self.make = make

            def __iter__(self):
                return iter(self.make())

        x_stores_done = [None]
        rec_all = tile("rec_all", [3, TT, NH])
        stats_c = tile("stats_c", [2, 3, NH])

        stage_x = [cut_at(R_V, i * D, D) for i in range(2)]
        stage_free = [None, None]
        arrivals = {}

        def fetch(m):
            src = x_in[m] if m < LT else ctx_in[m - LT]
            G.after(stage_free[m % 2])
            arrivals[m] = x_loads[m % 2].did(pool.dma_start(stage_x[m % 2], src))

        fetch(0)
        fetch(1)

        def tile_0(m):
            def freed(t):
                stage_free[m % 2] = t
                if m + 2 < TT:
                    fetch(m + 2)
            return stage_x[m % 2], freed

        z, z_ready = layer(0, tile_0, lambda m: arrivals[m])
        fence()
        z, z_ready = layer(1, lambda m: (z[:, m, :], lambda t: None), lambda m: z_ready[m])
        fence()

        xn_t = cut_at(R_HT, 0, KT * SEQ).rearrange("p (k t) -> p k t", k=KT)
        y_t = cut_at(R_G, 0, KT * SEQ).rearrange("p (k t) -> p k t", k=KT)
        gates = cut_at(R_G, KT * SEQ, LT * 12).rearrange("p (m g) -> p m g", m=LT)
        R_V.reset()
        ks_t, kw_t = R_V.cut(SEQ), R_V.cut(SEQ)
        v_s, v_w = R_V.cut(LT, P), R_V.cut(LT, P)
        q_2 = R_V.cut(LT, 256)
        kc_t, kc_rows = R_V.cut(N_CMP), R_V.cut(P)
        v_cmp, hid_c = R_V.cut(P), R_V.cut(2, 64)
        rows_b, cols_b, cols_pe = R_V.cut(P), R_V.cut(122), R_V.cut(32)
        R_QK.reset()
        u_g, v_g = R_QK.cut(LT, 256), R_QK.cut(LT, 256)
        z_pad, conv = R_QK.cut(2, SEQ + CONV_K - 1), R_QK.cut(2, SEQ)
        s_b, s_pad = R_QK.cut(2, SEQ), R_QK.cut(2, SEQ + SCONV_K - 1)
        ca = R_QK.cut(SEQ)
        y_b = cut_at(R_HT, KT * SEQ, LT * 256).rearrange("p (m n) -> p m n", m=LT)
        y_row = cut_at(R_HT, KT * SEQ + LT * 256, LT * 256).rearrange("p (m n) -> p m n", m=LT)
        R_WORK.reset()
        R_WORK.cut(LT, D)
        w1 = [R_WORK.cut(CMP_HID * 16).rearrange("p (k e) -> p k e", e=CMP_HID) for _ in range(2)]
        w2 = [R_WORK.cut(HD) for _ in range(2)]
        blocks_c = [R_WORK.cut(16, 2 * N_CMP) for _ in range(2)]
        gain2 = R_WORK.cut(4, HD)
        ln_rows = R_WORK.cut(4, 256)
        ws, ws_t = R_WORK.cut(4, P), R_WORK.cut(4, P)
        tri, cmp_mask, cmp_valid = R_WORK.cut(P), R_WORK.cut(LT, N_CMP), R_WORK.cut(LT, N_CMP)
        rows_pe = R_WORK.cut(P)
        prob = [R_WORK.cut(SEQ) for _ in range(2)]
        prob_t = [R_WORK.cut(SEQ) for _ in range(2)]
        q_pad2 = [[R_WORK.cut(P) for _ in range(4)] for _ in range(2)]
        tmp2 = [t_cos, t_sin]

        params2 = Transfers(sem("parameters_2"))
        r0 = 0
        for src, n in ((a["norm1_g_2"][0].rearrange("(k p) -> k p", p=P), 8), (a["norm2_g_2"][0].rearrange("(k p) -> k p", p=P), 8),
                       (a["gmlp_bs_2"][0], 4), (a["conf_conv_b_2"][0].rearrange("(k p) -> k p", p=P), 2),
                       (a["conf_conv_w_2"][0][:, 0:P], CONV_K), (a["conf_conv_w_2"][0][:, P:256], CONV_K),
                       (a["sconv_w_2"][0][:, 0:P], SCONV_K), (a["sconv_w_2"][0][:, P:256], SCONV_K),
                       (a["b_gate_2"][0].rearrange("(k p) -> k p", p=P), 32)):
            load(rows_b[r0:r0 + n, :], src, params2)
            r0 += n
        N1, N2, BS, CB, CW, SW, BG = 0, 8, 16, 20, 22, 84, 90
        for i in range(2):
            load(rows_pe[16 * i:16 * i + 16, :], a["nsa_cmp_pe_2"][0, i].rearrange("(k s) d -> k (s d)", s=2), params2)
            load(w1[i], a["nsa_cmp_w1_2"][0, i].rearrange("(k p) e -> p k e", p=P), params2)
            load(w2[i], a["nsa_cmp_w2_2"][0, i], params2)
        load(gain2[:, 0, :], spread(a["nsa_q_norm_g_2"][0], HD), params2)
        load(gain2[:, 1:4, :].rearrange("p a b -> p (a b)"), spread(a["nsa_k_norm_g_2"][0].rearrange("a b -> (a b)"), 3 * HD), params2)
        for i, name in enumerate(("gmlp_ln_g_2", "gmlp_ln_b_2", "conf_ln_g_2", "conf_ln_b_2")):
            load(ln_rows[:, i, :], spread(a[name][0], 256), params2)
        load(ws, a["gmlp_ws_2"][0].rearrange("g t s -> t g s"), params2)
        load(tri, a["c_tri"], params2)
        load(cmp_mask, a["c_cmp_mask"], params2)
        ready2 = load(cmp_valid, a["c_cmp_valid"], params2)

        T.after(ready2)
        t = T.did(pe.transpose(banks[0].ap[:, 0:122], rows_b[0:122, :], ident[0:122, 0:122]))
        S.after(t)
        t = S.did(act.activation(cols_b, banks[0].ap[:, 0:122], ACT.Copy))
        banks[0].read_by = [t]
        t = T.did(pe.transpose(banks[1].ap[:, 0:32], rows_pe[0:32, :], ident[0:32, 0:32]))
        S.after(t)
        t_cols = S.did(act.activation(cols_pe, banks[1].ap[:, 0:32], ACT.Copy))
        banks[1].read_by = [t_cols]
        V.after(ready2, t_cols)
        t_pad = [G.did(pool.memset(x, 0.0)) for x in
                 (z_pad[:, :, 0:CONV_K - 1], s_pad[:, :, 0:SCONV_K - 1], base[:, R_WORK.start + R_WORK.at - 8 * P:R_WORK.start + R_WORK.at])][-1]

        for g in range(4):
            t = V.did(dve.tensor_tensor(ws[:, g, :], ws[:, g, :], tri, ALU.mult))
        t = transposed(ws.rearrange("p g s -> p (g s)"), 4, banks[2], t)
        S.after(t)
        t_ws = S.did(act.activation(ws_t, banks[2].ap.rearrange("p (g n) -> p g n", n=P), ACT.Copy))
        banks[2].read_by = [t_ws]

        def rms_turned(gain_at, z_ready):
            ss, rs, tmp = stats[:, 0:4], stats[:, 4:8], stats[:, 8:12]
            junk = [ca, prob[0]]
            S.after(z_ready)
            for m in range(LT):
                for half in range(2):
                    S.after(S.now())
                    t = S.did(act.activation(raw[half], z[:, m, half * 512:half * 512 + 512], ACT.Square,
                                             accum_out=stats[:, 16 + 2 * m + half:17 + 2 * m + half]))
            V.after(t)
            t = V.did(dve.reduce_sum(ss, stats[:, 16:24].rearrange("p (m h) -> p m h", h=2), AX))
            t = rstd(ss, 1.0 / D, RMS_EPS, rs, tmp, t)
            done = []
            row_free = [S.now(), S.now()]
            for m in range(LT):
                for half in range(2):
                    row = raw[half]
                    V.after(row_free[half], z_ready, t)
                    x = V.did(dve.tensor_scalar(row, z[:, m, half * 512:half * 512 + 512], rs[:, m:m + 1], None, ALU.mult))
                    b = banks[4 + (2 * m + half) % 4]
                    x = transposed(row, 4, b, x)
                    row_free[half] = x
                    if half == 0:
                        S.after(x, t_cols)
                        for j in range(4):
                            y = S.did(act.activation(xn_t[:, j, m * P:(m + 1) * P], b.ap[:, j * P:(j + 1) * P], ACT.Copy,
                                                     scale=cols_b[:, gain_at + j:gain_at + j + 1]))
                    else:
                        V.after(x, t_cols)
                        y = V.did(dve.tensor_tensor(xn_t[:, 4:8, m * P:(m + 1) * P], b.ap.rearrange("p (j n) -> p j n", n=P),
                                                    bc(cols_b[:, gain_at + 4:gain_at + 8], 2, [P, 4, P]), ALU.mult))
                    b.read_by = [y]
                    done.append(y)
            return done

        xn_ready = rms_turned(N1, z_ready)
        lhs2 = lambda k, m: xn_t[:, k, m * P:(m + 1) * P]
        rhs2 = lambda k, t0, t1: xn_t[:, k, t0:t1]
        latent = list(range(LT))

        def run(gen):
            for _ in gen:
                pass

        def layer_norm_rows(x, ready, gain, offset, st):
            V.after(ready)
            t = V.did(dve.bn_stats(st[:, 0:6], x))
            V.after(t)
            t = V.did(dve.bn_aggr(st[:, 6:8], st[:, 0:6]))
            t = rstd(st[:, 7:8], 1.0, LN_EPS, st[:, 8:9], st[:, 9:10], t)
            V.after(t)
            t = V.did(dve.tensor_scalar(x, x, st[:, 6:7], st[:, 8:9], ALU.subtract, ALU.mult))
            V.after(t)
            t = V.did(dve.tensor_tensor(x, x, gain, ALU.mult))
            V.after(t)
            return V.did(dve.tensor_tensor(x, x, offset, ALU.add))

        def turn_rows(src, n_pair, ready):
            def one(m, bank):
                t = transposed(src[:, m, :], 2, bank, ready)
                S.after(t)
                t = S.did(act.activation(y_t[:, 2 * n_pair:2 * n_pair + 2, m * P:(m + 1) * P],
                                         bank.ap[:, 0:256].rearrange("p (j n) -> p j n", n=P), ACT.Copy))
                bank.read_by = [t]
                return t
            return one

        y_t_ready = []

        def gmlp_in(m, ps, ready):
            S.after(ready)
            S.did(act.activation(u_g[:, m, :], ps[:, 0:256], ACT.Gelu_apprx_tanh))
            t = S.did(act.activation(v_g[:, m, :], ps[:, 256:512], ACT.Gelu_apprx_tanh))
            gelu_done.append(t)
            return [t]

        gelu_done = []
        run(product_rows("gmlp", latent, lhs2, xn_ready, 512, (0, 1), gmlp_in))
        for m in latent:
            t = layer_norm_rows(v_g[:, m, :], gelu_done[m], ln_rows[:, 0, :], ln_rows[:, 1, :], stats[:, 32 + 12 * m:44 + 12 * m])
            b = banks[2 + m % 2]
            T.after(t, t_ws, b.read_by)
            for g in range(4):
                mm = pe.matmul(b.ap[:, g * 64:(g + 1) * 64], ws_t[:, g, :], v_g[:, m, g * 64:(g + 1) * 64], start=True, stop=True)
            t = T.did(mm)
            V.after(t)
            for g in range(4):
                t = V.did(dve.scalar_tensor_tensor(u_g[:, m, g * 64:(g + 1) * 64], b.ap[:, g * 64:(g + 1) * 64],
                                                   cols_b[:, BS + g:BS + g + 1], u_g[:, m, g * 64:(g + 1) * 64], ALU.add, ALU.mult))
            b.read_by = [t]
            y_t_ready.append(turn_rows(u_g, 0, t)(m, banks[4 + m % 2]))

        def head_rows_2(dst, gain, n_heads, st):
            n = n_heads * HD
            i = free_cell["n"] % 2
            free_cell["n"] += 1

            def go(ready):
                V.after(ready)
                t = V.did(dve.tensor_tensor(tmp2[i][0:dst.shape[0], 0:n], dst, dst, ALU.mult))
                V.after(t)
                t = V.did(dve.reduce_sum(st[:, 0:n_heads], tmp2[i][0:dst.shape[0], 0:n].rearrange("p (h d) -> p h d", d=HD), AX))
                t = rstd(st[:, 0:n_heads], 1.0 / HD, RMS_EPS, st[:, 4:4 + n_heads], st[:, 8:8 + n_heads], t)
                V.after(t)
                d3 = dst.rearrange("p (h d) -> p h d", d=HD)
                t = V.did(dve.tensor_tensor(d3, d3, bc(st[:, 4:4 + n_heads], 2, [dst.shape[0], n_heads, HD]), ALU.mult))
                V.after(t)
                return V.did(dve.tensor_tensor(d3, d3, bc(gain, 1, [dst.shape[0], n_heads, HD]), ALU.mult))
            return go

        def q_in(m, ps, ready):
            S.after(ready)
            t = S.did(act.activation(q_2[:, m, :], ps[:, 0:256], ACT.Copy))
            head_rows_2(q_2[:, m, :], gain2[:, 0, :], NH, stats[:, 96 + 12 * m:108 + 12 * m])(t)
            return [t]

        run(product_rows("q", latent, lhs2, xn_ready, 256, (0, 1), q_in))

        k_tmp = [raw[0], raw[1]]
        k_tmp_free = [T.now(), T.now()]

        def kv_in(m, ps, ready):
            i = m % 2
            S.after(ready, k_tmp_free[i])
            S.did(act.activation(k_tmp[i][:, 0:P], ps[:, 0:P], ACT.Copy))
            S.did(act.activation(v_s[:, m, :], ps[:, P:2 * P], ACT.Copy))
            S.did(act.activation(k_tmp[i][:, P:2 * P], ps[:, 2 * P:3 * P], ACT.Copy))
            t_read = S.did(act.activation(v_w[:, m, :], ps[:, 3 * P:4 * P], ACT.Copy))
            for j in range(2):
                t = head_rows_2(k_tmp[i][:, j * P:(j + 1) * P], gain2[:, 2 + j, :], NKV, stats[:, 144 + 12 * (2 * m + j):156 + 12 * (2 * m + j)])(t_read)
            b = banks[2 + m % 2]
            t = transposed(k_tmp[i][:, 0:256], 2, b, t)
            k_tmp_free[i] = t
            S.after(t)
            S.did(act.activation(ks_t[:, m * P:(m + 1) * P], b.ap[:, 0:P], ACT.Copy))
            b.read_by = [S.did(act.activation(kw_t[:, m * P:(m + 1) * P], b.ap[:, P:2 * P], ACT.Copy))]
            return [t_read]

        run(product_rows("kv", latent, lhs2, xn_ready, 512, (0, 1), kv_in))

        def ng_in(m, ps, ready):
            S.after(ready)
            return [S.did(act.activation(gates[:, m, :], ps[:, 0:12], ACT.Sigmoid))]

        run(product_rows("ng", latent, lhs2, xn_ready, P, (0, 1), ng_in))

        compress_ready = []
        for i in range(2):
            def blocks_in(t0, t1, ps, ready):
                (S, V)[i].after(ready)
                for hh in range(2):
                    src = ps[64 * hh:64 * hh + 64, :].rearrange("p (n k s) -> p s k n", k=8, s=2)
                    for s in range(2):
                        dst = blocks_c[i][64 * s:64 * s + 64, :, hh * N_CMP:(hh + 1) * N_CMP]
                        for part in range(2):
                            k8 = slice(8 * part, 8 * part + 8)
                            if i == 0:
                                t = S.did(act.activation(dst[:, k8, :], src[:, s, :, part:part + N_CMP], ACT.Copy))
                            else:
                                t = V.did(dve.tensor_copy(dst[:, k8, :], src[:, s, :, part:part + N_CMP]))
                V.after(t)
                compress_ready.append(V.did(dve.tensor_tensor(blocks_c[i], blocks_c[i], bc(cols_pe[:, 16 * i:16 * i + 16], 2, [P, 16, 2 * N_CMP]), ALU.add)))
                return [t]

            product_cols("fm", rhs2, xn_ready, [(0, SEQ)], (i,), blocks_in)

        for i in range(2):
            b = banks[2 + i]
            T.after(compress_ready[i], b.read_by)
            for k in range(16):
                mm = pe.matmul(b.ap[:, 0:2 * N_CMP], w1[i][:, k, :], blocks_c[i][:, k, :], start=k == 0, stop=k == 15)
            t = T.did(mm)
            S.after(t)
            t = S.did(act.activation(hid_c[:, i, 0:2 * N_CMP], b.ap[:, 0:2 * N_CMP], ACT.Gelu_apprx_tanh))
            b.read_by = [t]
            b = banks[4 + i]
            T.after(t, b.read_by)
            for hh in range(2):
                mm = pe.matmul(b.ap[0:N_CMP, hh * 64:(hh + 1) * 64], hid_c[:, i, hh * N_CMP:(hh + 1) * N_CMP], w2[i], start=True, stop=True)
            t = T.did(mm)
            S.after(t)
            dst = (kc_rows, v_cmp)[i][0:N_CMP, :]
            t = S.did(act.activation(dst, b.ap[0:N_CMP, 0:P], ACT.Copy))
            b.read_by = [t]
            if i == 0:
                t = head_rows_2(dst, gain2[0:N_CMP, 1, :], NKV, stats[0:N_CMP, 240:252])(t)
                b = banks[6]
                T.after(t, b.read_by)
                t = T.did(pe.transpose(b.ap[:, 0:N_CMP], dst, ident[0:N_CMP, 0:N_CMP]))
                S.after(t)
                t_kc = S.did(act.activation(kc_t, b.ap[:, 0:N_CMP], ACT.Copy))
                b.read_by = [t_kc]

        for c in range(2):
            def ca_in(t0, t1, ps, ready):
                S.after(ready)
                return [S.did(act.activation(z_pad[:, c, CONV_K - 1:], ps, ACT.Copy))]
            product_cols("fm", rhs2, xn_ready, [(0, SEQ)], (c,), ca_in)
        z_gated = []
        for c in range(2):
            def cb_in(t0, t1, ps, ready):
                S.after(ready, z_gated)
                t = S.did(act.activation(ca, ps, ACT.Sigmoid))
                V.after(t, t_pad)
                z_gated.append(V.did(dve.tensor_tensor(z_pad[:, c, CONV_K - 1:], z_pad[:, c, CONV_K - 1:], ca, ALU.mult)))
                return [t]
            product_cols("fm", rhs2, xn_ready, [(0, SEQ)], (c,), cb_in)
        for c in range(2):
            def sb_in(t0, t1, ps, ready):
                S.after(ready)
                return [S.did(act.activation(s_b[:, c, :], ps, ACT.Copy))]
            product_cols("fm", rhs2, xn_ready, [(0, SEQ)], (c,), sb_in)
        for c in range(2):
            def sc_in(t0, t1, ps, ready):
                S.after(ready)
                return [S.did(act.activation(s_pad[:, c, SCONV_K - 1:], ps, ACT.Copy))]
            product_cols("fm", rhs2, xn_ready, [(0, SEQ)], (c,), sc_in)
        s_gated = []
        for c in range(2):
            def sh_in(t0, t1, ps, ready):
                V.after(ready, S.now(), t_pad)
                s_gated.append(V.did(dve.tensor_tensor(s_pad[:, c, SCONV_K - 1:], s_pad[:, c, SCONV_K - 1:], ps, ALU.mult)))
                return [s_gated[-1]]
            product_cols("fm", rhs2, xn_ready, [(0, SEQ)], (c,), sh_in)

        def causal_conv(dst, src, taps, w_at, bias):
            first = cols_b[:, w_at:w_at + 1]
            if bias is None:
                t = V.did(dve.tensor_scalar(dst, src[:, 0:SEQ], first, None, ALU.mult))
            else:
                t = V.did(dve.tensor_scalar(dst, src[:, 0:SEQ], first, bias, ALU.mult, ALU.add))
            for j in range(1, taps):
                V.after(t)
                t = V.did(dve.scalar_tensor_tensor(dst, src[:, j:j + SEQ], cols_b[:, w_at + j:w_at + j + 1], dst, ALU.mult, ALU.add))
            return t

        V.after(s_gated, z_gated)
        for c in range(2):
            y = y_t[:, 6 + c, :]
            t = causal_conv(y, s_pad[:, c, :], SCONV_K, SW + SCONV_K * c, None)
            V.after(t)
            y_t_ready.append(V.did(dve.tensor_tensor(y, y, s_b[:, c, :], ALU.mult)))
        conv_done = [causal_conv(conv[:, c, :], z_pad[:, c, :], CONV_K, CW + CONV_K * c, cols_b[:, CB + c:CB + c + 1]) for c in range(2)]
        for m in latent:
            b = banks[2 + m % 2]
            T.after(conv_done, b.read_by)
            for c in range(2):
                mm = pe.transpose(b.ap[:, c * P:(c + 1) * P], conv[:, c, m * P:(m + 1) * P], ident[:])
            t = T.did(mm)
            S.after(t)
            t = S.did(act.activation(y_row[:, m, :], b.ap[:, 0:256], ACT.Copy))
            b.read_by = [t]
            t = layer_norm_rows(y_row[:, m, :], t, ln_rows[:, 2, :], ln_rows[:, 3, :], stats[:, 256 + 12 * m:268 + 12 * m])
            S.after(t)
            t = S.did(act.activation(y_row[:, m, :], y_row[:, m, :], ACT.Silu))
            y_t_ready.append(turn_rows(y_row, 2, t)(m, banks[4 + m % 2]))

        fence()

        free = {"p": [[], []], "pt": [[], []], "pt_second": [[], []]}
        cell = {"n": 0, "group": 0, "ready": None}
        free_q = [[], []]

        def prepare_2(m, shared):
            i = m % 2
            b = banks[6 + i]
            t = transposed(q_2[:, m, :], 2, b, None)
            toks = []
            for h in range(NH):
                e = (S, V)[h % 2]
                e.after(t, free_q[i], t_pad)
                dst = q_pad2[i][h][64 * (h // 2):64 * (h // 2) + 64, :]
                ps = b.ap[64 * (h % 2):64 * (h % 2) + 64, (h // 2) * P:(h // 2 + 1) * P]
                if e is S:
                    toks.append(S.did(act.activation(dst, ps, ACT.Copy, scale=HD ** -0.5)))
                else:
                    toks.append(V.did(dve.tensor_scalar(dst, ps, HD ** -0.5, None, ALU.mult)))
            b.read_by = toks[-2:]
            cell["ready"] = toks[-2:]

        items = []
        for m in latent:
            for branch in range(3):
                g = 3 * m + branch
                for h in range(NH):
                    it = {"q_ready": lambda: cell["ready"], "k_ready": None, "v_ready": None, "first": h == 0,
                          "bank": banks[g % 2], "col": h * P, "scale": 1.0, "rec": rec_all[:, branch, m, h:h + 1]}
                    if branch == 0 and h == 0:
                        it["prepare"] = lambda m=m: prepare_2(m, None)
                    if branch == 0:
                        it["maps"] = [(q_pad2[m % 2][h], [(kc_t, 0)])]
                        it["range"], it["masks"] = (0, N_CMP), [(0, cmp_mask[:, m, :])]
                        it["valid"] = cmp_valid[:, m, :]
                        it["blocks"] = [(0, N_CMP, v_cmp[0:N_CMP, :])]
                    else:
                        kt, vv = (ks_t, v_s) if branch == 1 else (kw_t, v_w)
                        it["maps"] = [(q_pad2[m % 2][h], [(kt[:, 0:(m + 1) * P], 0)])]
                        it["range"], it["masks"] = (0, (m + 1) * P), [(m * P, low_mask[:])]
                        it["blocks"] = [(j * P, P, vv[:, j, :]) for j in range(m + 1)]
                    if h == NH - 1:
                        def finish(t, m=m, branch=branch, g=g):
                            b = banks[g % 2]
                            rec = rec_all[:, branch, m, :]
                            V.after(V.now(), t)
                            x = V.did(dve.tensor_tensor(rec, rec, gates[:, m, :].rearrange("p (h b) -> p b h", b=3)[:, branch, :], ALU.mult))
                            V.after(x)
                            for h in range(NH):
                                o = b.ap[:, h * P + (h // 2) * HD:h * P + (h // 2) * HD + HD]
                                y = y_b[:, m, h * HD:(h + 1) * HD]
                                if branch == 0:
                                    x = V.did(dve.tensor_scalar(y, o, rec[:, h:h + 1], None, ALU.mult))
                                else:
                                    x = V.did(dve.scalar_tensor_tensor(y, o, rec[:, h:h + 1], y, ALU.mult, ALU.add))
                            if branch == 2:
                                free_q[m % 2] = [t]
                                y_b_ready[m] = x
                            return [x]
                        it["finish"] = finish
                    items.append(it)
        y_b_ready = {}
        run(attend(items, prob, prob_t, free))
        for m in latent:
            y_t_ready.append(turn_rows(y_b, 1, y_b_ready[m])(m, banks[4 + m % 2]))
        fence()

        mixed = cut_at(R_QK, 0, KT * SEQ).rearrange("p (k t) -> p k t", k=KT)
        sig = [cut_at(R_QK, KT * SEQ + i * SEQ, SEQ) for i in range(4)]
        sig_free = [None] * 4
        acc_ready = []
        for d in range(KT):
            gate_done = []
            for n in range(4):
                def gate_in(t0, t1, ps, ready):
                    S.after(ready, sig_free[n])
                    t = S.did(act.activation(sig[n], ps, ACT.Sigmoid, bias=cols_b[:, BG + n * KT + d:BG + n * KT + d + 1]))
                    gate_done.append(t)
                    return [t]
                product_cols("gate", rhs2, xn_ready, [(0, SEQ)], (n % 2,), gate_in)
            view, arrived = ring.take("branch")
            T.after(arrived, y_t_ready)
            for n in range(4):
                b = banks[2 + (4 * d + n) % 6]
                T.after(b.read_by)
                for c in range(2):
                    mm = pe.matmul(b.ap, view[:, 2 * n + c, :], y_t[:, 2 * n + c, :], start=c == 0, stop=c == 1)
                t = T.did(mm)
                if n == 3:
                    ring.release(t)
                V.after(t, gate_done[n])
                if n == 0:
                    x = V.did(dve.tensor_tensor(mixed[:, d, :], b.ap, sig[n], ALU.mult))
                    b.read_by = [x]
                    sig_free[n] = x
                else:
                    x = V.did(dve.tensor_tensor(sig[n], b.ap, sig[n], ALU.mult))
                    b.read_by = [x]
                    V.after(x)
                    sig_free[n] = x = V.did(dve.tensor_tensor(mixed[:, d, :], mixed[:, d, :], sig[n], ALU.add))
            acc_ready.append(x)

        def add_to_x(c0):
            def evacuate(m, ps, ready):
                V.after(ready)
                t = V.did(dve.tensor_tensor(z[:, m, c0:c0 + 512], z[:, m, c0:c0 + 512], ps, ALU.add))
                x_new.append(t)
                return [t]
            return evacuate

        x_new = []
        for n in range(2):
            run(product_rows("out2", latent, lambda k, m: mixed[:, k, m * P:(m + 1) * P], acc_ready, 512, (2, 3, 4, 5), add_to_x(512 * n)))
        fence()
        hn_ready = rms_turned(N2, x_new)
        fence()

        hid = base[:, R_WORK.start + LT * D:R_WORK.start + LT * D + FT * SEQ].rearrange("p (f t) -> p f t", f=FT)
        relu = [cut_at(R_QK, i * SEQ, SEQ) for i in range(2)]
        relu_free = [None, None]
        hid_ready = []
        for f in range(FT):
            def mlp_in(t0, t1, ps, ready):
                i = f % 2
                S.after(ready, relu_free[i])
                t = S.did(act.activation(relu[i], ps, ACT.Relu))
                V.after(t)
                relu_free[i] = V.did(dve.tensor_tensor(hid[:, f, :], relu[i], relu[i], ALU.mult))
                hid_ready.append(relu_free[i])
                return [t]
            product_cols("mlp1", rhs2, hn_ready, [(0, SEQ)], (f % 2,), mlp_in)
        out_rows = out[0].rearrange("(m p) d -> m p d", p=P)
        for n in range(2):
            acc = [banks[4 * (1 - n) + m] for m in latent]
            for f2 in range(FT // 2):
                view, arrived = ring.take("mlp2")
                T.after(arrived)
                for m in latent:
                    if f2 == 0:
                        T.after(acc[m].read_by)
                    for k in range(2):
                        f = 2 * f2 + k
                        T.after(hid_ready[f])
                        mm = pe.matmul(acc[m].ap, hid[:, f, m * P:(m + 1) * P], view[:, k, :], start=f == 0, stop=f == FT - 1)
                    if f2 == FT // 2 - 1:
                        t = T.did(mm)
                        V.after(t)
                        c0 = 512 * n
                        x = V.did(dve.tensor_tensor(z[:, m, c0:c0 + 512], z[:, m, c0:c0 + 512], acc[m].ap, ALU.add))
                        acc[m].read_by = [x]
                        G.after(x)
                        stored = out_stores.did(pool.dma_start(out_rows[m][:, c0:c0 + 512], z[:, m, c0:c0 + 512]))
                ring.release(T.did(mm) if f2 < FT // 2 - 1 else t)
        G.after(stored)
        Y.after(stored)


_INPUTS = ["x", "c", "ctx", "c_ctx", "w_in", "w_out", "w_ada", "b_ada", "ln_g", "ln_b", "hg_lb_logits", "hg_norm_g",
           "ga_q_norm_g", "ga_k_norm_g", "df_lambda", "df_subln_g", "wn_sink", "norm1_g_2", "w_in_2", "gmlp_ln_g_2",
           "gmlp_ln_b_2", "gmlp_ws_2", "gmlp_bs_2", "nsa_q_norm_g_2", "nsa_k_norm_g_2", "nsa_cmp_pe_2",
           "nsa_cmp_w1_2", "nsa_cmp_w2_2", "conf_conv_w_2", "conf_conv_b_2", "conf_ln_g_2", "conf_ln_b_2",
           "sconv_w_2", "w_branch_2", "w_gate_2", "b_gate_2", "w_out_2", "norm2_g_2", "w_mlp1_2", "w_mlp2_2"]


def shape_constants():
    f = np.float32
    i = np.arange(P)
    out = {"c_ident": np.eye(P, dtype=f)}
    levels = [(i[:, None] // (2 << n) == i[None, :] // (2 << n)) & (i[:, None] // (1 << n) != i[None, :] // (1 << n)) for n in range(7)]
    out["c_levels"] = np.stack(levels, 1).astype(f)
    out["c_low"] = np.where(i[None, :] <= i[:, None], 0.0, -1e30).astype(f)
    out["c_up"] = np.where(i[None, :] >= i[:, None], 0.0, -1e30).astype(f)
    out["c_tri"] = (i[None, :] <= i[:, None]).astype(f)
    t = np.arange(SEQ)
    row, col = (t // GRID_W).astype(f), (t % GRID_W).astype(f)
    for dim in (HD, DQ):
        axis = dim // 2
        inv = (f(10000.0) ** (-np.arange(0, axis, 2, dtype=f) / f(axis))).astype(f)
        ar, ac = row[:, None] * inv, col[:, None] * inv
        cos = np.concatenate([np.cos(ar), np.cos(ar), np.cos(ac), np.cos(ac)], -1)
        sin = np.concatenate([-np.sin(ar), np.sin(ar), -np.sin(ac), np.sin(ac)], -1)
        for name, v in (("cos", cos), ("sin", sin)):
            out[f"c_{name}{dim}"] = np.ascontiguousarray(v.astype(f).reshape(LT, P, dim).transpose(1, 0, 2))
    last = np.arange(N_CMP) * CMP_STRIDE + CMP_LEN - 1
    valid = (last[None, :] <= t[:, None]).reshape(LT, P, N_CMP).transpose(1, 0, 2)
    out["c_cmp_valid"] = np.ascontiguousarray(valid.astype(f))
    out["c_cmp_mask"] = np.ascontiguousarray(np.where(valid, 0.0, -1e30).astype(f))
    return out


def kernel(**inputs):
    import concourse.bacc as bacc
    from concourse.bass_utils import run_bass_kernel_spmd

    nc = bacc.Bacc("TRN2", target_bir_lowering=False, num_devices=1)
    arrays, aps = {}, {}
    for name in _INPUTS:
        arrays[f"in_{name}"] = np.ascontiguousarray(inputs[name])
    for name, value in shape_constants().items():
        arrays[f"in_{name}"] = value
    for name, value in arrays.items():
        aps[name[3:]] = nc.dram_tensor(name, value.shape, mybir.dt.from_np(value.dtype), kind="ExternalInput").ap()
    aps["x_scratch"] = nc.dram_tensor("x_scratch", (SEQ, D), F32, kind="Internal").ap()
    result = nc.dram_tensor("result", (1, SEQ, D), F32, kind="ExternalOutput").ap()
    build(nc, aps, result)
    r = run_bass_kernel_spmd(nc, [arrays], core_ids=[0])
    return r.results[0]["result"]
```

```python
import math
from contextlib import ExitStack

import numpy as np

import concourse.bass as bass
from concourse import mybir
from concourse.alu_op_type import AluOpType as ALU

F32 = mybir.dt.float32
U8 = mybir.dt.uint8
I32 = mybir.dt.int32
F32R = mybir.dt.float32r
ACT = mybir.ActivationFunctionType
AX = mybir.AxisListType.X

P = 128
D = 1024
KT = D // P
SEQ, CTX = 512, 256
TOK = SEQ + CTX
LT, CT = SEQ // P, CTX // P
TT = LT + CT
DEPTH = 2
GRID_W = 64
HD = 64
DQ = 32
NH, NKV = 4, 2
IN_W = 3840
C_AQ, C_AI, C_FF, C_FB, C_B, C_C, C_CV, C_D, C_G = 0, 256, 512, 768, 1024, 1536, 2048, 2304, 2816
IN_W2 = 2828
N_CMP, CMP_LEN, CMP_STRIDE, CMP_HID = 31, 32, 16, 128
CONV_K, SCONV_K = 31, 3
D_FF = 4096
FT = D_FF // P
RSQRT_GUESS = float(0x5F3759DF)
RMS_EPS, LN_EPS = 1e-6, 1e-5
ALPHA = (2.0 * DEPTH) ** 0.25
SLOT = 1024
N_SLOTS = 6
ARENA = 50632
LOG_FLOOR = 1e-19


class Engine:

    def __init__(self, eng, sem):
        self.eng, self.sem, self.count, self.seen = eng, sem, 0, {}

    def after(self, *tokens):
        for t in tokens:
            if t is None:
                continue
            if isinstance(t, list):
                self.after(*t)
                continue
            sem, value = t
            if self.seen.get(id(sem), 0) < value:
                self.seen[id(sem)] = value
                self.eng.wait_ge(sem, value)

    def did(self, instruction):
        self.count += 1
        instruction.then_inc(self.sem, 1)
        return (self.sem, self.count)

    def now(self):
        return (self.sem, self.count) if self.count else None


class Transfers:

    def __init__(self, sem):
        self.sem, self.count = sem, 0

    def did(self, dma):
        self.count += 16
        dma.then_inc(self.sem, 16)
        return (self.sem, self.count)


class Bank:

    def __init__(self, ap):
        self.ap, self.read_by = ap, []


class WeightRing:

    def __init__(self, sync, slots, sems, plan):
        self.sync, self.slots = sync, slots
        self.loads = [Transfers(s) for s in sems]
        self.plan, self.issued, self.taken = plan, 0, 0
        self.arrived = {}
        for _ in range(min(len(slots), len(plan))):
            self.issue(None)

    def view(self, n):
        shape = self.plan[n][1]
        ap = self.slots[n % len(self.slots)][:, 0:shape[0] * shape[1]]
        return ap.rearrange("p (k n) -> p k n", k=shape[0])

    def issue(self, released_by):
        n = self.issued
        if n >= len(self.plan):
            return
        self.issued += 1
        self.sync.after(released_by)
        self.arrived[n] = self.loads[n % len(self.slots)].did(
            self.sync.eng.dma_start(self.view(n), self.plan[n][0]))

    def take(self, tag):
        n = self.taken
        self.taken += 1
        assert self.plan[n][2] == tag, (self.plan[n][2], tag)
        return self.view(n), self.arrived[n]

    def release(self, last_read):
        self.issue(last_read)


def alongside(main, n_main, filler, n_filler):
    done = 0
    for i, _ in enumerate(main):
        while done * n_main < (i + 1) * n_filler:
            if next(filler, None) is None:
                break
            done += 1
    for _ in filler:
        pass


def rows_plan(w, c0, n, tag):
    v = w.rearrange("(k p) n -> p k n", p=P)
    return [(v[:, 2 * i:2 * i + 2, c0:c0 + n], (2, n), tag) for i in range(v.shape[1] // 2)]


def wide_plan(w, tag):
    return [(w[k * P:(k + 1) * P, :].rearrange("p (k n) -> p k n", k=1), (1, D), tag) for k in range(w.shape[0] // P)]


def cols_plan(w, c0, tag, n=P):
    v = w.rearrange("(k p) n -> p k n", p=P)
    return [(v[:, :, c0:c0 + n], (KT, n), tag)]


def weight_plan(a):
    plan = []
    for n in range(6):
        plan += rows_plan(a["w_ada"][0], 512 * n, 512, "ada")
    for l in range(DEPTH):
        w = a["w_in"][l]
        for t in range(2):
            for c in (C_AQ, C_FF, C_FB):
                plan += cols_plan(w, c + P * t, "hg")
            if t == 0:
                plan += rows_plan(w, C_AI, 256, "ai")
                plan += rows_plan(w, C_B, 512, "b")
                plan += rows_plan(w, C_C, 512, "c")
            else:
                plan += rows_plan(w, C_CV, 256, "cv")
                plan += rows_plan(w, C_D, 512, "d")
        plan += rows_plan(w, C_G, 512, "g") + rows_plan(w, C_G + 512, 512, "g")
        if l < DEPTH - 1:
            for n in range(6):
                plan += rows_plan(a["w_ada"][l + 1], 512 * n, 512, "ada")
        for n in range(2):
            plan += rows_plan(a["w_out"][l], 512 * n, 512, "out")
    w = a["w_in_2"][0]
    for c in FM2[2:]:
        plan += cols_plan(w, c, "fm")
    plan += rows_plan(w, 0, 512, "gmlp") + rows_plan(w, 512, 256, "q") + rows_plan(w, 1024, 512, "kv")
    plan += rows_plan(w, 1536, P, "ng")
    for c in FM2[:2]:
        plan += cols_plan(w, c, "fm")
    for d in range(KT):
        for n in range(4):
            plan += cols_plan(a["w_gate_2"][0], n * D + d * P, "gate")
        plan += cols_plan(a["w_branch_2"][0].rearrange("n c d -> (n c) d"), d * P, "branch")
    plan += wide_plan(a["w_out_2"][0], "out2")
    for f in range(FT):
        plan += cols_plan(a["w_mlp1_2"][0], f * P, "mlp1")
    plan += wide_plan(a["w_mlp2_2"][0], "mlp2")
    return plan


FM2 = (768, 896, 1548, 1804, 1676, 1932, 2316, 2572, 2444, 2700, 2060, 2188)


def build(nc, a, out):
    ctx = ExitStack()
    with ctx:
        def sem(name):
            return ctx.enter_context(nc.semaphore(name))

        T = Engine(nc.tensor, sem("pe_steps"))
        S = Engine(nc.scalar, sem("act_steps"))
        V = Engine(nc.vector, sem("dve_steps"))
        G = Engine(nc.gpsimd, sem("pool_steps"))
        Y = Engine(nc.sync, sem("sp_steps"))
        pe, act, dve, pool = nc.tensor, nc.scalar, nc.vector, nc.gpsimd

        base = ctx.enter_context(nc.sbuf_tensor("arena", [P, ARENA], F32))
        arena_at = nc.sbuf_base - 4 * ARENA

        def part(start, n):
            return nc.alloc_sbuf_tensor_at(f"part_{start}_{n}", [P, n], F32R, offset=arena_at + 4 * start)[:]

        def parts(start, count, n):
            return [part(start + i * n, n) for i in range(count)]

        class Region:

            def __init__(self, start, size):
                self.start, self.size, self.at = start, size, 0

            def reset(self):
                self.at = 0

            def cut(self, *dims):
                n = int(np.prod(dims))
                assert self.at + n <= self.size, (self.at, n, self.size)
                ap = base[:, self.start + self.at:self.start + self.at + n]
                self.at += n
                if len(dims) == 2:
                    return ap.rearrange("p (a b) -> p a b", a=dims[0])
                if len(dims) == 3:
                    return ap.rearrange("p (a b c) -> p a b c", a=dims[0], b=dims[1])
                if len(dims) == 4:
                    return ap.rearrange("p (a b c d) -> p a b c d", a=dims[0], b=dims[1], c=dims[2])
                return ap

        at = 0
        regions = []
        for size in (6144, 17152, 4608, 6144, 7680, N_SLOTS * SLOT, 2760):
            regions.append(Region(at, size))
            at += size
        assert at == ARENA, at
        R_HT, R_WORK, R_V, R_G, R_QK, R_RING, R_TMP = regions

        def tile(name, shape, dt=F32):
            return ctx.enter_context(nc.sbuf_tensor(name, [P] + shape, dt))

        ident = tile("ident", [P])
        level_mask = tile("level_mask", [7, P], U8)
        cos64, sin64 = tile("cos64", [LT, HD]), tile("sin64", [LT, HD])
        cos32, sin32 = tile("cos32", [LT, DQ]), tile("sin32", [LT, DQ])
        low_mask, up_mask = tile("low_mask", [P]), tile("up_mask", [P])
        cols_a = tile("cols_a", [72])
        small = tile("small", [64])
        stats = tile("stats", [320])
        ada_t = tile("ada_t", [DEPTH, 24, 2])
        csil = tile("csil", [KT, 2])
        lb = tile("lb", [2, 2, 2])
        lb1m = tile("lb1m", [2, 2, 2])

        psum = ctx.enter_context(nc.psum_tensor("psum", [P, 8, 512], F32))
        psum_flat = psum[:].rearrange("p b n -> p (b n)")
        banks = [Bank(psum[:, b, :]) for b in range(8)]

        slots = [R_RING.cut(SLOT) for _ in range(N_SLOTS)]
        ring = WeightRing(Y, slots, [sem(f"weights_{i}") for i in range(N_SLOTS)], weight_plan(a))

        constants = Transfers(sem("constants"))
        parameters = Transfers(sem("parameters"))
        x_loads = [Transfers(sem(f"x_load_{i}")) for i in range(2)]
        x_stores = Transfers(sem("x_stores"))
        out_stores = Transfers(sem("out_stores"))

        def load(dst, src, group, by=G):
            return group.did(by.eng.dma_start(dst, src))

        stage = R_TMP.cut(P)
        levels_wide = base[:, R_QK.start:R_QK.start + 7 * P].rearrange("p (l n) -> p l n", l=7)
        for dst, src in ((ident[:], a["c_ident"]), (levels_wide, a["c_levels"]),
                         (cos64[:], a["c_cos64"]), (sin64[:], a["c_sin64"]),
                         (cos32[:], a["c_cos32"]), (sin32[:], a["c_sin32"]),
                         (low_mask[:], a["c_low"]), (up_mask[:], a["c_up"])):
            load(dst, src, constants)
        load(stage[0:8, :], a["c"].rearrange("b (k p) -> (b k) p", p=P), constants)
        load(stage[8:16, :], a["c_ctx"].rearrange("(k p) -> k p", p=P), constants)
        load(stage[16:24, :], a["hg_lb_logits"].rearrange("l d (t p) -> (l d t) p", p=P), constants)
        ready = load(stage[24:72, :], a["b_ada"].rearrange("l (j p) -> (l j) p", p=P), constants)

        def bc(ap, axis, shape):
            return ap.unsqueeze(axis).to_broadcast(shape)

        def everyone():
            return [e.now() for e in (T, S, V, G)]

        class Later:

            def __init__(self):
                self.tiles, self.steps = 0, []

            def add(self, tiles, step):
                self.steps.append((self.tiles + tiles, step))

            def next_tile(self):
                self.tiles += 1
                self.run(self.tiles)

            def run(self, due):
                while self.steps:
                    first = min(self.steps, key=lambda s: s[0])
                    if due is not None and first[0] > due:
                        break
                    self.steps.remove(first)
                    first[1]()

        later = Later()

        def fence():
            later.run(None)
            all_now = everyone()
            for e in (T, S, V, G):
                e.after(*all_now)

        def rstd(v, scale, eps, r, tmp, token):
            V.after(token)
            V.after(V.did(dve.tensor_scalar(v, v, scale, eps, ALU.mult, ALU.add)))
            rb = r.bitcast(I32)
            V.after(V.did(dve.tensor_scalar(rb, v.bitcast(I32), 1, None, ALU.logical_shift_right)))
            V.after(V.did(dve.tensor_scalar(rb, rb, -1.0, RSQRT_GUESS, ALU.mult, ALU.add)))
            for _ in range(3):
                V.after(V.did(dve.tensor_tensor(tmp, r, r, ALU.mult)))
                V.after(V.did(dve.scalar_tensor_tensor(tmp, tmp, -0.5, v, ALU.mult, ALU.mult)))
                t = V.did(dve.scalar_tensor_tensor(r, tmp, 1.5, r, ALU.add, ALU.mult))
                V.after(t)
            return t

        V.after(ready)
        V.did(dve.tensor_copy(level_mask[:], levels_wide))

        T.after(ready)
        t = T.did(pe.transpose(banks[0].ap[:, 0:72], stage[0:72, :], ident[0:72, 0:72]))
        S.after(t)
        t = S.did(act.activation(cols_a[:], banks[0].ap[:, 0:72], ACT.Copy))
        banks[0].read_by = [t]
        S.after(t)
        csil_ready = S.did(act.activation(csil[:], cols_a[:, 0:16].rearrange("p (v k) -> p k v", v=2), ACT.Silu))
        lg = cols_a[:, 16:24].rearrange("p (l n) -> p l n", l=2)
        sm = small[:, 0:16].rearrange("p (l n) -> p l n", l=4)
        V.after(t)
        t = V.did(dve.tensor_tensor(sm[:, 0, :], lg[:, 0, :], lg[:, 1, :], ALU.max))
        V.after(t)
        V.did(dve.tensor_tensor(sm[:, 1, :], lg[:, 0, :], sm[:, 0, :], ALU.subtract))
        t = V.did(dve.tensor_tensor(sm[:, 2, :], lg[:, 1, :], sm[:, 0, :], ALU.subtract))
        S.after(t)
        t = S.did(act.activation(sm[:, 1:3, :], sm[:, 1:3, :], ACT.Exp))
        V.after(t)
        t = V.did(dve.tensor_tensor(sm[:, 3, :], sm[:, 1, :], sm[:, 2, :], ALU.add))
        V.after(t)
        t = V.did(dve.reciprocal(sm[:, 3, :], sm[:, 3, :]))
        V.after(t)
        V.did(dve.memset(lb[:, 0], 0.0))
        t = V.did(dve.tensor_tensor(lb[:, 1].rearrange("p d t -> p (d t)"), sm[:, 2, :], sm[:, 3, :], ALU.mult))
        V.after(t)
        lb_ready = V.did(dve.tensor_scalar(lb1m[:], lb[:], -1.0, 1.0, ALU.mult, ALU.add))

        def product_rows(tag, tiles, lhs, lhs_ready, n, use, evacuate, cols=lambda m: None, kt=KT):
            got = [ring.take(tag) for _ in range(kt // 2)]
            for j, m in enumerate(tiles):
                b = banks[use[j % len(use)]]
                c0, c1 = cols(m) or (0, n)
                T.after(lhs_ready(m) if callable(lhs_ready) else lhs_ready, b.read_by)
                for k in range(kt):
                    view, arrived = got[k // 2]
                    T.after(arrived)
                    mm = pe.matmul(b.ap[:, c0:c1], lhs(k, m), view[:, k % 2, c0:c1], start=k == 0, stop=k == kt - 1)
                    if j == len(tiles) - 1 and k % 2 == 1 and k < kt - 1:
                        ring.release(T.did(mm))
                done = T.did(mm)
                if j == len(tiles) - 1:
                    ring.release(done)
                later.next_tile()
                b.read_by = evacuate(m, b.ap, done)
                yield True

        def product_cols(tag, rhs, rhs_ready, spans, use, evacuate):
            view, arrived = ring.take(tag)
            T.after(rhs_ready, arrived)
            for j, (t0, t1) in enumerate(spans):
                b = banks[use[j % len(use)]]
                T.after(b.read_by)
                for k in range(KT):
                    mm = pe.matmul(b.ap[:, 0:t1 - t0], view[:, k, :], rhs(k, t0, t1), start=k == 0, stop=k == KT - 1)
                done = T.did(mm)
                if j == len(spans) - 1:
                    ring.release(done)
                later.next_tile()
                b.read_by = evacuate(t0, t1, b.ap[:, 0:t1 - t0], done)

        def split(src, hi, lo, ready, free=None):
            S.after(ready, free)
            t = S.did(act.activation(hi, src, ACT.Copy))
            V.after(t, free)
            return V.did(dve.tensor_tensor(lo, src, hi.bitcast(F32), ALU.subtract))

        class SplitWeights:

            def __init__(self, plan, pairs):
                self.plan, self.pairs, self.n = plan, pairs, 0
                self.free = [None] * len(pairs)
                self.got = []
                self.fetch()

            def fetch(self):
                if self.n == len(self.plan):
                    return
                tag, k = self.plan[self.n]
                i = self.n % len(self.pairs)
                self.n += 1
                view, arrived = ring.take(tag)
                hi, lo = (ap.rearrange("p (k n) -> p k n", k=k) for ap in self.pairs[i])
                t = split(view, hi, lo, arrived, self.free[i])
                ring.release(t)
                self.got.append((i, hi, lo, t))

            def take(self):
                self.fetch()
                return self.got.pop(0)

        def product_3(out, w_hi, w_lo, x_hi, x_lo, first, last):
            pe.matmul(out, w_lo, x_hi, start=first, stop=False)
            pe.matmul(out, w_hi, x_lo, start=False, stop=False)
            return pe.matmul(out, w_hi, x_hi, start=False, stop=last)

        def transposed(src, n_blocks, bank, token, width=P):
            T.after(token, bank.read_by)
            for i in range(n_blocks):
                mm = pe.transpose(bank.ap[0:width, i * P:(i + 1) * P], src[:, i * width:(i + 1) * width], ident[:])
            return T.did(mm)

        def attend(items, prob, prob_t, free, chores=(), skew=2):
            pairs = [(banks[2], banks[3]), (banks[4], banks[5])]
            state = {}
            n_pair = [0]

            def score(i):
                it = items[i]
                st = state[i] = {"sum": [], "p": []}
                for q, segments in it["maps"]:
                    n = n_pair[0]
                    n_pair[0] += 1
                    pr = pairs[n % 2]
                    s_ap = psum_flat[:, 1024 * (1 + n % 2):1024 * (2 + n % 2)]
                    T.after(it["q_ready"](), pr[0].read_by, pr[1].read_by, it["k_ready"])
                    for rhs, c0 in segments:
                        w = rhs.shape[-1]
                        mm = pe.matmul(s_ap[:, c0:c0 + w], q, rhs, start=True, stop=True)
                    t = T.did(mm)
                    V.after(t)
                    for c0, mask in it.get("masks", ()):
                        w = mask.shape[-1]
                        V.after(V.did(dve.tensor_tensor(s_ap[:, c0:c0 + w], s_ap[:, c0:c0 + w], mask, ALU.add)))
                    col = stats[:, 8 * (i % 40):8 * (i % 40) + 8]
                    j = len(st["sum"])
                    lo, hi = it["range"]
                    t = V.did(dve.reduce_max(col[:, j:j + 1], s_ap[:, lo:hi], AX, negate=True))
                    V.after(t)
                    if it.get("sink"):
                        neg_sink, sink = it["sink"]
                        t = V.did(dve.tensor_scalar(col[:, j:j + 1], col[:, j:j + 1], it["scale"], neg_sink, ALU.mult, ALU.min))
                    elif it["scale"] != 1.0:
                        t = V.did(dve.tensor_scalar(col[:, j:j + 1], col[:, j:j + 1], it["scale"], None, ALU.mult))
                    p = prob[n % len(prob)]
                    S.after(t, free["p"][n % len(prob)])
                    t = S.did(act.activation(p[:, lo:hi], s_ap[:, lo:hi], ACT.Exp, bias=col[:, j:j + 1],
                                             scale=it["scale"], accum_out=col[:, 2 + j:3 + j]))
                    pr[0].read_by = pr[1].read_by = [t]
                    if it.get("sink"):
                        t = S.did(act.activation(col[:, 6:7], sink, ACT.Exp, bias=col[:, 0:1]))
                    st["sum"].append(col[:, 2 + j:3 + j])
                    st["p"].append((p, n % len(prob), t))

            def settle(i):
                it, st = items[i], state[i]
                col = stats[:, 8 * (i % 40):8 * (i % 40) + 8]
                V.after(st["p"][-1][2])
                if it.get("sink"):
                    V.after(V.did(dve.tensor_tensor(col[:, 2:3], col[:, 2:3], col[:, 6:7], ALU.add)))
                t = V.did(dve.reciprocal(it["rec"], st["sum"][0]))
                p = st["p"][0][0]
                if "neg_lam" in it:
                    lo, hi = it["range"]
                    V.did(dve.reciprocal(col[:, 4:5], st["sum"][1]))
                    t = V.now()
                    V.after(t)
                    t = V.did(dve.scalar_tensor_tensor(col[:, 5:6], st["sum"][0], it["neg_lam"], col[:, 4:5], ALU.mult, ALU.mult))
                    V.after(t)
                    p2 = st["p"][1][0]
                    t = V.did(dve.scalar_tensor_tensor(p[:, lo:hi], p2[:, lo:hi], col[:, 5:6], p[:, lo:hi], ALU.mult, ALU.add))
                    free["p"][st["p"][1][1]] = [t]
                if it.get("valid") is not None:
                    lo, hi = it["range"]
                    t = V.did(dve.tensor_tensor(p[:, lo:hi], p[:, lo:hi], it["valid"], ALU.mult))
                st["ready"] = t

            def turn(i):
                it, st = items[i], state[i]
                p, n_p, _ = st["p"][0]
                n = i % 2
                st["pt"] = []
                blocks = it["blocks"]
                for half in range(0, len(blocks), 3):
                    bank = banks[6 + (half // 3)]
                    part = blocks[half:half + 3]
                    T.after(st["ready"], [x[2] for x in st["p"]], bank.read_by)
                    for j, (c0, w, _) in enumerate(part):
                        mm = pe.transpose(bank.ap[0:w, j * P:(j + 1) * P], p[:, c0:c0 + w], ident[:])
                    t = T.did(mm)
                    w = part[0][1]
                    e = S if "neg_lam" in it else (S, V)[(half // 3 + i) % 2]
                    e.after(t, free["pt"][n])
                    dst = prob_t[n][0:w, half * P:(half + len(part)) * P]
                    src = bank.ap[0:w, 0:len(part) * P]
                    if e is S:
                        t = S.did(act.activation(dst, src, ACT.Copy))
                    else:
                        t = V.did(dve.tensor_copy(dst, src))
                    bank.read_by = [t]
                    st["pt"].append(t)
                free["p"][n_p] = [T.now()]

            def value(i):
                it, st = items[i], state[i]
                n = i % 2
                T.after(st["pt"], it["v_ready"])
                if it["first"]:
                    T.after(it["bank"].read_by)
                blocks = it["blocks"]
                for j, (_, w, v) in enumerate(blocks):
                    mm = pe.matmul(it["bank"].ap[:, it["col"]:it["col"] + P], prob_t[n][0:w, j * P:(j + 1) * P], v,
                                   start=j == 0, stop=j == len(blocks) - 1)
                t = T.did(mm)
                free["pt"][n] = [t]
                if it.get("finish"):
                    it["bank"].read_by = it["finish"](t)
                del state[i]

            if items[0].get("prepare"):
                items[0]["prepare"]()
            for i in range(len(items) + skew + 1):
                if i + 2 < len(items) and items[i + 2].get("prepare"):
                    items[i + 2]["prepare"]()
                if i < len(items):
                    score(i)
                if 1 <= i <= len(items):
                    settle(i - 1)
                if 0 <= i - skew < len(items):
                    turn(i - skew)
                if i > skew:
                    value(i - skew - 1)
                if chores:
                    chores.pop(0)()
                yield True
            while chores:
                chores.pop(0)()

        h_t = R_HT.cut(KT, TOK)
        gated = R_G.cut(TT, D)
        q_b, q_c, q_d = R_QK.cut(TT, 256), R_QK.cut(TT, 256), R_QK.cut(TT, 256)
        k_b, k_c, k_d = R_QK.cut(1, TOK), R_QK.cut(2, TOK), R_QK.cut(1, TOK)
        v_a, v_b, v_c, v_d = R_V.cut(TT, 256), R_V.cut(TT, P), R_V.cut(TT, 256), R_V.cut(TT, P)
        R_TMP.reset()
        raw = [R_TMP.cut(512), R_TMP.cut(512)]
        t_cos, t_sin = R_TMP.cut(512), R_TMP.cut(512)
        gain_b = R_TMP.cut(384)
        t_small = R_TMP.cut(3, 24)
        raw_free = [[], []]
        free_cell = {"n": 0}

        x_scratch = a["x_scratch"].rearrange("(m p) d -> m p d", p=P)
        x_in = a["x"][0].rearrange("(m p) d -> m p d", p=P)
        ctx_in = a["ctx"][0].rearrange("(m p) d -> m p d", p=P)

        ada_ready = {}

        def ada(l):
            for n in range(6):
                got = [ring.take("ada") for _ in range(KT // 2)]
                b = banks[0]
                T.after(csil_ready, b.read_by)
                for k in range(KT):
                    T.after(got[k // 2][1])
                    mm = pe.matmul(b.ap[0:2, :], csil[:, k, :], got[k // 2][0][:, k % 2, :], start=k == 0, stop=k == KT - 1)
                    if k % 2:
                        t = T.did(mm)
                        ring.release(t)
                row = raw[n % 2]
                S.after(t, raw_free[n % 2])
                t = S.did(act.activation(row[0:2, :], b.ap[0:2, :], ACT.Copy))
                b.read_by = [t]
                b2 = banks[6 + n % 2]
                T.after(t, b2.read_by)
                for j in range(4):
                    mm = pe.transpose(b2.ap[:, 2 * j:2 * j + 2], row[0:2, j * P:(j + 1) * P], ident[0:2, 0:2])
                t = T.did(mm)
                raw_free[n % 2] = [t]
                V.after(t)
                bias = cols_a[:, 24 + 24 * l + 4 * n:24 + 24 * l + 4 * n + 4]
                t_add = V.did(dve.tensor_tensor(ada_t[:, l, 4 * n:4 * n + 4, :], b2.ap[:, 0:8].rearrange("p (j v) -> p j v", v=2),
                                                bc(bias, 2, [P, 4, 2]), ALU.add))
                b2.read_by = [t_add]
                yield True
            V.after(t_add)
            ada_ready[l] = V.did(dve.tensor_scalar(ada_t[:, l, 8:16, :], ada_t[:, l, 8:16, :], 1.0, None, ALU.add))

        def modulate(l, m, x_tile, x_ready, columns_free):
            last = []
            v = 0 if m < LT else 1
            for half in range(2):
                b = banks[4 + (2 * m + half) % 4]
                t = transposed(x_tile[:, half * 512:half * 512 + 512], 4, b, x_ready)
                e = (S, V)[half]
                e.after(t, ada_ready[l], columns_free)
                for j in range(4):
                    k = 4 * half + j
                    dst, ps = h_t[:, k, m * P:(m + 1) * P], b.ap[:, j * P:(j + 1) * P]
                    if e is S:
                        t = S.did(act.activation(dst, ps, ACT.Identity, bias=ada_t[:, l, k, v:v + 1], scale=ada_t[:, l, 8 + k, v:v + 1]))
                    else:
                        t = V.did(dve.tensor_scalar(dst, ps, ada_t[:, l, 8 + k, v:v + 1], ada_t[:, l, k, v:v + 1], ALU.mult, ALU.add))
                b.read_by = [t]
                last.append(t)
            return last

        def heads_rows(m, ps, ready, n_q, n_k, d, gain, q_dst, k_dst, v_dst):
            i = free_cell["n"] % 2
            free_cell["n"] += 1
            r = raw[i]
            nq, nk = n_q * d, n_k * d
            n = nq + nk
            c0 = 0 if q_dst is not None else nq
            S.after(ready, raw_free[i])
            t = S.did(act.activation(r[:, c0:n], ps[:, c0:n], ACT.Copy))
            if v_dst is not None:
                t = S.did(act.activation(v_dst, ps[:, n:512], ACT.Copy))
            read = [t]
            if gain is not None:
                h0 = c0 // d
                nh = n_q + n_k
                sq = t_sin
                V.after(t, V.now())
                t = V.did(dve.tensor_tensor(sq[:, c0:n], r[:, c0:n], r[:, c0:n], ALU.mult))
                V.after(t)
                ss = t_small[:, 0, h0:nh]
                t = V.did(dve.reduce_sum(ss, sq[:, c0:n].rearrange("p (h d) -> p h d", d=d), AX))
                t = rstd(ss, 1.0 / d, RMS_EPS, t_small[:, 1, h0:nh], t_small[:, 2, h0:nh], t)
                V.after(t)
                rr = r[:, c0:n].rearrange("p (h d) -> p h d", d=d)
                t = V.did(dve.tensor_tensor(rr, rr, bc(t_small[:, 1, h0:nh], 2, [P, nh - h0, d]), ALU.mult))
                V.after(t, gain_ready[0])
                t = V.did(dve.tensor_tensor(r[:, c0:n], r[:, c0:n], gain_b[:, c0:n], ALU.mult))
            if m < LT:
                cos, sin = (cos64, sin64) if d == HD else (cos32, sin32)
                nh = n // d
                V.after(t, V.now())
                V.did(dve.tensor_tensor(t_cos[:, 0:n].rearrange("p (h d) -> p h d", d=d),
                                        r[:, 0:n].rearrange("p (h d) -> p h d", d=d),
                                        bc(cos[:, m, :], 1, [P, nh, d]), ALU.mult))
                x4 = d // 4
                split = lambda ap: ap.rearrange("p (h e s x) -> p h e s x", e=2, s=2, x=x4)
                tab = sin[:, m, :].rearrange("p (e s x) -> p e s x", e=2, s=2)
                for s in range(2):
                    t = V.did(dve.tensor_tensor(split(t_sin[:, 0:n])[:, :, :, s, :], split(r[:, 0:n])[:, :, :, 1 - s, :],
                                                bc(tab[:, :, s, :], 1, [P, nh, 2, x4]), ALU.mult))
                V.after(t)
                V.did(dve.tensor_tensor(q_dst, t_cos[:, 0:nq], t_sin[:, 0:nq], ALU.add))
                t = V.did(dve.tensor_tensor(r[:, nq:n], t_cos[:, nq:n], t_sin[:, nq:n], ALU.add))
                raw_free[i] = []
            else:
                if q_dst is not None:
                    G.after(t)
                    raw_free[i] = [G.did(pool.tensor_copy(q_dst, r[:, 0:nq]))]
                else:
                    raw_free[i] = []

            def turn_keys():
                b = banks[2 + i]
                x = transposed(r[:, nq:n], nk // P, b, t)
                raw_free[i].append(x)
                S.after(x)
                b.read_by = [S.did(act.activation(k_dst[:, :, m * P:(m + 1) * P],
                                                  b.ap[:, 0:nk].rearrange("p (b n) -> p b n", n=P), ACT.Copy))]

            later.add(2, turn_keys)
            return read

        gain_ready = [None]

        def split_halves(ap, h):
            return ap.rearrange("p (n s h) -> p n s h", s=2, h=h)

        def hgrn_inputs(l, t, ctx_out, work):
            rhs = lambda k, t0, t1: h_t[:, k, t0:t1]
            f, r, e, att, att_c, q, k_f, k_b, o = work
            done = []

            def evac_q(t0, t1, ps, ready):
                S.after(ready)
                x = S.did(act.activation(q[:, t0:t1], ps, ACT.Sigmoid))
                V.after(x)
                x = V.did(dve.tensor_tensor(q[:, t0:t1], q[:, t0:t1], ps, ALU.mult))
                done.append(x)
                return [x]

            product_cols("hg", rhs, h_ready[0], [(0, SEQ)] + ([(SEQ, TOK)] if ctx_out else []), (0, 1), evac_q)
            for d, k in ((0, k_f), (1, k_b)):
                def evac_f(t0, t1, ps, ready):
                    S.after(ready)
                    x = S.did(act.activation(f[:, d, t0:t1], ps, ACT.Sigmoid))
                    V.after(x, lb_ready)
                    y = V.did(dve.tensor_scalar(f[:, d, t0:t1], f[:, d, t0:t1], lb1m[:, l, d, t:t + 1], lb[:, l, d, t:t + 1], ALU.mult, ALU.add))
                    V.after(y)
                    V.did(dve.tensor_scalar(k[:, t0:t1], f[:, d, t0:t1], -1.0, 1.0, ALU.mult, ALU.add))
                    done.append(V.did(dve.tensor_scalar(f[:, d, t0:t1], f[:, d, t0:t1], LOG_FLOOR, None, ALU.max)))
                    return [x]

                product_cols("hg", rhs, h_ready[0], [(0, SEQ), (SEQ, TOK)], (0, 1), evac_f)
            S.after(done)
            done.append(S.did(act.activation(f[:], f[:], ACT.Ln)))
            return done

        def hgrn(l, t, ctx_out, work, inputs_ready):
            f, r, e, att, att_c, q, k_f, k_b, o = work
            nq = TOK if ctx_out else SEQ
            att_flat = [att[:, hh].rearrange("p i t -> p (i t)") for hh in range(2)]
            e_free = [[], []]
            G.after(inputs_ready)
            V.after(inputs_ready)
            S.after(inputs_ready)
            T.after(inputs_ready)
            t_r = G.did(pool.memset(r[:], 0.0))
            t_k = V.did(dve.tensor_tensor(e[1][:, 1, 0:nq], k_f[:, 0:nq], k_b[:, 0:nq], ALU.add))

            def next_bank():
                bank_turn[0] += 1
                return banks[2 + bank_turn[0] % 6]

            def products(keys, queries, ready):
                T.after(ready)
                got = []
                for g in range(4 if ctx_out else 2):
                    b = next_bank()
                    T.after(b.read_by)
                    hh = g % 2
                    for j in range(LT if g < 2 else CT):
                        c = j if g < 2 else LT + j
                        rows = slice(64 * hh, 64 * hh + 64)
                        mm = pe.matmul(b.ap[:, j * P:(j + 1) * P], keys[rows, c * P:(c + 1) * P],
                                       queries[rows, c * P:(c + 1) * P], start=True, stop=True)
                    got.append((b, T.did(mm)))
                return got

            def places(g):
                if g < 2:
                    x = SEQ + P
                    return [(att_flat[g][:, 0:LT * x].rearrange("p (j x) -> p j x", x=x)[:, :, 0:P], slice(0, 512))]
                return [(att_c[:, g - 2, c, c * P:(c + 1) * P].unsqueeze(1), slice(c * P, (c + 1) * P)) for c in range(CT)]

            got = products(e[1][:, 1], q, t_k)
            base = []
            for g, (b, ready) in enumerate(got):
                S.after(ready)
                for dst, src in places(g):
                    x = S.did(act.activation(dst, b.ap[:, src].rearrange("p (j n) -> p j n", n=P), ACT.Copy))
                b.read_by = [x]
                base.append(x)
            e_free[1] = [T.now()]
            last_update = [t_r]
            yield True

            def decays(level):
                h = 1 << level
                n = TOK if level < 8 else SEQ
                E = e[level % 2]
                sf, sb = split_halves(f[:, 0, 0:n], h), split_halves(f[:, 1, 0:n], h)
                rf, rb = split_halves(r[:, 0, 0:n], h), split_halves(r[:, 1, 0:n], h)
                eq, ek = split_halves(E[:, 0, 0:n], h), split_halves(E[:, 1, 0:n], h)
                S.after(last_update[0], e_free[level % 2])
                S.did(act.activation(eq[:, :, 0], sb[:, :, 0], ACT.Exp))
                S.did(act.activation(eq[:, :, 1], sf[:, :, 1], ACT.Exp))
                S.did(act.activation(ek[:, :, 0], rf[:, :, 0], ACT.Exp))
                t_e = S.did(act.activation(ek[:, :, 1], rb[:, :, 1], ACT.Exp))
                V.after(t_e)
                w = n // (2 * h)
                V.did(dve.tensor_tensor(rf[:, :, 0], rf[:, :, 0], sf[:, :, 1, h - 1:h].to_broadcast([P, w, h]), ALU.add))
                V.after(V.did(dve.tensor_tensor(rb[:, :, 1], rb[:, :, 1], sb[:, :, 0, 0:1].to_broadcast([P, w, h]), ALU.add)))
                V.did(dve.tensor_tensor(sf[:, :, 1], sf[:, :, 1], sf[:, :, 0, h - 1:h].to_broadcast([P, w, h]), ALU.add))
                last_update[0] = V.did(dve.tensor_tensor(sb[:, :, 0], sb[:, :, 0], sb[:, :, 1, 0:1].to_broadcast([P, w, h]), ALU.add))
                m = min(n, nq)
                V.did(dve.tensor_tensor(E[:, 0, 0:m], E[:, 0, 0:m], q[:, 0:m], ALU.mult))
                V.did(dve.tensor_tensor(ek[:, :, 0], ek[:, :, 0], split_halves(k_f[:, 0:n], h)[:, :, 0], ALU.mult))
                return V.did(dve.tensor_tensor(ek[:, :, 1], ek[:, :, 1], split_halves(k_b[:, 0:n], h)[:, :, 1], ALU.mult))

            def level_products(level, t_m):
                E, h = e[level % 2], 1 << level
                if h < P:
                    got = products(E[:, 1], E[:, 0], t_m)
                    for g, (b, ready) in enumerate(got):
                        V.after(ready, base)
                        for dst, src in places(g):
                            nb = (src.stop - src.start) // P
                            x = V.did(dve.copy_predicated(dst, bc(level_mask[:, level, :], 1, [P, nb, P]),
                                                          b.ap[:, src].rearrange("p (j n) -> p j n", n=P)))
                        b.read_by = [x]
                elif h == P:
                    T.after(t_m)
                    for g in range(4 if ctx_out else 2):
                        b = next_bank()
                        T.after(b.read_by)
                        blocks = [(g % 2, s, q_) for s, q_ in (((0, 1), (2, 3), (1, 0), (3, 2)) if g < 2 else ((4, 5), (5, 4)))]
                        for j, (hh, s, q_) in enumerate(blocks):
                            rows = slice(64 * hh, 64 * hh + 64)
                            mm = pe.matmul(b.ap[:, j * P:(j + 1) * P], E[rows, 1, s * P:(s + 1) * P],
                                           E[rows, 0, q_ * P:(q_ + 1) * P], start=True, stop=True)
                        ready = T.did(mm)
                        S.after(ready)
                        if g < 2:
                            x = 2 * SEQ + 2 * P
                            for i, at0 in enumerate((P, SEQ)):
                                dst = att_flat[g][:, at0:at0 + 2 * x].rearrange("p (j x) -> p j x", x=x)[:, :, 0:P]
                                y = S.did(act.activation(dst, b.ap[:, i * 256:i * 256 + 256].rearrange("p (j n) -> p j n", n=P), ACT.Copy))
                        else:
                            for j, (hh, s, q_) in enumerate(blocks):
                                y = S.did(act.activation(att_c[:, hh, s - LT, (q_ - LT) * P:(q_ - LT + 1) * P],
                                                         b.ap[:, j * P:(j + 1) * P], ACT.Copy))
                        b.read_by = [y]
                else:
                    T.after(t_m)
                    for hh in range(2):
                        rows = slice(64 * hh, 64 * hh + 64)
                        for s0 in (0, 2):
                            q0 = SEQ // 2 - s0 * P
                            b = banks[2 + (2 * hh + s0 // 2)]
                            T.after(b.read_by)
                            for j in range(2):
                                mm = pe.matmul(b.ap[:, j * 256:(j + 1) * 256], E[rows, 1, (s0 + j) * P:(s0 + j + 1) * P],
                                               E[rows, 0, q0:q0 + 256], start=True, stop=True)
                            ready = T.did(mm)
                            S.after(ready)
                            b.read_by = [S.did(act.activation(att[:, hh, s0:s0 + 2, q0:q0 + 256],
                                                              b.ap[:, 0:512].rearrange("p (j n) -> p j n", n=256), ACT.Copy))]
                e_free[level % 2] = [T.now()]

            t_m = decays(0)
            yield True
            for level in range(9):
                t_next = decays(level + 1) if level < 8 else None
                level_products(level, t_m)
                t_m = t_next
                yield True
            t_upd = last_update[0]
            S.after(t_upd, e_free[0], e_free[1])
            for d in range(2):
                S.did(act.activation(e[d][:, 0, 0:SEQ], f[:, d, 0:SEQ], ACT.Exp))
                t_e = S.did(act.activation(e[d][:, 1, SEQ:TOK], r[:, d, SEQ:TOK], ACT.Exp))
            V.after(t_e)
            for d, k in ((0, k_f), (1, k_b)):
                V.did(dve.tensor_tensor(e[d][:, 0, 0:SEQ], e[d][:, 0, 0:SEQ], q[:, 0:SEQ], ALU.mult))
                t_m = V.did(dve.tensor_tensor(e[d][:, 1, SEQ:TOK], e[d][:, 1, SEQ:TOK], k[:, SEQ:TOK], ALU.mult))
            T.after(t_m)
            for hh in range(2):
                rows = slice(64 * hh, 64 * hh + 64)
                for c in range(CT):
                    b = banks[2 + (2 * hh + c)]
                    T.after(b.read_by)
                    for d in range(2):
                        mm = pe.matmul(b.ap[:, 0:SEQ], e[d][rows, 1, SEQ + c * P:SEQ + (c + 1) * P], e[d][rows, 0, 0:SEQ],
                                       start=d == 0, stop=d == 1)
                    x = T.did(mm)
                    S.after(x)
                    b.read_by = [S.did(act.activation(att[:, hh, LT + c, :], b.ap[:, 0:SEQ], ACT.Copy))]
            yield True
            att_done = [S.now(), V.now()]
            for j in range(TT if ctx_out else LT):
                b = banks[2 + j % 6]
                T.after(b.read_by, att_done, v_a_ready[0])
                for hh in range(2):
                    if j < LT:
                        terms = [(att[:, hh, i, j * P:(j + 1) * P], i) for i in range(TT)]
                    else:
                        terms = [(att_c[:, hh, c, (j - LT) * P:(j - LT + 1) * P], LT + c) for c in range(CT)]
                    for i, (w_ap, s) in enumerate(terms):
                        mm = pe.matmul(b.ap[:, hh * P:(hh + 1) * P], w_ap, v_a[:, s, t * P:(t + 1) * P],
                                       start=i == 0, stop=i == len(terms) - 1)
                x = T.did(mm)
                S.after(x)
                y = S.did(act.activation(o[:, j, t * P:(t + 1) * P].rearrange("p (h d) -> p h d", d=HD),
                                         b.ap[:, 0:384].rearrange("p (h x) -> p h x", x=192)[:, :, 0:HD], ACT.Copy))
                b.read_by = [y]
            yield True

        bank_turn = [0]
        v_a_ready = [None]
        h_ready = [None]

        def hgrn_buffers():
            R_WORK.reset()
            f, r = R_WORK.cut(2, TOK), R_WORK.cut(2, TOK)
            e = [R_WORK.cut(2, TOK), R_WORK.cut(2, TOK)]
            att, att_c = R_WORK.cut(2, TT, SEQ), R_WORK.cut(2, CT, CTX)
            q, k_f, k_b, o = R_WORK.cut(TOK), R_WORK.cut(TOK), R_WORK.cut(TOK), R_WORK.cut(TT, 256)
            return f, r, e, att, att_c, q, k_f, k_b, o

        gain_hg, gain_df = tile("gain_hg", [HD]), tile("gain_df", [HD])
        sinks, neg_sinks = tile("sinks", [NH]), tile("neg_sinks", [NH])
        lam_rows, lam = tile("lam_rows", [4, DQ]), tile("lam", [8])

        def spread(ap, n):
            return ap.unsqueeze(0).to_broadcast([P, n])

        def layer(l, after_tile, before_out=None):
            ctx_out = l < DEPTH - 1
            last_q = TT if ctx_out else LT
            lam_init = 0.8 - 0.6 * math.exp(-0.3 * l)
            G.after(*everyone())
            for h in range(NH + NKV):
                load(gain_b[:, h * HD:(h + 1) * HD], spread(a["ga_q_norm_g" if h < NH else "ga_k_norm_g"][l], HD), parameters)
            load(gain_hg[:], spread(a["hg_norm_g"][l], HD), parameters)
            load(gain_df[:], spread(a["df_subln_g"][l], HD), parameters)
            load(sinks[:], spread(a["wn_sink"][l], NH), parameters)
            params = load(lam_rows[:].rearrange("p a b -> p (a b)"), spread(a["df_lambda"][l].rearrange("a b -> (a b)"), 4 * DQ), parameters)
            gain_ready[0] = params
            V.after(params)
            V.did(dve.tensor_scalar(neg_sinks[:], sinks[:], -1.0, None, ALU.mult))
            t = V.did(dve.tensor_tensor(lam_rows[:, 0::2, :], lam_rows[:, 0::2, :], lam_rows[:, 1::2, :], ALU.mult))
            V.after(t)
            t = V.did(dve.reduce_sum(lam[:, 0:2], lam_rows[:, 0::2, :], AX))
            S.after(t)
            t = S.did(act.activation(lam[:, 2:4], lam[:, 0:2], ACT.Exp))
            V.after(t)
            t = V.did(dve.tensor_tensor(lam[:, 4:5], lam[:, 3:4], lam[:, 2:3], ALU.subtract))
            V.after(t)
            t_lam = V.did(dve.tensor_scalar(lam[:, 5:6], lam[:, 4:5], -lam_init, None, ALU.add))

            lhs = lambda k, m: h_t[:, k, m * P:(m + 1) * P]
            every = list(range(TT))
            work = hgrn_buffers()
            done_v = {}

            def copy_to(dst, key):
                def evacuate(m, ps, ready):
                    S.after(ready)
                    t = S.did(act.activation(dst(m), ps[:, 0:dst(m).shape[-1]], ACT.Copy))
                    done_v[key] = t
                    return [t]
                return evacuate

            def proj_first():
                yield from product_rows("ai", every, lhs, h_ready[0], 256, (0, 1), copy_to(lambda m: v_a[:, m, :], "a"))
                v_a_ready[0] = done_v["a"]
                skip = lambda lo: (lambda m: (lo, 512) if m >= last_q else None)
                yield from product_rows("b", every, lhs, h_ready[0], 512, (0, 1), lambda m, ps, t: heads_rows(
                    m, ps, t, NH, NKV, HD, gain_b, q_b[:, m, :] if m < last_q else None, k_b, v_b[:, m, :]), cols=skip(256))
                yield from product_rows("c", every, lhs, h_ready[0], 512, (0, 1), lambda m, ps, t: heads_rows(
                    m, ps, t, 8, 8, DQ, None, q_c[:, m, :] if m < last_q else None, k_c, None), cols=skip(256))

            def proj_second():
                skip = lambda lo: (lambda m: (lo, 512) if m >= last_q else None)
                yield from product_rows("cv", every, lhs, h_ready[0], 256, (0, 1), copy_to(lambda m: v_c[:, m, :], "c"))
                yield from product_rows("d", every, lhs, h_ready[0], 512, (0, 1), lambda m, ps, t: heads_rows(
                    m, ps, t, NH, NKV, HD, None, q_d[:, m, :] if m < last_q else None, k_d, v_d[:, m, :]), cols=skip(256))

            def gate_and_ada():
                for c0 in (0, 512):
                    yield from product_rows("g", every[0:last_q], lhs, h_ready[0], 512, (0,),
                                            copy_to(lambda m: gated[:, m, c0:c0 + 512], "g"))
                if l < DEPTH - 1:
                    yield from ada(l + 1)

            for t, stream in ((0, proj_first), (1, proj_second)):
                inputs = hgrn_inputs(l, t, ctx_out, work)
                beside = stream()
                next(beside)
                alongside(hgrn(l, t, ctx_out, work, inputs), 13, beside, 20 if t == 0 else 13)
                fence()

            o_a = work[8]
            R_WORK.reset()
            prob = [R_WORK.cut(TOK) for _ in range(6)]
            prob_t = [R_WORK.cut(TOK) for _ in range(2)]
            q_pad = {"b": [[R_WORK.cut(P) for _ in range(4)] for _ in range(2)],
                     "c": [[R_WORK.cut(P) for _ in range(8)] for _ in range(2)]}
            q_pad["d"] = q_pad["b"]
            o_bcd = cut_at(R_WORK, R_WORK.size - TT * D, TT * 768).rearrange("p (m n) -> p m n", m=TT)
            pad_at = R_WORK.start + 8 * TOK
            t_pad = G.did(pool.memset(base[:, pad_at:pad_at + 24 * P], 0.0))
            free = {"p": [[] for _ in prob], "pt": [[], []]}

            def padded_queries(src, kind, n_maps, rows_to, scale):
                n = [0]
                sets = q_pad[kind]

                def prepare(m):
                    i = n[0] % 2
                    n[0] += 1
                    b = banks[6 + i]
                    t = transposed(src[:, m, :], 2, b, None)
                    toks = []
                    for g in range(n_maps):
                        e = (S, V)[g % 2]
                        e.after(t, t_pad)
                        r0, r1, w = rows_to(g)
                        blk = g * 2 // n_maps
                        dst, ps = sets[i][g][r1:r1 + w, :], b.ap[r0:r0 + w, blk * P:(blk + 1) * P]
                        if e is S:
                            toks.append(S.did(act.activation(dst, ps, ACT.Copy, scale=scale)))
                        else:
                            toks.append(V.did(dve.tensor_scalar(dst, ps, scale, None, ALU.mult)))
                    b.read_by = toks[-2:]
                    return sets[i], toks[-2:]
                return prepare

            def items_of(kind):
                items = []
                if kind == "c":
                    prepare = padded_queries(q_c, kind, 8, lambda g: (32 * (g % 4), 32 * (g % 4), 32), 1.0)
                else:
                    prepare = padded_queries(q_b if kind == "b" else q_d, kind, 4,
                                                            lambda h: (64 * (h % 2), 64 * (h // 2), 64), HD ** -0.5)
                for m in range(last_q):
                    shared = {"m": m}
                    if m >= LT:
                        lo_tile = hi_tile = LT
                    elif kind == "d":
                        lo_tile, hi_tile = max(m - 1, 0), min(m + 2, LT)
                    else:
                        lo_tile, hi_tile = 0, LT
                    w = (hi_tile - lo_tile) * P
                    lo = SEQ - w
                    tiles = list(range(lo_tile, hi_tile)) + [LT, LT + 1]

                    def make(h, m=m, lo=lo, lo_tile=lo_tile, hi_tile=hi_tile, tiles=tiles, shared=shared, w=w):
                        def segments(kt):
                            s = [(kt[:, lo_tile * P:hi_tile * P], lo)] if w else []
                            return s + [(kt[:, SEQ:TOK], SEQ)]

                        def prepare_m():
                            shared["sets"], shared["ready"] = prepare(m)

                        it = {"prepare": prepare_m if h == 0 else None, "q_ready": lambda: shared["ready"], "k_ready": None,
                              "range": (lo, TOK), "v_ready": None, "first": h == 0, "bank": banks[1], "col": h * P}
                        if kind == "c":
                            it["maps"] = Lazy(lambda: [(shared["sets"][2 * h + j], segments(k_c[:, (2 * h + j) // 4, :])) for j in range(2)])
                            it["scale"], it["neg_lam"] = DQ ** -0.5, lam[:, 5:6]
                            v = lambda s: v_c[:, s, (h // 2) * P:(h // 2 + 1) * P]
                        else:
                            kt, vv = (k_b, v_b) if kind == "b" else (k_d, v_d)
                            it["maps"] = Lazy(lambda: [(shared["sets"][h], segments(kt[:, 0, :]))])
                            it["scale"] = 1.0
                            v = lambda s: vv[:, s, :]
                        if kind == "d":
                            it["sink"] = (neg_sinks[:, h:h + 1], sinks[:, h:h + 1])
                            if m < LT:
                                it["masks"] = ([(lo, up_mask[:])] if m > 0 else []) + ([(SEQ - P, low_mask[:])] if m < LT - 1 else [])
                        it["blocks"] = [(lo + j * P, P, v(s)) for j, s in enumerate(tiles)]
                        it["rec"] = rec_all[:, kinds.index(kind), m, h:h + 1]
                        if h == NH - 1:
                            it["finish"] = lambda t: finish(kind, m, t)
                        return it
                    items += [make(h) for h in range(NH)]
                return items

            def finish(kind, m, t):
                b = banks[1]
                V.after(t, V.now())
                at_c = 256 * "bcd".index(kind)
                for h in range(NH):
                    own = h % 2 if kind == "c" else h // 2
                    x = V.did(dve.tensor_scalar(o_bcd[:, m, at_c + h * HD:at_c + (h + 1) * HD],
                                                b.ap[:, h * P + own * HD:h * P + own * HD + HD],
                                                rec_all[:, kinds.index(kind), m, h:h + 1], None, ALU.mult))
                if kind == "c" and m == last_q - 1:
                    head_norm(o_bcd[:, 0:last_q, 256:512], gain_df[:], 1.0 - lam_init)
                    head_norm(o_a[:, 0:last_q, :], gain_hg[:], 1.0)
                return [x]

            def head_norm(o, gain, scale):
                st = stats_n[:]
                n = last_q * NH

                def sums(m):
                    V.after(V.now())
                    V.after(V.did(dve.tensor_tensor(o_sq, o[:, m, :], o[:, m, :], ALU.mult)))
                    V.did(dve.reduce_sum(st[:, 0, m * NH:(m + 1) * NH], o_sq.rearrange("p (h d) -> p h d", d=HD), AX))

                def norm(m):
                    o3 = o[:, m, :].rearrange("p (h d) -> p h d", d=HD)
                    V.after(V.now(), params)
                    V.after(V.did(dve.tensor_tensor(o3, o3, bc(st[:, 1, m * NH:(m + 1) * NH], 2, [P, NH, HD]), ALU.mult)))
                    V.did(dve.scalar_tensor_tensor(o3, o3, scale, bc(gain, 1, [P, NH, HD]), ALU.mult, ALU.mult))

                chores.extend([lambda m=m: sums(m) for m in range(last_q)])
                chores.append(lambda: rstd(st[:, 0, 0:n], 1.0 / HD, RMS_EPS, st[:, 1, 0:n], st[:, 2, 0:n], V.now()))
                chores.extend([lambda m=m: norm(m) for m in range(last_q)])

            o_sq = t_cos[:, 0:256]
            chores = []
            kinds = ["c", "b", "d"]
            V.after(t_lam)
            items = [it for kind in kinds for it in items_of(kind)]
            alongside(attend(items, prob, prob_t, free, chores), len(items) + 4, gate_and_ada(), 2 * last_q + (6 if l < DEPTH - 1 else 0))
            fence()

            R_WORK.reset()
            z, diag = R_WORK.cut(TT, D), R_WORK.cut(8, P)
            xs = cut_at(R_QK, 0, TT * D).rearrange("p (m n) -> p m n", m=TT)
            ln_g, ln_b, ones = cut_at(R_V, 0, D), cut_at(R_V, D, D), cut_at(R_V, 4 * D, P)
            gate_bc = cut_at(R_V, 2 * D, 2 * D).rearrange("p (v d) -> p v d", v=2)
            G.after(x_stores_done[0])
            if l == 0:
                load(xs[:, 0:LT, :], a["x"][0].rearrange("(m p) d -> p m d", p=P), parameters)
                load(xs[:, LT:TT, :], a["ctx"][0].rearrange("(m p) d -> p m d", p=P), parameters)
            else:
                load(xs[:, 0:LT, :], a["x_scratch"][0:SEQ].rearrange("(m p) d -> p m d", p=P), parameters)
            load(ln_g, spread(a["ln_g"][l], D), parameters)
            tail_ready = load(ln_b, spread(a["ln_b"][l], D), parameters)
            y_rows, y_ready = {}, {}

            def gate_y(m):
                S.after(S.now())
                t = S.did(act.activation(gated[:, m, :], gated[:, m, :], ACT.Silu))
                V.after(t)
                V.did(dve.tensor_tensor(gated[:, m, 0:256], gated[:, m, 0:256], o_a[:, m, :], ALU.mult))
                y_rows[m] = V.did(dve.tensor_tensor(gated[:, m, 256:D], gated[:, m, 256:D], o_bcd[:, m, :], ALU.mult))

            def turn_y(m):
                y_ready[m] = []
                for half in range(2):
                    b = banks[4 + (2 * m + half) % 4]
                    t = transposed(gated[:, m, half * 512:half * 512 + 512], 4, b, y_rows[m])
                    e = (S, V)[half]
                    e.after(t)
                    dst = h_t[:, 4 * half:4 * half + 4, m * P:(m + 1) * P]
                    src = b.ap.rearrange("p (j n) -> p j n", n=P)
                    t = S.did(act.activation(dst, src, ACT.Copy)) if e is S else V.did(dve.tensor_copy(dst, src))
                    b.read_by = [t]
                    y_ready[m].append(t)

            gate_y(0)
            gate_y(1)
            turn_y(0)
            gate_y(2)
            turn_y(1)

            t_one = V.did(dve.memset(ones, 1.0))
            free_d = [None] * 2
            for v in range(2 if ctx_out else 1):
                for half in range(2):
                    V.after(free_d[half])
                    for j in range(4):
                        t = V.did(dve.tensor_scalar(diag[:, 4 * half + j, :], ident[:], ada_t[:, l, 16 + 4 * half + j, v:v + 1], None, ALU.mult))
                    b = banks[2 + half]
                    T.after(t, t_one, b.read_by)
                    t = T.did(pe.matmul(b.ap, ones, diag[:, 4 * half:4 * half + 4, :].rearrange("p i n -> p (i n)"), start=True, stop=True))
                    free_d[half] = t
                    S.after(t)
                    t_gate = S.did(act.activation(gate_bc[:, v, half * 512:half * 512 + 512], b.ap, ACT.Copy))
                    b.read_by = [t_gate]

            z_ready = {}
            out_read = {}

            def tail(m):
                st = stats[:, 20 * m:20 * m + 20]
                V.after(V.now())
                V.after(V.did(dve.bn_aggr(st[:, 12:14], st[:, 0:12])))
                t = rstd(st[:, 13:14], 1.0, LN_EPS, st[:, 14:15], st[:, 15:16], None)
                V.after(t)
                V.after(V.did(dve.tensor_scalar(z[:, m, :], z[:, m, :], st[:, 12:13], st[:, 14:15], ALU.subtract, ALU.mult)))
                V.after(V.did(dve.tensor_tensor(z[:, m, :], z[:, m, :], ln_g, ALU.mult)))
                z_ready[m] = V.did(dve.tensor_tensor(z[:, m, :], z[:, m, :], ln_b, ALU.add))
                if ctx_out and m < LT:
                    G.after(z_ready[m])
                    x_stores_done[0] = x_stores.did(pool.dma_start(x_scratch[m], z[:, m, :]))

            for n in range(2):
                c0 = 512 * n

                def evacuate(m, ps, ready):
                    zz = z[:, m, c0:c0 + 512]
                    V.after(ready, t_gate, tail_ready)
                    t = V.did(dve.tensor_tensor(zz, ps, gate_bc[:, 0 if m < LT else 1, c0:c0 + 512], ALU.mult))
                    V.after(t)
                    t2 = V.did(dve.scalar_tensor_tensor(zz, xs[:, m, c0:c0 + 512], ALPHA, zz, ALU.mult, ALU.add))
                    V.after(t2)
                    V.did(dve.bn_stats(stats[:, 20 * m + 6 * n:20 * m + 6 * n + 6], zz))
                    if n == 1:
                        out_read[m] = ready
                        tail(m)
                    return [t]

                for i, _ in enumerate(product_rows("out", list(range(last_q)), lhs, lambda m: y_ready[m], 512, (0, 1, 2, 3), evacuate)):
                    if n == 0 and i + 2 < last_q:
                        turn_y(i + 2)
                        if i + 3 < last_q:
                            gate_y(i + 3)
                    if n == 0 and i + 3 == last_q and before_out is not None:
                        G.after(*everyone())
                        before_out()
                    if n == 1 and i >= 1 and after_tile is not None:
                        after_tile(i - 1, z, z_ready[i - 1], out_read[i - 1])
            if after_tile is not None:
                after_tile(last_q - 1, z, z_ready[last_q - 1], out_read[last_q - 1])
            return z, z_ready

        def cut_at(region, at_, n):
            assert at_ + n <= region.size
            return base[:, region.start + at_:region.start + at_ + n]

        class Lazy:

            def __init__(self, make):
                self.make = make

            def __iter__(self):
                return iter(self.make())

        x_stores_done = [None]
        rec_all = tile("rec_all", [3, TT, NH])
        stats_n = tile("stats_n", [3, TT * NH])

        stage_x = [cut_at(R_V, i * D, D) for i in range(2)]
        stage_free = [None, None]
        arrivals = {}

        def fetch(m):
            src = x_in[m] if m < LT else ctx_in[m - LT]
            G.after(stage_free[m % 2])
            arrivals[m] = x_loads[m % 2].did(pool.dma_start(stage_x[m % 2], src))

        fetch(0)
        fetch(1)
        for _ in ada(0):
            pass
        h_ready[0] = []
        for m in range(TT):
            h_ready[0] += modulate(0, m, stage_x[m % 2], arrivals[m], None)
            stage_free[m % 2] = T.now()
            if m + 2 < TT:
                fetch(m + 2)
        fence()
        next_h = []
        layer(0, lambda m, z, ready, read: next_h.extend(modulate(1, m, z[:, m, :], ready, read)))
        h_ready[0] = next_h
        fence()
        for e in (T, S, V, G):
            e.after(x_stores_done[0])
        xn_t = cut_at(R_HT, 0, KT * SEQ).rearrange("p (k t) -> p k t", k=KT)
        y_t = cut_at(R_G, 0, KT * SEQ).rearrange("p (k t) -> p k t", k=KT)
        gates = cut_at(R_G, KT * SEQ, LT * 12).rearrange("p (m g) -> p m g", m=LT)
        y_b = cut_at(R_HT, KT * SEQ, LT * 256).rearrange("p (m n) -> p m n", m=LT)
        y_row = cut_at(R_HT, KT * SEQ + LT * 256, LT * 256).rearrange("p (m n) -> p m n", m=LT)
        R_WORK.reset()
        R_WORK.cut(LT, D)
        w1 = [R_WORK.cut(CMP_HID * 16).rearrange("p (k e) -> p k e", e=CMP_HID) for _ in range(2)]
        w2 = [R_WORK.cut(HD) for _ in range(2)]
        blocks_c = [R_WORK.cut(16, 2 * N_CMP) for _ in range(2)]
        gain2 = R_WORK.cut(4, HD)
        ln_rows = R_WORK.cut(4, 256)
        ws, ws_t = R_WORK.cut(4, P), R_WORK.cut(4, P)
        tri, cmp_mask, cmp_valid = R_WORK.cut(P), R_WORK.cut(LT, N_CMP), R_WORK.cut(LT, N_CMP)
        rows_pe, rows_b = R_WORK.cut(P), R_WORK.cut(P)
        prob = [R_WORK.cut(SEQ) for _ in range(3)]
        prob_t = [R_WORK.cut(SEQ) for _ in range(2)]
        q_pad2_all = R_WORK.cut(8 * P)
        q_pad2 = [[q_pad2_all[:, (4 * i + h) * P:(4 * i + h + 1) * P] for h in range(4)] for i in range(2)]
        tmp2 = [t_cos, t_sin]

        params2 = Transfers(sem("parameters_2"))
        N1, N2, BS, CB, CW, SW, BG = 0, 8, 16, 20, 22, 84, 90
        ready2 = []

        def load_parameters_2():
            r0 = 0
            for src, n in ((a["norm1_g_2"][0].rearrange("(k p) -> k p", p=P), 8), (a["norm2_g_2"][0].rearrange("(k p) -> k p", p=P), 8),
                           (a["gmlp_bs_2"][0], 4), (a["conf_conv_b_2"][0].rearrange("(k p) -> k p", p=P), 2),
                           (a["conf_conv_w_2"][0][:, 0:P], CONV_K), (a["conf_conv_w_2"][0][:, P:256], CONV_K),
                           (a["sconv_w_2"][0][:, 0:P], SCONV_K), (a["sconv_w_2"][0][:, P:256], SCONV_K),
                           (a["b_gate_2"][0].rearrange("(k p) -> k p", p=P), 32)):
                load(rows_b[r0:r0 + n, :], src, params2)
                r0 += n
            for i in range(2):
                load(rows_pe[16 * i:16 * i + 16, :], a["nsa_cmp_pe_2"][0, i].rearrange("(k s) d -> k (s d)", s=2), params2)
                load(w1[i], a["nsa_cmp_w1_2"][0, i].rearrange("(k p) e -> p k e", p=P), params2)
                load(w2[i], a["nsa_cmp_w2_2"][0, i], params2)
            load(gain2[:, 0, :], spread(a["nsa_q_norm_g_2"][0], HD), params2)
            load(gain2[:, 1:4, :].rearrange("p a b -> p (a b)"), spread(a["nsa_k_norm_g_2"][0].rearrange("a b -> (a b)"), 3 * HD), params2)
            for i, name in enumerate(("gmlp_ln_g_2", "gmlp_ln_b_2", "conf_ln_g_2", "conf_ln_b_2")):
                load(ln_rows[:, i, :], spread(a[name][0], 256), params2)
            load(ws, a["gmlp_ws_2"][0].rearrange("g t s -> t g s"), params2)
            load(tri, a["c_tri"], params2)
            load(cmp_mask, a["c_cmp_mask"], params2)
            ready2.append(load(cmp_valid, a["c_cmp_valid"], params2))

        z, z_ready = layer(1, None, load_parameters_2)
        z_ready = [z_ready[m] for m in range(LT)]
        fence()

        R_V.reset()
        ks_t, kw_t = R_V.cut(SEQ), R_V.cut(SEQ)
        v_s, v_w = R_V.cut(LT, P), R_V.cut(LT, P)
        q_2 = R_V.cut(LT, 256)
        kc_t, kc_rows = R_V.cut(N_CMP), R_V.cut(P)
        v_cmp, hid_c = R_V.cut(P), R_V.cut(2, 64)
        cols_pe = R_V.cut(32)
        cols_b = cut_at(R_G, KT * SEQ + LT * 12, 122)
        R_QK.reset()
        u_g, v_g = R_QK.cut(LT, 256), R_QK.cut(LT, 256)
        z_pad, conv = R_QK.cut(2, SEQ + CONV_K - 1), R_QK.cut(2, SEQ)
        s_b, s_pad = R_QK.cut(2, SEQ), R_QK.cut(2, SEQ + SCONV_K - 1)
        ca = R_QK.cut(SEQ)
        T.after(ready2)
        t = T.did(pe.transpose(banks[0].ap[:, 0:122], rows_b[0:122, :], ident[0:122, 0:122]))
        S.after(t)
        t = S.did(act.activation(cols_b, banks[0].ap[:, 0:122], ACT.Copy))
        banks[0].read_by = [t]
        t = T.did(pe.transpose(banks[1].ap[:, 0:32], rows_pe[0:32, :], ident[0:32, 0:32]))
        S.after(t)
        t_cols = S.did(act.activation(cols_pe, banks[1].ap[:, 0:32], ACT.Copy))
        banks[1].read_by = [t_cols]
        V.after(ready2, t_cols)
        t_pad = [G.did(pool.memset(x, 0.0)) for x in
                 (z_pad[:, :, 0:CONV_K - 1], s_pad[:, :, 0:SCONV_K - 1], q_pad2_all)][-1]

        for g in range(4):
            t = V.did(dve.tensor_tensor(ws[:, g, :], ws[:, g, :], tri, ALU.mult))
        t = transposed(ws.rearrange("p g s -> p (g s)"), 4, banks[2], t)
        S.after(t)
        t_ws = S.did(act.activation(ws_t, banks[2].ap.rearrange("p (g n) -> p g n", n=P), ACT.Copy))
        banks[2].read_by = [t_ws]

        def rms_turned(gain_at, z_ready):
            ss, rs, tmp = stats[:, 0:4], stats[:, 4:8], stats[:, 8:12]
            S.after(z_ready)
            for m in range(LT):
                for half in range(2):
                    S.after(S.now())
                    t = S.did(act.activation(raw[half], z[:, m, half * 512:half * 512 + 512], ACT.Square,
                                             accum_out=stats[:, 16 + 2 * m + half:17 + 2 * m + half]))
            V.after(t)
            t = V.did(dve.reduce_sum(ss, stats[:, 16:24].rearrange("p (m h) -> p m h", h=2), AX))
            t = rstd(ss, 1.0 / D, RMS_EPS, rs, tmp, t)
            done = []
            row_free = [S.now(), S.now()]
            for m in range(LT):
                for half in range(2):
                    row = raw[half]
                    V.after(row_free[half], z_ready, t)
                    x = V.did(dve.tensor_scalar(row, z[:, m, half * 512:half * 512 + 512], rs[:, m:m + 1], None, ALU.mult))
                    b = banks[4 + (2 * m + half) % 4]
                    x = transposed(row, 4, b, x)
                    row_free[half] = x
                    if half == 0:
                        S.after(x, t_cols)
                        for j in range(4):
                            y = S.did(act.activation(xn_t[:, j, m * P:(m + 1) * P], b.ap[:, j * P:(j + 1) * P], ACT.Copy,
                                                     scale=cols_b[:, gain_at + j:gain_at + j + 1]))
                    else:
                        V.after(x, t_cols)
                        y = V.did(dve.tensor_tensor(xn_t[:, 4:8, m * P:(m + 1) * P], b.ap.rearrange("p (j n) -> p j n", n=P),
                                                    bc(cols_b[:, gain_at + 4:gain_at + 8], 2, [P, 4, P]), ALU.mult))
                    b.read_by = [y]
                    done.append(y)
            return done

        xn_ready = rms_turned(N1, z_ready)
        lhs2 = lambda k, m: xn_t[:, k, m * P:(m + 1) * P]
        rhs2 = lambda k, t0, t1: xn_t[:, k, t0:t1]
        latent = list(range(LT))

        def run(gen):
            for _ in gen:
                pass

        def layer_norm_rows(x, ready, gain, offset, st):
            V.after(ready)
            t = V.did(dve.bn_stats(st[:, 0:6], x))
            V.after(t)
            t = V.did(dve.bn_aggr(st[:, 6:8], st[:, 0:6]))
            t = rstd(st[:, 7:8], 1.0, LN_EPS, st[:, 8:9], st[:, 9:10], t)
            V.after(t)
            t = V.did(dve.tensor_scalar(x, x, st[:, 6:7], st[:, 8:9], ALU.subtract, ALU.mult))
            V.after(t)
            t = V.did(dve.tensor_tensor(x, x, gain, ALU.mult))
            V.after(t)
            return V.did(dve.tensor_tensor(x, x, offset, ALU.add))

        def turn_rows(src, n_pair, ready):
            def one(m, bank):
                t = transposed(src[:, m, :], 2, bank, ready)
                S.after(t)
                t = S.did(act.activation(y_t[:, 2 * n_pair:2 * n_pair + 2, m * P:(m + 1) * P],
                                         bank.ap[:, 0:256].rearrange("p (j n) -> p j n", n=P), ACT.Copy))
                bank.read_by = [t]
                return t
            return one

        y_t_ready = []

        def conv_inputs():
            spans, n = [(0, SEQ)], 0
            for c in range(2):
                def ca_in(t0, t1, ps, ready):
                    S.after(ready)
                    return [S.did(act.activation(z_pad[:, c, CONV_K - 1:], ps, ACT.Copy))]

                def cb_in(t0, t1, ps, ready):
                    S.after(ready, z_gated)
                    t = S.did(act.activation(ca, ps, ACT.Sigmoid))
                    V.after(t, t_pad)
                    z_gated.append(V.did(dve.tensor_tensor(z_pad[:, c, CONV_K - 1:], z_pad[:, c, CONV_K - 1:], ca, ALU.mult)))
                    return [t]

                for use in (ca_in, cb_in):
                    product_cols("fm", rhs2, xn_ready, spans, (n % 4,), use)
                    n += 1
                    yield 8 * c
            for c in range(2):
                def sc_in(t0, t1, ps, ready):
                    S.after(ready)
                    return [S.did(act.activation(s_pad[:, c, SCONV_K - 1:], ps, ACT.Copy))]

                def sh_in(t0, t1, ps, ready):
                    V.after(ready, S.now(), t_pad)
                    s_gated.append(V.did(dve.tensor_tensor(s_pad[:, c, SCONV_K - 1:], s_pad[:, c, SCONV_K - 1:], ps, ALU.mult)))
                    return [s_gated[-1]]

                for use in (sc_in, sh_in):
                    product_cols("fm", rhs2, xn_ready, spans, (n % 4,), use)
                    n += 1
                    yield 8
            for c in range(2):
                def sb_in(t0, t1, ps, ready):
                    S.after(ready)
                    return [S.did(act.activation(s_b[:, c, :], ps, ACT.Copy))]
                product_cols("fm", rhs2, xn_ready, spans, (n % 4,), sb_in)
                n += 1
                yield 8

        z_gated, s_gated = [], []

        def causal_conv(dst, src, taps, w_at, bias):
            first = cols_b[:, w_at:w_at + 1]
            if bias is None:
                t = V.did(dve.tensor_scalar(dst, src[:, 0:SEQ], first, None, ALU.mult))
            else:
                t = V.did(dve.tensor_scalar(dst, src[:, 0:SEQ], first, bias, ALU.mult, ALU.add))
            for j in range(1, taps):
                V.after(t)
                t = V.did(dve.scalar_tensor_tensor(dst, src[:, j:j + SEQ], cols_b[:, w_at + j:w_at + j + 1], dst, ALU.mult, ALU.add))
                yield t

        def turned_later(src, n_pair, m, ready):
            later.add(2, lambda: y_t_ready.append(turn_rows(src, n_pair, ready)(m, banks[4 + m % 2])))

        def gmlp_in(m, ps, ready):
            S.after(ready)
            S.did(act.activation(u_g[:, m, :], ps[:, 0:256], ACT.Gelu_apprx_tanh))
            t = S.did(act.activation(v_g[:, m, :], ps[:, 256:512], ACT.Gelu_apprx_tanh))
            normed = layer_norm_rows(v_g[:, m, :], t, ln_rows[:, 0, :], ln_rows[:, 1, :], stats[:, 32 + 12 * m:44 + 12 * m])

            def mix():
                b = banks[2 + m % 2]
                T.after(normed, t_ws, b.read_by)
                for g in range(4):
                    mm = pe.matmul(b.ap[:, g * 64:(g + 1) * 64], ws_t[:, g, :], v_g[:, m, g * 64:(g + 1) * 64], start=True, stop=True)
                V.after(T.did(mm))
                for g in range(4):
                    x = V.did(dve.scalar_tensor_tensor(u_g[:, m, g * 64:(g + 1) * 64], b.ap[:, g * 64:(g + 1) * 64],
                                                       cols_b[:, BS + g:BS + g + 1], u_g[:, m, g * 64:(g + 1) * 64], ALU.add, ALU.mult))
                b.read_by = [x]
                turned_later(u_g, 0, m, x)

            later.add(2, mix)
            return [t]

        def head_rows_2(dst, gain, n_heads, st):
            n = n_heads * HD
            i = free_cell["n"] % 2
            free_cell["n"] += 1

            def go(ready):
                V.after(ready)
                t = V.did(dve.tensor_tensor(tmp2[i][0:dst.shape[0], 0:n], dst, dst, ALU.mult))
                V.after(t)
                t = V.did(dve.reduce_sum(st[:, 0:n_heads], tmp2[i][0:dst.shape[0], 0:n].rearrange("p (h d) -> p h d", d=HD), AX))
                t = rstd(st[:, 0:n_heads], 1.0 / HD, RMS_EPS, st[:, 4:4 + n_heads], st[:, 8:8 + n_heads], t)
                V.after(t)
                d3 = dst.rearrange("p (h d) -> p h d", d=HD)
                t = V.did(dve.tensor_tensor(d3, d3, bc(st[:, 4:4 + n_heads], 2, [dst.shape[0], n_heads, HD]), ALU.mult))
                V.after(t)
                return V.did(dve.tensor_tensor(d3, d3, bc(gain, 1, [dst.shape[0], n_heads, HD]), ALU.mult))
            return go

        def q_in(m, ps, ready):
            S.after(ready)
            t = S.did(act.activation(q_2[:, m, :], ps[:, 0:256], ACT.Copy))
            head_rows_2(q_2[:, m, :], gain2[:, 0, :], NH, stats[:, 96 + 12 * m:108 + 12 * m])(t)
            return [t]

        k_tmp = [raw[0], raw[1]]
        k_tmp_free = [T.now(), T.now()]

        def kv_in(m, ps, ready):
            i = m % 2
            S.after(ready, k_tmp_free[i])
            S.did(act.activation(k_tmp[i][:, 0:P], ps[:, 0:P], ACT.Copy))
            S.did(act.activation(v_s[:, m, :], ps[:, P:2 * P], ACT.Copy))
            S.did(act.activation(k_tmp[i][:, P:2 * P], ps[:, 2 * P:3 * P], ACT.Copy))
            t_read = S.did(act.activation(v_w[:, m, :], ps[:, 3 * P:4 * P], ACT.Copy))
            for j in range(2):
                t = head_rows_2(k_tmp[i][:, j * P:(j + 1) * P], gain2[:, 2 + j, :], NKV, stats[:, 144 + 12 * (2 * m + j):156 + 12 * (2 * m + j)])(t_read)

            def turn_keys():
                b = banks[6 + i]
                k_tmp_free[i] = x = transposed(k_tmp[i][:, 0:256], 2, b, t)
                S.after(x)
                S.did(act.activation(ks_t[:, m * P:(m + 1) * P], b.ap[:, 0:P], ACT.Copy))
                b.read_by = [S.did(act.activation(kw_t[:, m * P:(m + 1) * P], b.ap[:, P:2 * P], ACT.Copy))]

            later.add(2, turn_keys)
            return [t_read]

        def ng_in(m, ps, ready):
            S.after(ready)
            return [S.did(act.activation(gates[:, m, :], ps[:, 0:12], ACT.Sigmoid))]

        def convolutions():
            for c in range(2):
                V.after(z_gated[c], t_cols)
                for t in causal_conv(conv[:, c, :], z_pad[:, c, :], CONV_K, CW + CONV_K * c, cols_b[:, CB + c:CB + c + 1]):
                    yield t
                conv_done.append(t)
            for c in range(2):
                y = y_t[:, 6 + c, :]
                V.after(s_gated[c], S.now())
                for t in causal_conv(y, s_pad[:, c, :], SCONV_K, SW + SCONV_K * c, None):
                    yield t
                V.after(t)
                y_t_ready.append(V.did(dve.tensor_tensor(y, y, s_b[:, c, :], ALU.mult)))

        def conformer_rows():
            for m in latent:
                def norm_rows(m=m):
                    b = banks[4 + m % 2]
                    T.after(conv_done, b.read_by)
                    for c in range(2):
                        mm = pe.transpose(b.ap[:, c * P:(c + 1) * P], conv[:, c, m * P:(m + 1) * P], ident[:])
                    S.after(T.did(mm))
                    t = S.did(act.activation(y_row[:, m, :], b.ap[:, 0:256], ACT.Copy))
                    b.read_by = [t]
                    t = layer_norm_rows(y_row[:, m, :], t, ln_rows[:, 2, :], ln_rows[:, 3, :], stats[:, 256 + 12 * m:268 + 12 * m])
                    S.after(t)
                    t = S.did(act.activation(y_row[:, m, :], y_row[:, m, :], ACT.Silu))
                    turned_later(y_row, 2, m, t)
                later.add(1 + m, norm_rows)

        def rows_2():
            yield from product_rows("gmlp", latent, lhs2, xn_ready, 512, (0, 1), gmlp_in)
            yield from product_rows("q", latent, lhs2, xn_ready, 256, (0, 1), q_in)
            conformer_rows()
            yield from product_rows("kv", latent, lhs2, xn_ready, 512, (0, 1), kv_in)
            yield from product_rows("ng", latent, lhs2, xn_ready, P, (0, 1), ng_in)

        conv_done = []
        taps = convolutions()
        for n_taps in conv_inputs():
            for _ in range(n_taps):
                next(taps)
        alongside(rows_2(), 14, taps, 2 * (SCONV_K - 1) + 2 * (CONV_K - 1) - 48)

        compress_ready = []
        for i in range(2):
            def blocks_in(t0, t1, ps, ready):
                (S, V)[i].after(ready)
                for hh in range(2):
                    src = ps[64 * hh:64 * hh + 64, :].rearrange("p (n k s) -> p s k n", k=8, s=2)
                    for s in range(2):
                        dst = blocks_c[i][64 * s:64 * s + 64, :, hh * N_CMP:(hh + 1) * N_CMP]
                        for part in range(2):
                            k8 = slice(8 * part, 8 * part + 8)
                            if i == 0:
                                t = S.did(act.activation(dst[:, k8, :], src[:, s, :, part:part + N_CMP], ACT.Copy))
                            else:
                                t = V.did(dve.tensor_copy(dst[:, k8, :], src[:, s, :, part:part + N_CMP]))
                V.after(t)
                compress_ready.append(V.did(dve.tensor_tensor(blocks_c[i], blocks_c[i], bc(cols_pe[:, 16 * i:16 * i + 16], 2, [P, 16, 2 * N_CMP]), ALU.add)))
                return [t]

            product_cols("fm", rhs2, xn_ready, [(0, SEQ)], (i,), blocks_in)

        for i in range(2):
            b = banks[2 + i]
            T.after(compress_ready[i], b.read_by)
            for k in range(16):
                mm = pe.matmul(b.ap[:, 0:2 * N_CMP], w1[i][:, k, :], blocks_c[i][:, k, :], start=k == 0, stop=k == 15)
            t = T.did(mm)
            S.after(t)
            t = S.did(act.activation(hid_c[:, i, 0:2 * N_CMP], b.ap[:, 0:2 * N_CMP], ACT.Gelu_apprx_tanh))
            b.read_by = [t]
            b = banks[4 + i]
            T.after(t, b.read_by)
            for hh in range(2):
                mm = pe.matmul(b.ap[0:N_CMP, hh * 64:(hh + 1) * 64], hid_c[:, i, hh * N_CMP:(hh + 1) * N_CMP], w2[i], start=True, stop=True)
            t = T.did(mm)
            S.after(t)
            dst = (kc_rows, v_cmp)[i][0:N_CMP, :]
            t = S.did(act.activation(dst, b.ap[0:N_CMP, 0:P], ACT.Copy))
            b.read_by = [t]
            if i == 0:
                t = head_rows_2(dst, gain2[0:N_CMP, 1, :], NKV, stats[0:N_CMP, 240:252])(t)
                b = banks[6]
                T.after(t, b.read_by)
                t = T.did(pe.transpose(b.ap[:, 0:N_CMP], dst, ident[0:N_CMP, 0:N_CMP]))
                S.after(t)
                t_kc = S.did(act.activation(kc_t, b.ap[:, 0:N_CMP], ACT.Copy))
                b.read_by = [t_kc]

        fence()

        prob = prob + [w1[0].rearrange("p k e -> p (k e)")[:, i * SEQ:(i + 1) * SEQ] for i in range(2)]
        free = {"p": [[] for _ in prob], "pt": [[], []]}
        q_ready = {}

        def prepare_2(m):
            i = m % 2
            b = banks[6 + i]
            t = transposed(q_2[:, m, :], 2, b, None)
            toks = []
            for h in range(NH):
                e = (S, V)[h % 2]
                e.after(t, t_pad)
                dst = q_pad2[i][h][64 * (h // 2):64 * (h // 2) + 64, :]
                ps = b.ap[64 * (h % 2):64 * (h % 2) + 64, (h // 2) * P:(h // 2 + 1) * P]
                if e is S:
                    toks.append(S.did(act.activation(dst, ps, ACT.Copy, scale=HD ** -0.5)))
                else:
                    toks.append(V.did(dve.tensor_scalar(dst, ps, HD ** -0.5, None, ALU.mult)))
            b.read_by = toks[-2:]
            q_ready[m] = toks[-2:]

        items = []
        for m in latent:
            for branch in range(3):
                g = 3 * m + branch
                for h in range(NH):
                    it = {"q_ready": lambda m=m: q_ready[m], "k_ready": None, "v_ready": None, "first": h == 0,
                          "bank": banks[g % 2], "col": h * P, "scale": 1.0, "rec": rec_all[:, branch, m, h:h + 1]}
                    if branch == 0 and h == 0:
                        it["prepare"] = lambda m=m: prepare_2(m)
                    if branch == 0:
                        it["maps"] = [(q_pad2[m % 2][h], [(kc_t, 0)])]
                        it["range"], it["masks"] = (0, N_CMP), [(0, cmp_mask[:, m, :])]
                        it["valid"] = cmp_valid[:, m, :]
                        it["blocks"] = [(0, N_CMP, v_cmp[0:N_CMP, :])]
                    else:
                        kt, vv = (ks_t, v_s) if branch == 1 else (kw_t, v_w)
                        it["maps"] = [(q_pad2[m % 2][h], [(kt[:, 0:(m + 1) * P], 0)])]
                        it["range"], it["masks"] = (0, (m + 1) * P), [(m * P, low_mask[:])]
                        it["blocks"] = [(j * P, P, vv[:, j, :]) for j in range(m + 1)]
                    if h == NH - 1:
                        def finish(t, m=m, branch=branch, g=g):
                            b = banks[g % 2]
                            rec = rec_all[:, branch, m, :]
                            V.after(V.now(), t)
                            x = V.did(dve.tensor_tensor(rec, rec, gates[:, m, :].rearrange("p (h b) -> p b h", b=3)[:, branch, :], ALU.mult))
                            V.after(x)
                            for h in range(NH):
                                o = b.ap[:, h * P + (h // 2) * HD:h * P + (h // 2) * HD + HD]
                                y = y_b[:, m, h * HD:(h + 1) * HD]
                                if branch == 0:
                                    x = V.did(dve.tensor_scalar(y, o, rec[:, h:h + 1], None, ALU.mult))
                                else:
                                    x = V.did(dve.scalar_tensor_tensor(y, o, rec[:, h:h + 1], y, ALU.mult, ALU.add))
                            if branch == 2:
                                y_b_ready[m] = x
                            return [x]
                        it["finish"] = finish
                    items.append(it)
        y_b_ready = {}
        run(attend(items, prob, prob_t, free))
        for m in latent:
            y_t_ready.append(turn_rows(y_b, 1, y_b_ready[m])(m, banks[4 + m % 2]))
        fence()

        work_at = R_WORK.start + LT * D
        x_hi, y_hi, mixed_hi = (parts(work_at + i * KT * SEQ, KT, SEQ) for i in range(3))
        x_lo = parts(R_HT.start, KT, SEQ)
        y_lo = parts(R_G.start, KT, SEQ)
        mixed_lo = parts(R_QK.start, KT, SEQ)
        sig = [cut_at(R_QK, KT * SEQ + i * SEQ, SEQ) for i in range(4)]
        mixed = [cut_at(R_QK, KT * SEQ + (4 + i) * SEQ, SEQ) for i in range(2)]

        def pairs_at(start):
            return [parts(start + 2 * i * SLOT, 2, SLOT) for i in range(2)]

        weights = SplitWeights((4 * [("gate", KT)] + [("branch", KT)]) * KT + KT * [("out2", 1)], pairs_at(R_V.start))
        x_split = [split(xn_t[:, k, :], x_hi[k], x_lo[k], xn_ready) for k in range(KT)]
        y_split = []
        sig_free = [None] * 4
        mixed_free = [None] * 2
        mixed_ready = []
        for d in range(KT):
            gate_done = []
            for n in range(4):
                i, w_hi, w_lo, w_ready = weights.take()
                b = banks[n % 2]
                T.after(w_ready, b.read_by)
                for k in range(KT):
                    T.after(x_split[k])
                    mm = product_3(b.ap, w_hi[:, k, :], w_lo[:, k, :], x_hi[k], x_lo[k], k == 0, k == KT - 1)
                weights.free[i] = t = T.did(mm)
                S.after(t, sig_free[n])
                t = S.did(act.activation(sig[n], b.ap, ACT.Sigmoid, bias=cols_b[:, BG + n * KT + d:BG + n * KT + d + 1]))
                b.read_by = [t]
                gate_done.append(t)
                if d == 0:
                    y_split += [split(y_t[:, k, :], y_hi[k], y_lo[k], y_t_ready) for k in (2 * n, 2 * n + 1)]
            i, w_hi, w_lo, w_ready = weights.take()
            T.after(w_ready, y_split)
            acc = mixed[d % 2]
            for n in range(4):
                b = banks[2 + (4 * d + n) % 6]
                T.after(b.read_by)
                for c in range(2):
                    k = 2 * n + c
                    mm = product_3(b.ap, w_hi[:, k, :], w_lo[:, k, :], y_hi[k], y_lo[k], c == 0, c == 1)
                t = T.did(mm)
                V.after(t, gate_done[n])
                if n == 0:
                    V.after(mixed_free[d % 2])
                    x = V.did(dve.tensor_tensor(acc, b.ap, sig[n], ALU.mult))
                    b.read_by = [x]
                    sig_free[n] = x
                else:
                    x = V.did(dve.tensor_tensor(sig[n], b.ap, sig[n], ALU.mult))
                    b.read_by = [x]
                    V.after(x)
                    sig_free[n] = x = V.did(dve.tensor_tensor(acc, acc, sig[n], ALU.add))
            weights.free[i] = t
            mixed_free[d % 2] = split(acc, mixed_hi[d], mixed_lo[d], x)
            mixed_ready.append(mixed_free[d % 2])

        def product_wide(weights, n_k, lhs, use_last):
            for k in range(n_k):
                i, w_hi, w_lo, w_ready = weights.take()
                l_hi, l_lo, l_ready = lhs(k)
                T.after(w_ready, l_ready)
                for m in latent:
                    for half in range(2):
                        b = banks[2 * m + half]
                        if k == 0:
                            T.after(b.read_by)
                        cols = slice(half * 512, half * 512 + 512)
                        rows = slice(m * P, m * P + P)
                        mm = product_3(b.ap, l_hi[:, rows], l_lo[:, rows], w_hi[:, 0, cols], w_lo[:, 0, cols], k == 0, k == n_k - 1)
                        if k == n_k - 1:
                            use_last(m, half, b, T.did(mm))
                weights.free[i] = T.now() if k == n_k - 1 else T.did(mm)
                yield weights.free[i]

        def add_to_x(m, half, b, ready):
            V.after(ready)
            cols = slice(half * 512, half * 512 + 512)
            t = V.did(dve.tensor_tensor(z[:, m, cols], z[:, m, cols], b.ap, ALU.add))
            b.read_by = [t]
            x_new.append(t)

        x_new = []
        run(product_wide(weights, KT, lambda k: (mixed_hi[k], mixed_lo[k], mixed_ready[k]), add_to_x))
        fence()
        weights = SplitWeights(FT * [("mlp1", KT)] + FT * [("mlp2", 1)], pairs_at(R_QK.start))
        hn_ready = rms_turned(N2, x_new)
        hn_hi = parts(R_G.start, KT, SEQ)
        hn_lo = parts(R_HT.start, KT, SEQ)
        hn_split = [split(xn_t[:, k, :], hn_hi[k], hn_lo[k], hn_ready) for k in range(KT)]
        hid = base[:, work_at:work_at + FT * SEQ].rearrange("p (f t) -> p f t", f=FT)
        relu = [cut_at(R_QK, 4 * SLOT + i * SEQ, SEQ) for i in range(2)]
        hid_at = R_QK.start + 4 * SLOT + 2 * SEQ
        hid_pairs = [parts(hid_at + 2 * i * SEQ, 2, SEQ) for i in range(2)]
        relu_free = [None, None]
        hid_ready = []
        for f in range(FT):
            i, w_hi, w_lo, w_ready = weights.take()
            b = banks[f % 2]
            T.after(w_ready, b.read_by)
            for k in range(KT):
                T.after(hn_split[k])
                mm = product_3(b.ap, w_hi[:, k, :], w_lo[:, k, :], hn_hi[k], hn_lo[k], k == 0, k == KT - 1)
            weights.free[i] = t = T.did(mm)
            S.after(t, relu_free[f % 2])
            t = S.did(act.activation(relu[f % 2], b.ap, ACT.Relu))
            b.read_by = [t]
            V.after(t)
            relu_free[f % 2] = V.did(dve.tensor_tensor(hid[:, f, :], relu[f % 2], relu[f % 2], ALU.mult))
            hid_ready.append(relu_free[f % 2])
        out_rows = out[0].rearrange("(m p) d -> m p d", p=P)
        hid_free = [None, None]
        hid_split = {}

        def split_hidden(f):
            if f < FT:
                hi, lo = hid_pairs[f % 2]
                hid_split[f] = (hi, lo, split(hid[:, f, :], hi, lo, hid_ready[f], hid_free[f % 2]))

        def hidden(f):
            split_hidden(f + 1)
            return hid_split.pop(f)

        def add_and_store(m, half, b, ready):
            V.after(ready)
            cols = slice(half * 512, half * 512 + 512)
            t = V.did(dve.tensor_tensor(z[:, m, cols], z[:, m, cols], b.ap, ALU.add))
            if half:
                G.after(t)
                stored.append(out_stores.did(pool.dma_start(out_rows[m], z[:, m, :])))

        stored = []
        split_hidden(0)
        for f, t in enumerate(product_wide(weights, FT, hidden, add_and_store)):
            hid_free[f % 2] = t
        stored = stored[-1]
        G.after(stored)
        Y.after(stored)


_INPUTS = ["x", "c", "ctx", "c_ctx", "w_in", "w_out", "w_ada", "b_ada", "ln_g", "ln_b", "hg_lb_logits", "hg_norm_g",
           "ga_q_norm_g", "ga_k_norm_g", "df_lambda", "df_subln_g", "wn_sink", "norm1_g_2", "w_in_2", "gmlp_ln_g_2",
           "gmlp_ln_b_2", "gmlp_ws_2", "gmlp_bs_2", "nsa_q_norm_g_2", "nsa_k_norm_g_2", "nsa_cmp_pe_2",
           "nsa_cmp_w1_2", "nsa_cmp_w2_2", "conf_conv_w_2", "conf_conv_b_2", "conf_ln_g_2", "conf_ln_b_2",
           "sconv_w_2", "w_branch_2", "w_gate_2", "b_gate_2", "w_out_2", "norm2_g_2", "w_mlp1_2", "w_mlp2_2"]


def shape_constants():
    f = np.float32
    i = np.arange(P)
    out = {"c_ident": np.eye(P, dtype=f)}
    levels = [(i[:, None] // (2 << n) == i[None, :] // (2 << n)) & (i[:, None] // (1 << n) != i[None, :] // (1 << n)) for n in range(7)]
    out["c_levels"] = np.stack(levels, 1).astype(f)
    out["c_low"] = np.where(i[None, :] <= i[:, None], 0.0, -1e30).astype(f)
    out["c_up"] = np.where(i[None, :] >= i[:, None], 0.0, -1e30).astype(f)
    out["c_tri"] = (i[None, :] <= i[:, None]).astype(f)
    t = np.arange(SEQ)
    row, col = (t // GRID_W).astype(f), (t % GRID_W).astype(f)
    for dim in (HD, DQ):
        axis = dim // 2
        inv = (f(10000.0) ** (-np.arange(0, axis, 2, dtype=f) / f(axis))).astype(f)
        ar, ac = row[:, None] * inv, col[:, None] * inv
        cos = np.concatenate([np.cos(ar), np.cos(ar), np.cos(ac), np.cos(ac)], -1)
        sin = np.concatenate([-np.sin(ar), np.sin(ar), -np.sin(ac), np.sin(ac)], -1)
        for name, v in (("cos", cos), ("sin", sin)):
            out[f"c_{name}{dim}"] = np.ascontiguousarray(v.astype(f).reshape(LT, P, dim).transpose(1, 0, 2))
    last = np.arange(N_CMP) * CMP_STRIDE + CMP_LEN - 1
    valid = (last[None, :] <= t[:, None]).reshape(LT, P, N_CMP).transpose(1, 0, 2)
    out["c_cmp_valid"] = np.ascontiguousarray(valid.astype(f))
    out["c_cmp_mask"] = np.ascontiguousarray(np.where(valid, 0.0, -1e30).astype(f))
    return out


def kernel(**inputs):
    import concourse.bacc as bacc
    from concourse.bass_utils import run_bass_kernel_spmd

    nc = bacc.Bacc("TRN2", target_bir_lowering=False, num_devices=1)
    arrays, aps = {}, {}
    for name in _INPUTS:
        arrays[f"in_{name}"] = np.ascontiguousarray(inputs[name])
    for name, value in shape_constants().items():
        arrays[f"in_{name}"] = value
    for name, value in arrays.items():
        aps[name[3:]] = nc.dram_tensor(name, value.shape, mybir.dt.from_np(value.dtype), kind="ExternalInput").ap()
    aps["x_scratch"] = nc.dram_tensor("x_scratch", (SEQ, D), F32, kind="Internal").ap()
    result = nc.dram_tensor("result", (1, SEQ, D), F32, kind="ExternalOutput").ap()
    build(nc, aps, result)
    r = run_bass_kernel_spmd(nc, [arrays], core_ids=[0])
    return r.results[0]["result"]
```
